# Optimizing a Trainium2 kernel written in Bass

```python
import jax, jax.numpy as jnp
from jax import lax
import numpy as np

D_MODEL = 1024
BATCH = 1
SEQ = 512
DEPTH = 1

EPS = 1e-6
D_FF = 2816
FFN_RES_WEIGHT = 0.5
CONV_DIM = D_MODEL
CONV_K = 3
GLA_HEADS = 4
GLA_DK = D_MODEL // 2 // GLA_HEADS
GLA_DV = D_MODEL // GLA_HEADS
GLA_QK = GLA_HEADS * GLA_DK
GLA_V = GLA_HEADS * GLA_DV
GATE_RANK = 16
GATE_TAU = 16.0
CHUNK = 64
IN_SIZES = (CONV_DIM, CONV_DIM, CONV_DIM, GLA_QK, GLA_QK, GLA_V, GATE_RANK, GLA_V, D_MODEL, D_MODEL)
IN_COLS = sum(IN_SIZES)
SPLIT_POINTS = tuple(int(s) for s in np.cumsum(IN_SIZES)[:-1])


def rmsnorm(x, g):
    xf = x.astype(jnp.float32)
    y = xf * lax.rsqrt(jnp.mean(xf * xf, axis=-1, keepdims=True) + EPS)
    return (y * g.astype(jnp.float32)).astype(x.dtype)

def swiglu(x, w_gu, w_down):
    g, u = jnp.split(x @ w_gu, 2, axis=-1)
    return (jax.nn.silu(g) * u) @ w_down

def causal_short_conv(u, w):
    S = u.shape[1]
    up = jnp.pad(u, ((0, 0), (CONV_K - 1, 0), (0, 0)))
    out = up[:, 0:S] * w[0]
    for j in range(1, CONV_K):
        out = out + up[:, j:j + S] * w[j]
    return out

def gla_chunked(q, k, v, log_a):
    B, S = q.shape[0], q.shape[1]
    N = S // CHUNK
    f32 = jnp.float32

    def to_chunks(t):
        return t.reshape(B, N, CHUNK, GLA_HEADS, t.shape[-1]).transpose(0, 3, 1, 2, 4).astype(f32)

    qc = to_chunks(q) * (GLA_DK ** -0.5)
    kc, vc, gc = to_chunks(k), to_chunks(v), to_chunks(log_a)
    b = jnp.cumsum(gc, axis=3)
    b_last = b[:, :, :, -1:]
    b_ref = b[:, :, :, CHUNK // 2 - 1:CHUNK // 2]

    q_ref = qc * jnp.exp(b - b_ref)
    k_ref = kc * jnp.exp(b_ref - b)
    scores = jnp.einsum('bhnid,bhnjd->bhnij', q_ref, k_ref)
    causal = jnp.tril(jnp.ones((CHUNK, CHUNK), dtype=bool))
    scores = jnp.where(causal, scores, 0.0)
    o_intra = jnp.einsum('bhnij,bhnjv->bhniv', scores, vc)

    q_inter = q_ref * jnp.exp(b_ref)
    k_state = kc * jnp.exp(b_last - b)
    kv = jnp.einsum('bhncd,bhncv->nbhdv', k_state, vc)
    decay = jnp.exp(b_last[:, :, :, 0]).transpose(2, 0, 1, 3)

    def step(state, inp):
        dec, kv_n = inp
        return state * dec[..., None] + kv_n, state

    init = jnp.zeros((B, GLA_HEADS, GLA_DK, GLA_DV), f32)
    _, states = lax.scan(step, init, (decay, kv))
    o_inter = jnp.einsum('bhncd,nbhdv->bhncv', q_inter, states)
    o = o_intra + o_inter
    return o.transpose(0, 2, 3, 1, 4).reshape(B, S, GLA_HEADS, GLA_DV)

def hybrid_mixer(h, w_in, conv_w, gate_w_up, gate_b, gla_norm_g, w_out_conv, w_out_gla, w_o):
    B, S, _ = h.shape
    z = h @ w_in
    cb, cc, cu, q, k, v, g_lr, r, ga, gb = jnp.split(z, SPLIT_POINTS, axis=-1)

    y_conv = (cb * causal_short_conv(cc * cu, conv_w)) @ w_out_conv

    log_a = jax.nn.log_sigmoid((g_lr @ gate_w_up + gate_b).astype(jnp.float32)) / GATE_TAU
    o = gla_chunked(q.reshape(B, S, GLA_HEADS, GLA_DK),
                    k.reshape(B, S, GLA_HEADS, GLA_DK),
                    v.reshape(B, S, GLA_HEADS, GLA_DV),
                    log_a.reshape(B, S, GLA_HEADS, GLA_DK))
    o = o * lax.rsqrt(jnp.mean(o * o, axis=-1, keepdims=True) + EPS)
    o = o.reshape(B, S, GLA_V) * gla_norm_g.astype(jnp.float32)
    y_gla = (o.astype(h.dtype) * jax.nn.silu(r)) @ w_out_gla

    merged = jax.nn.sigmoid(ga) * y_conv + jax.nn.sigmoid(gb) * y_gla
    return merged @ w_o

def first_inputs(seed: int = 0) -> dict:
    key = jax.random.key(seed)
    ks = jax.random.split(key, 20)
    f32 = jnp.float32

    def nrm(k, shape, fan_in):
        return jax.random.normal(k, shape, f32) * (fan_in ** -0.5)

    def gain(k, shape):
        return 1.0 + 0.02 * jax.random.normal(k, shape, f32)

    L = DEPTH
    return {
        'x': jax.random.normal(ks[0], (BATCH, SEQ, D_MODEL), f32),
        'norm_ffn1_g': gain(ks[1], (L, D_MODEL)),
        'ffn1_w_gu': nrm(ks[2], (L, D_MODEL, 2 * D_FF), D_MODEL),
        'ffn1_w_down': nrm(ks[3], (L, D_FF, D_MODEL), D_FF),
        'norm_mix_g': gain(ks[4], (L, D_MODEL)),
        'w_in': nrm(ks[5], (L, D_MODEL, IN_COLS), D_MODEL),
        'conv_w': nrm(ks[6], (L, CONV_K, CONV_DIM), CONV_K),
        'gate_w_up': nrm(ks[7], (L, GATE_RANK, GLA_QK), GATE_RANK),
        'gate_b': 0.1 * jax.random.normal(ks[8], (L, GLA_QK), f32),
        'gla_norm_g': gain(ks[9], (L, GLA_V)),
        'w_out_conv': nrm(ks[10], (L, CONV_DIM, D_MODEL), CONV_DIM),
        'w_out_gla': nrm(ks[11], (L, GLA_V, D_MODEL), GLA_V),
        'w_o': nrm(ks[12], (L, D_MODEL, D_MODEL), D_MODEL),
        'norm_ffn2_g': gain(ks[13], (L, D_MODEL)),
        'ffn2_w_gu': nrm(ks[14], (L, D_MODEL, 2 * D_FF), D_MODEL),
        'ffn2_w_down': nrm(ks[15], (L, D_FF, D_MODEL), D_FF),
        'final_norm_g': gain(ks[16], (D_MODEL,)),
    }

def first_block(x, norm_ffn1_g, ffn1_w_gu, ffn1_w_down, norm_mix_g, w_in, conv_w, gate_w_up, gate_b,
              gla_norm_g, w_out_conv, w_out_gla, w_o, norm_ffn2_g, ffn2_w_gu, ffn2_w_down, final_norm_g):
    for l in range(DEPTH):
        x = x + FFN_RES_WEIGHT * swiglu(rmsnorm(x, norm_ffn1_g[l]), ffn1_w_gu[l], ffn1_w_down[l])
        x = x + hybrid_mixer(rmsnorm(x, norm_mix_g[l]), w_in[l], conv_w[l], gate_w_up[l], gate_b[l],
                             gla_norm_g[l], w_out_conv[l], w_out_gla[l], w_o[l])
        x = x + FFN_RES_WEIGHT * swiglu(rmsnorm(x, norm_ffn2_g[l]), ffn2_w_gu[l], ffn2_w_down[l])
    return rmsnorm(x, final_norm_g)


GRID_W = 64
NA_HEADS = 8
NA_HEAD_DIM = 64
NA_WIDTH = NA_HEADS * NA_HEAD_DIM
NA_ROWS = 8
NA_COLS = 16
RET_HEADS = 4
RET_QK_DIM = 64
RET_V_DIM = 2 * RET_QK_DIM
RET_QK_WIDTH = RET_HEADS * RET_QK_DIM
RET_V_WIDTH = RET_HEADS * RET_V_DIM
RET_CHUNK = 128
ROPE_BASE = 10000.0
MIX_WIDTH = NA_WIDTH + RET_V_WIDTH
IN_WIDTH = 3 * NA_WIDTH + 2 * RET_QK_WIDTH + 2 * RET_V_WIDTH
D_FF_2 = 4 * D_MODEL
NEG = -1e30


F32 = jnp.float32

def rms_norm(x, gain):
    x32 = x.astype(F32)
    y = x32 * lax.rsqrt(jnp.mean(jnp.square(x32), axis=-1, keepdims=True) + EPS)
    return (y * gain.astype(F32)).astype(x.dtype)

def head_group_norm(y, gain):
    bsz, seq, heads, dv = y.shape
    mu = jnp.mean(y, axis=-1, keepdims=True)
    var = jnp.mean(jnp.square(y - mu), axis=-1, keepdims=True)
    y = (y - mu) * lax.rsqrt(var + EPS)
    return y.reshape(bsz, seq, heads * dv) * gain.astype(F32)

def rotary(x, pos):
    d = x.shape[-1]
    inv = 1.0 / (ROPE_BASE ** (jnp.arange(0, d, 2, dtype=F32) / d))
    ang = pos.astype(F32)[:, None] * inv[None, :]
    cos = jnp.cos(ang)[None, :, None, :]
    sin = jnp.sin(ang)[None, :, None, :]
    x1, x2 = x[..., : d // 2], x[..., d // 2:]
    return jnp.concatenate([x1 * cos - x2 * sin, x1 * sin + x2 * cos], axis=-1)

def neighbourhood_attention(q, k, v, rpb):
    bsz, seq, heads, dh = q.shape
    rows = seq // GRID_W
    kh = min(NA_ROWS, rows)
    n_cb = GRID_W // NA_COLS
    band = 2 * NA_COLS
    col = np.arange(GRID_W)
    col_start = np.clip(col - NA_COLS // 2, 0, GRID_W - NA_COLS)
    band_start = np.clip(np.arange(n_cb) * NA_COLS - NA_COLS // 2, 0, GRID_W - band)
    band_idx = band_start[:, None] + np.arange(band)
    q_col = col.reshape(n_cb, NA_COLS)
    lo = col_start[q_col][..., None]
    kcol = band_idx[:, None, :]
    valid = jnp.asarray((kcol >= lo) & (kcol < lo + NA_COLS))
    dc = np.clip(kcol - q_col[..., None], -(NA_COLS - 1), NA_COLS - 1) + NA_COLS - 1
    bias_c = rpb.astype(F32)[:, :, dc]

    kb = k.reshape(bsz, rows, GRID_W, heads, dh)[:, :, band_idx]
    vb = v.reshape(bsz, rows, GRID_W, heads, dh)[:, :, band_idx]
    q_rows = jnp.moveaxis(q.reshape(bsz, rows, n_cb, NA_COLS, heads, dh), 1, 0)
    scale = dh ** -0.5

    def one_row(args):
        q_row, r = args
        rs = jnp.clip(r - kh // 2, 0, rows - kh)
        k_win = lax.dynamic_slice_in_dim(kb, rs, kh, axis=1)
        v_win = lax.dynamic_slice_in_dim(vb, rs, kh, axis=1)
        s = jnp.einsum('bcqhd,bicjhd->bhcqij', q_row, k_win).astype(F32) * scale
        dr = rs - r + jnp.arange(kh) + NA_ROWS - 1
        bias = jnp.take(bias_c, dr, axis=1)
        s = s + jnp.transpose(bias, (0, 2, 3, 1, 4))[None]
        s = jnp.where(valid[None, None, :, :, None, :], s, NEG)
        p = jax.nn.softmax(s.reshape(s.shape[:4] + (kh * band,)), axis=-1)
        p = p.reshape(s.shape).astype(v.dtype)
        return jnp.einsum('bhcqij,bicjhd->bcqhd', p, v_win)

    out = lax.map(one_row, (q_rows, jnp.arange(rows)))
    return jnp.moveaxis(out, 0, 1).reshape(bsz, seq, heads * dh)

def retention_scan(q, k, v, log_gamma, include_diag):
    bsz, seq, heads, dk = q.shape
    dv = v.shape[-1]
    c = RET_CHUNK
    n = seq // c
    qc = q.reshape(bsz, n, c, heads, dk)
    kc = k.reshape(bsz, n, c, heads, dk)
    vc = v.reshape(bsz, n, c, heads, dv)
    idx = jnp.arange(c, dtype=F32)
    diff = idx[:, None] - idx[None, :]
    keep = (diff >= 0) if include_diag else (diff > 0)
    dmat = jnp.where(keep[None], jnp.exp(log_gamma[:, None, None] * jnp.maximum(diff, 0.0)[None]), 0.0)
    s = jnp.einsum('bnihd,bnjhd->bnhij', qc, kc) * dmat
    intra = jnp.einsum('bnhij,bnjhe->bnihe', s, vc)
    zeta = jnp.exp(log_gamma[:, None] * (c - 1 - idx)[None, :])
    chunk_kv = jnp.einsum('bnjhd,hj,bnjhe->nbhde', kc, zeta, vc)
    chunk_decay = jnp.exp(log_gamma * c)[None, :, None, None]

    def step(state, kv):
        return chunk_decay * state + kv, state

    _, prev = lax.scan(step, jnp.zeros((bsz, heads, dk, dv), F32), chunk_kv)
    xi = jnp.exp(log_gamma[:, None] * (idx + 1.0)[None, :])
    cross = jnp.einsum('bnihd,nbhde,hi->bnihe', qc, prev, xi)
    return (intra + cross).reshape(bsz, seq, heads, dv)

def bidirectional_retention(q, k, v, lg_fwd, lg_bwd):
    flip = lambda t: jnp.flip(t, axis=1)
    fwd = retention_scan(q, k, v, lg_fwd, True)
    bwd = flip(retention_scan(flip(q), flip(k), flip(v), lg_bwd, False))
    return fwd + bwd

def log_decay(z):
    return jnp.log1p(-jnp.exp(z.astype(F32)))

def second_inputs(seed: int = 0) -> dict:
    key = jax.random.key(seed)
    ks = jax.random.split(key, 12)
    base_decay = -(5.0 + jnp.arange(RET_HEADS, dtype=F32)) * float(np.log(2.0))
    x = jax.random.normal(ks[0], (BATCH, SEQ, D_MODEL), F32)
    w_in = jax.random.normal(ks[1], (DEPTH, D_MODEL, IN_WIDTH), F32) * D_MODEL ** -0.5
    w_out = jax.random.normal(ks[2], (DEPTH, MIX_WIDTH, D_MODEL), F32) * MIX_WIDTH ** -0.5
    na_rpb = jax.random.normal(ks[3], (DEPTH, NA_HEADS, 2 * NA_ROWS - 1, 2 * NA_COLS - 1), F32) * 0.02
    ret_decay_fwd = base_decay[None] + 0.05 * jax.random.normal(ks[4], (DEPTH, RET_HEADS), F32)
    ret_decay_bwd = base_decay[None] + 0.05 * jax.random.normal(ks[5], (DEPTH, RET_HEADS), F32)
    ret_norm_gain = 1.0 + 0.02 * jax.random.normal(ks[6], (DEPTH, RET_V_WIDTH), F32)
    norm_mix = 1.0 + 0.02 * jax.random.normal(ks[7], (DEPTH, D_MODEL), F32)
    norm_mlp = 1.0 + 0.02 * jax.random.normal(ks[8], (DEPTH, D_MODEL), F32)
    w_up = jax.random.normal(ks[9], (DEPTH, D_MODEL, D_FF_2), F32) * D_MODEL ** -0.5
    w_down = jax.random.normal(ks[10], (DEPTH, D_FF_2, D_MODEL), F32) * D_FF_2 ** -0.5
    norm_final = 1.0 + 0.02 * jax.random.normal(ks[11], (D_MODEL,), F32)
    return {'x': x, 'w_in': w_in, 'w_out': w_out, 'na_rpb': na_rpb,
            'ret_decay_fwd': ret_decay_fwd, 'ret_decay_bwd': ret_decay_bwd,
            'ret_norm_gain': ret_norm_gain, 'norm_mix': norm_mix, 'norm_mlp': norm_mlp,
            'w_up': w_up, 'w_down': w_down, 'norm_final': norm_final}

def second_block(x, w_in, w_out, na_rpb, ret_decay_fwd, ret_decay_bwd, ret_norm_gain,
              norm_mix, norm_mlp, w_up, w_down, norm_final):
    bsz, seq, _ = x.shape
    pos = jnp.arange(seq)
    splits = np.cumsum([NA_WIDTH, NA_WIDTH, NA_WIDTH, RET_QK_WIDTH, RET_QK_WIDTH, RET_V_WIDTH])
    for l in range(DEPTH):
        h = rms_norm(x, norm_mix[l])
        proj = h @ w_in[l]
        na_q, na_k, na_v, r_q, r_k, r_v, r_g = jnp.split(proj, splits, axis=-1)
        na_out = neighbourhood_attention(na_q.reshape(bsz, seq, NA_HEADS, NA_HEAD_DIM),
                                         na_k.reshape(bsz, seq, NA_HEADS, NA_HEAD_DIM),
                                         na_v.reshape(bsz, seq, NA_HEADS, NA_HEAD_DIM),
                                         na_rpb[l])
        rq = rotary(r_q.reshape(bsz, seq, RET_HEADS, RET_QK_DIM).astype(F32), pos)
        rk = rotary(r_k.reshape(bsz, seq, RET_HEADS, RET_QK_DIM).astype(F32), pos) * RET_QK_DIM ** -0.5
        rv = r_v.reshape(bsz, seq, RET_HEADS, RET_V_DIM).astype(F32)
        ret = bidirectional_retention(rq, rk, rv, log_decay(ret_decay_fwd[l]), log_decay(ret_decay_bwd[l]))
        ret = head_group_norm(ret, ret_norm_gain[l])
        ret_out = (jax.nn.silu(r_g.astype(F32)) * ret).astype(x.dtype)
        mix = jnp.concatenate([na_out.astype(x.dtype), ret_out], axis=-1)
        x = x + mix @ w_out[l]
        h = rms_norm(x, norm_mlp[l])
        x = x + jnp.square(jax.nn.relu(h @ w_up[l])) @ w_down[l]
    return rms_norm(x, norm_final)


def setup_inputs(seed=0):
    out = dict(first_inputs(seed))
    for name, value in second_inputs(seed + 1).items():
        if name != "x":
            out[name + "_2"] = value
    return out


def reference(
    x, norm_ffn1_g, ffn1_w_gu, ffn1_w_down, norm_mix_g, w_in, conv_w, gate_w_up, gate_b,
    gla_norm_g, w_out_conv, w_out_gla, w_o, norm_ffn2_g, ffn2_w_gu, ffn2_w_down, final_norm_g,
    w_in_2, w_out_2, na_rpb_2, ret_decay_fwd_2, ret_decay_bwd_2, ret_norm_gain_2, norm_mix_2,
    norm_mlp_2, w_up_2, w_down_2, norm_final_2,
):
    x = first_block(
        x, norm_ffn1_g, ffn1_w_gu, ffn1_w_down, norm_mix_g, w_in, conv_w, gate_w_up, gate_b,
        gla_norm_g, w_out_conv, w_out_gla, w_o, norm_ffn2_g, ffn2_w_gu, ffn2_w_down,
        final_norm_g,
    )
    return second_block(
        x, w_in_2, w_out_2, na_rpb_2, ret_decay_fwd_2, ret_decay_bwd_2, ret_norm_gain_2,
        norm_mix_2, norm_mlp_2, w_up_2, w_down_2, norm_final_2,
    )


_drawn_inputs = setup_inputs


def setup_inputs(seed=0):
    import zlib

    import numpy as np

    out = dict(_drawn_inputs(seed))
    spreads = {}
    factors = {'norm_ffn1_g': 3.689,
     'gate_b': 3.791,
     'gla_norm_g': 8.0,
     'norm_ffn2_g': 6.05,
     'na_rpb_2': 127.178,
     'ret_norm_gain_2': 18.836,
     'norm_mix_2': 3.119,
     'norm_mlp_2': 9.711,
     'norm_final_2': 19.085}
    for name, (base, spread) in spreads.items():
        noise = np.random.default_rng([zlib.crc32(name.encode()), seed]).standard_normal(out[name].shape)
        drawn = base * np.exp(spread * noise) if base else spread * noise
        out[name] = __import__('jax').numpy.asarray(drawn.astype(out[name].dtype))
    for name, factor in factors.items():
        out[name] = (out[name] * factor).astype(out[name].dtype)
    return out
```

```python
from contextlib import ExitStack

import numpy as np

import concourse.bass as bass
from concourse import mybir

ALU = mybir.AluOpType
ACT = mybir.ActivationFunctionType
AX_X = mybir.AxisListType.X
F32 = mybir.dt.float32
F32R = mybir.dt.float32r
I32 = mybir.dt.int32

P = 128
T = 512
D = 1024
KT = D // P
FF = 2816
FT = FF // P
FF2 = 4096
EPS = 1e-6
NRAW = 3
NW = 3
NTMP = 9

VEC = ["g1", "gm", "g2", "gf", "gm2", "gl2", "gf2", "gla", "gb", "cw0", "cw1", "cw2", "rg", "dec"]
VECN = dict(g1=8, gm=8, g2=8, gf=8, gm2=8, gl2=8, gf2=8, gla=8, gb=4, cw0=8, cw1=8, cw2=8, rg=4, dec=8)
VECO = {}
_o = 0
for _n in VEC:
    VECO[_n] = _o
    _o += VECN[_n]
NVEC = _o
GW = 896
BW = 272


class Prog:

    def __init__(self):
        self.q = {e: [] for e in "PAVGS"}
        self.n = {}
        self.seen = {e: {} for e in "PAVGS"}

    def put(self, eng, fn, waits, sem=None, by=1):
        need = {}
        for w in waits:
            if w is not None:
                need[w[0]] = max(need.get(w[0], 0), w[1])
        todo = []
        for s, v in need.items():
            if self.seen[eng].get(s, 0) < v:
                self.seen[eng][s] = v
                todo.append((s, v))
        tok = None
        if sem is not None:
            self.n[sem] = self.n.get(sem, 0) + by
            tok = (sem, self.n[sem])
        self.q[eng].append((todo, fn, sem, by))
        return tok

    def run(self, eng, e, sems):
        for todo, fn, sem, by in self.q[eng]:
            for s, v in todo:
                e.wait_ge(sems[s], v)
            if fn is None:
                continue
            ins = fn(e)
            if sem is not None:
                ins.then_inc(sems[sem], by)


def build(nc, dr, out):
    pr = Prog()

    def V(fn, *waits):
        return pr.put("V", fn, waits, "V")

    def A(fn, *waits):
        return pr.put("A", fn, waits, "A")

    def G(fn, *waits):
        return pr.put("G", fn, waits, "G")

    def PE(fn, *waits, sig=False):
        return pr.put("P", fn, waits, "P" if sig else None)

    def DMA(q, sem, dst, src, *waits):
        return pr.put(q, lambda e: e.dma_start(dst, src), waits, sem, 16)

    at = [int(nc.sbuf_base)]

    def sb(name, shape, dt=F32, off=None):
        nb = 4 * int(np.prod(shape[1:]))
        if off is None:
            off = (at[0] + 31) // 32 * 32
            at[0] = off + nb
        t = nc.alloc_sbuf_tensor_at(name, list(shape), dt, offset=off)
        return t, off

    X, _ = sb("X", [P, KT, T])
    Hhi, oHhi = sb("Hhi", [P, KT, T], F32R)
    Hlo, oHlo = sb("Hlo", [P, KT, T], F32R)
    Ahi, oAhi = sb("Ahi", [P, KT, T], F32R)
    Alo, oAlo = sb("Alo", [P, KT, T], F32R)
    RAW = [sb(f"raw{i}", [P, 1024])[0] for i in range(NRAW)]
    WH = [sb(f"wh{i}", [P, 1024], F32R)[0] for i in range(NW)]
    WL = [sb(f"wl{i}", [P, 1024], F32R)[0] for i in range(NW)]
    R, _ = sb("R", [P, T])
    SS, _ = sb("SS", [P, T])
    SS2, _ = sb("SS2", [P, T])
    TM = [sb(f"tm{i}", [P, T + 2])[0] for i in range(NTMP)]
    vec, _ = sb("vec", [P, NVEC])
    gfm, _ = sb("gfm", [P, 8])
    ident, _ = sb("ident", [P, P])
    ones, _ = sb("ones", [P, P])
    st, _ = sb("st", [P, 8, 16])
    rt, _ = sb("rt", [P, 16])
    rt2, _ = sb("rt2", [P, 16])
    small, _ = sb("small", [P, 64])
    M = (at[0] + 31) // 32 * 32
    KB = 1024
    VT, _ = sb("VT", [P, 4, D], off=M)
    MC, _ = sb("MC", [P, KT, T], off=M)
    QR, _ = sb("QR", [P, 4, T], off=M + 16 * KB)
    KR, _ = sb("KR", [P, 4, T], off=M + 24 * KB)
    O, _ = sb("O", [P, KT, T], off=M + 16 * KB)
    MGhi, _ = sb("MGhi", [P, KT, T], F32R, off=M + 16 * KB)
    QI, _ = sb("QI", [P, 4, T], off=M + 32 * KB)
    KS, _ = sb("KS", [P, 4, T], off=M + 40 * KB)
    SG, _ = sb("SG", [P, KT, T], off=M + 32 * KB)
    MGlo, _ = sb("MGlo", [P, KT, T], F32R, off=M + 32 * KB)
    KST, _ = sb("KST", [P, T], off=M + 48 * KB)
    ST, _ = sb("ST", [P, T], off=M + 50 * KB)
    STATE, _ = sb("STATE", [P, 8, 256], off=M + 52 * KB)
    SCM, _ = sb("SCM", [P, T], off=M + 60 * KB)
    CAU, _ = sb("CAU", [P, T], off=M + 62 * KB)
    EBD, _ = sb("EBD", [P, 4, 2, 8], off=M + 64 * KB)
    NQ, _ = sb("NQ", [P, 4, T], off=M)
    NK, _ = sb("NK", [P, 4, T], off=M + 8 * KB)
    VB, _ = sb("VB", [P, 8, T], off=M + 16 * KB)
    RB = [sb(f"RB{i}", [P, 2, BW], off=M + 32 * KB + 2304 * i)[0] for i in range(2)]
    NAM, _ = sb("NAM", [P, 3, 32], off=M + 37 * KB)
    RQ, _ = sb("RQ", [P, 2, T], off=M + 38 * KB)
    RK, _ = sb("RK", [P, 2, T], off=M + 42 * KB)
    RV, _ = sb("RV", [P, 4, T], off=M + 46 * KB)
    RG, _ = sb("RG", [P, 4, T], off=M + 54 * KB)
    NV, _ = sb("NV", [P, 4, T], off=oAhi + 8 * KB)
    ROPE, _ = sb("ROPE", [P, 2, T], off=oAlo + 8 * KB)
    GD, _ = sb("GD", [P, GW], off=oAlo + 12 * KB)
    GE0, _ = sb("GE0", [P, GW], off=M + 54 * KB)
    GE1, _ = sb("GE1", [P, GW], off=M + 54 * KB + 4 * GW)
    RS, _ = sb("RS", [P, T], off=M + 62 * KB)
    GE2, _ = sb("GE2", [P, GW], off=oAlo + 8 * KB)
    YH, _ = sb("YH", [P, 4, T], off=oAhi + 8 * KB)
    assert M + 64 * KB + 256 <= 229376, M
    PS = nc.alloc_psum_tensor("ps", [P, 8, 512], F32)
    BK = [PS[:, i, :] for i in range(8)]

    def f32(ap):
        return ap.bitcast(F32)

    def vc(name, i=0, n=1):
        return vec[:, VECO[name] + i:VECO[name] + i + n]

    class Slot:
        def __init__(self, t):
            self.t = t
            self.free = []

    tring = [Slot(t) for t in TM]
    tpos = [0]

    def tmp():
        s = tring[tpos[0] % NTMP]
        tpos[0] += 1
        s.ap = s.t[:, 0:T]
        return s

    bfree = [[] for _ in range(8)]
    mpos = [0]
    spos = [0]

    mset = [list(range(7))]

    def mbank():
        b = mset[0][mpos[0] % len(mset[0])]
        mpos[0] += 1
        return b

    def sbank():
        b = 3 + spos[0] % 4
        spos[0] += 1
        return b

    vec_tok = DMA("A", "dv", vec[:, :], dr["vec"])
    on_tok = V(lambda e: e.memset(ones[:, :], 1.0))

    units = []

    def add(name, n, k0=0, k1=8):
        units.append((dr[name][n, :, k0:k1, :], (k1 - k0)))

    def addv(name, half):
        for kk in range(4):
            units.append((dr[name][half, :, 2 * kk:2 * kk + 2, :], 8))

    FG = [(0, 8), (8, 16), (16, 22)]

    def add_ffn(gu, dn):
        for a, b in FG:
            for j in range(a, b):
                add(gu, j)
                add(gu, FT + j)
            for n in range(KT):
                add(dn, n, a, b)

    add_ffn("w_gu1", "w_d1")
    add("w_glr", 0)
    addv("w_v", 0)
    addv("w_v", 1)
    for h in range(4):
        add("w_q", h)
        add("w_k", h)
    for i in range(8):
        add("w_cc", i)
        add("w_cu", i)
        add("w_cb", i)
    for i in range(8):
        add("w_ga", i)
        add("w_oc", i)
    for i in range(8):
        add("w_r", i)
    for i in range(8):
        add("w_gb", i)
    for i in range(8):
        add("w_og", i)
    for i in range(8):
        add("w_o", i)
    add_ffn("w_gu2", "w_d2")
    addv("w_nv", 0)
    addv("w_rv", 0)
    for i in range(2):
        add("w_rq", i)
        add("w_rk", i)
    for i in range(4):
        add("w_nq", i)
        add("w_nk", i)
    for i in range(4):
        add("w_rg", i)
    for i in range(8):
        add("w_out2", i)
    for g in range(4):
        for j in range(8):
            add("w_up", 8 * g + j)
        for n in range(KT):
            add("w_dn", n, 8 * g, 8 * g + 8)
    NU = len(units)

    dtok = [None] * NU
    htok = [None] * NU
    ltok = [None] * NU
    ptok = [None] * NU

    def load(u):
        if u >= NU:
            return
        src, nb = units[u]
        if u == 0:
            for i in range(4):
                first_d[i] = DMA("S", f"df{i}", RAW[0][:, 256 * i:256 * i + 256].rearrange("p (k n) -> p k n", k=2),
                                 src[:, 2 * i:2 * i + 2, :])
            return
        w = [htok[u - NRAW], ltok[u - NRAW]] if u >= NRAW else []
        shape = [int(s) for s in src.shape]
        dst = RAW[u % NRAW][:, 0:128 * nb].rearrange("p (k n) -> p k n", k=shape[1])
        dtok[u] = DMA("S", f"dw{u % NRAW}", dst, src, *w)

    first_d, first_l = [None] * 4, [None] * 4

    def split_first(i):
        c = slice(256 * i, 256 * i + 256)
        htok[0] = A(lambda e: e.activation(WH[0][:, c], RAW[0][:, c], ACT.Copy), first_d[i])
        ltok[0] = first_l[i] = V(lambda e: e.tensor_tensor(WL[0][:, c], RAW[0][:, c], f32(WH[0][:, c]), ALU.subtract),
                                 htok[0])

    def split(u):
        if u >= NU:
            return
        n = 128 * units[u][1]
        raw, wh, wl = RAW[u % NRAW][:, 0:n], WH[u % NW][:, 0:n], WL[u % NW][:, 0:n]
        w = ptok[u - NW] if u >= NW else None
        htok[u] = A(lambda e: e.activation(wh, raw, ACT.Copy), dtok[u], w)
        ltok[u] = V(lambda e: e.tensor_tensor(wl, raw, f32(wh), ALU.subtract), htok[u])
        load(u + NRAW)

    cur = [0]
    pend = []
    late = [False]
    side = []

    def step(pe, evac, nside=1):
        u = cur[0]
        cur[0] += 1
        if not late[0]:
            flush()
        tok = pe(u)
        ptok[u] = tok[-1] if isinstance(tok, list) else tok
        for _ in range(min(nside, len(side))):
            side.pop(0)()
        if not late[0]:
            flush()
        split(u + NW - 1)
        pend.append(lambda: evac(tok))

    def flush():
        while pend:
            pend.pop(0)()

    def lin(rhi, rlo, rtok, evac, nside=1):
        b = mbank()
        ps = BK[b][:, :]

        def pe(u):
            nb = units[u][1]
            wh, wl = WH[u % NW], WL[u % NW]
            tok = None
            for k in range(nb):
                kc = slice(k * P, k * P + P)
                first = [ltok[u], *bfree[b]] if k == 0 else []
                if u == 0:
                    first = [first_l[k // 2]]
                PE(lambda e, k=k, kc=kc: e.matmul(ps, wh[:, kc], rhi[:, k, :], start=(k == 0), stop=False),
                   rtok[k], *first)
                PE(lambda e, k=k, kc=kc: e.matmul(ps, wh[:, kc], rlo[:, k, :], start=False, stop=False))
                tok = PE(lambda e, k=k, kc=kc: e.matmul(ps, wl[:, kc], rhi[:, k, :], start=False, stop=(k == nb - 1)),
                         sig=(k == nb - 1))
            return tok

        def ev(tok):
            bfree[b] = evac(ps, tok)

        step(pe, ev, nside)

    def linv(rhi, rlo, rtok, dst, htag):
        bs = [sbank() for _ in range(4)]
        for kk in range(4):
            def pe(u, kk=kk):
                wh, wl = WH[u % NW], WL[u % NW]
                toks = []
                for t in range(4):
                    ps = BK[bs[t]][:, :]
                    tc = slice(t * P, t * P + P)
                    for j in range(2):
                        k = 2 * kk + j
                        wc = slice(j * 512, j * 512 + 512)
                        first = [ltok[u], rtok[k], *(bfree[bs[t]] if kk == 0 else [])]
                        PE(lambda e, ps=ps, k=k, tc=tc, wc=wc: e.matmul(
                            ps, rhi[:, k, tc], wh[:, wc], start=(k == 0), stop=False), *first)
                        PE(lambda e, ps=ps, k=k, tc=tc, wc=wc: e.matmul(
                            ps, rlo[:, k, tc], wh[:, wc], start=False, stop=False))
                        tok = PE(lambda e, ps=ps, k=k, tc=tc, wc=wc: e.matmul(
                            ps, rhi[:, k, tc], wl[:, wc], start=False, stop=(k == 7)), sig=(j == 1))
                    toks.append(tok)
                return toks

            def ev(toks, kk=kk):
                if kk < 3:
                    return
                for t in range(4):
                    a = A(lambda e, t=t: e.activation(dst(t), BK[bs[t]][:, :], ACT.Copy, scale=rt[:, t:t + 1]),
                          toks[t], rt_tok[0], *dst_free[0])
                    bfree[bs[t]] = [a]
                    vt_tok[htag, t] = a

            step(pe, ev)

    vt_tok = {}
    dst_free = [[]]

    R_tok = [None]
    rt_tok = [None]
    x_tok = [None] * KT
    h_tok = [None] * KT
    a_tok = [None] * KT

    def rsq(dst, src, n, sc, *waits):
        m, s, y, t, t2 = (st[:, i, 0:n] for i in range(5))
        v = V(lambda e: e.tensor_scalar(m, src, sc, EPS, ALU.mult, ALU.add), *waits)
        a = A(lambda e: e.activation(s, m, ACT.Sqrt), v)
        v = V(lambda e: e.reciprocal(y, s), a)
        v = V(lambda e: e.tensor_tensor(t, y, y, ALU.mult), v)
        v = V(lambda e: e.tensor_tensor(t2, t, m, ALU.mult), v)
        v = V(lambda e: e.tensor_scalar(t, t2, -0.5, 1.5, ALU.mult, ALU.add), v)
        return V(lambda e: e.tensor_tensor(dst, y, t, ALU.mult), v)

    def token_sums(col, srcs, toks, n=1):
        tok = None
        for t in range(4):
            for i, s in enumerate(srcs):
                tok = PE(lambda e, t=t, i=i, s=s: e.matmul(
                    BK[7][:, col + t * n:col + t * n + 1], s[:, t * P:t * P + P], ones[:, 0:1],
                    start=(i == 0), stop=(i == len(srcs) - 1)), *toks, on_tok, *bfree[7], sig=(t == 3))
        return tok

    def rows(src, n, tok, b=None):
        b = sbank() if b is None else b
        for t in range(4):
            p = PE(lambda e, t=t: e.matmul(BK[b][:, t * P:t * P + P], src[:, t * n:t * n + 1].broadcast_to([P, P]),
                                           ident[:, :], start=True, stop=True), tok, c_tok, *bfree[b], sig=(t == 3))
        return b, p

    ss_tok = [None]

    def square_into(acc, key, n, src, tok, scale=None):
        kw = {} if scale is None else {"scale": scale}
        if n == 0:
            key[0] = A(lambda e: e.activation(acc[:, :], src, ACT.Square, **kw), tok, *key[1:])
        else:
            q = tmp()
            a = A(lambda e: e.activation(q.ap, src, ACT.Square, **kw), tok, *q.free)
            key[0] = V(lambda e: e.tensor_tensor(acc[:, :], acc[:, :], q.ap, ALU.add), a, key[0])
            q.free = [key[0]]

    def to_h(n, gname, tok, garr=None):
        g = garr[:, n:n + 1] if garr is not None else vc(gname, n)
        a = A(lambda e: e.activation(Hhi[:, n, :], X[:, n, :], ACT.Copy, scale=g), tok, vec_tok)
        h_tok[n] = V(lambda e: e.scalar_tensor_tensor(out=Hlo[:, n, :], in0=X[:, n, :], scalar=g,
                                                      in1=f32(Hhi[:, n, :]), op0=ALU.mult, op1=ALU.subtract), a)

    def norm_side():
        keep = {}

        def one():
            keep["p"] = token_sums(0, [SS], [ss_tok[0]])
            keep["v"] = rsq(rt[:, 0:4], BK[7][:, 0:4], 4, 1.0 / D, keep["p"], *rt_free)
            bfree[7] = [keep["v"]]
            rt_tok[0] = keep["v"]

        def two():
            b, p = rows(rt, 1, keep["v"], 7)
            R_tok[0] = V(lambda e: e.tensor_copy(R[:, :], BK[b][:, :]), p)
            bfree[b] = [R_tok[0]]
            late[0] = False

        late[0] = True
        side.insert(0, two)
        side.insert(0, one)

    rt_free = []

    def hilo(hi, lo, src, tok, *waits):
        a = A(lambda e: e.activation(hi, src, ACT.Copy), tok, *waits)
        return V(lambda e: e.tensor_tensor(lo, src, f32(hi), ALU.subtract), a), a

    def ffn(nxt):
        for gi, (a, b) in enumerate(FG):
            keep = {}
            for j in range(a, b):
                def ev_g(ps, tok):
                    t, s, m = tmp(), tmp(), tmp()
                    v = V(lambda e: e.tensor_tensor(t.ap, ps, R[:, :], ALU.mult), tok, R_tok[0], *t.free)
                    q = A(lambda e: e.activation(s.ap, t.ap, ACT.Silu), v, *s.free)
                    w = V(lambda e: e.tensor_tensor(m.ap, s.ap, R[:, :], ALU.mult), q, *m.free)
                    t.free, s.free = [q], [w]
                    keep["m"] = (m, w)
                    return [v]

                def ev_u(ps, tok, j=j - a):
                    m, w = keep["m"]
                    t = tmp()
                    v = V(lambda e: e.tensor_tensor(t.ap, ps, m.ap, ALU.mult), tok, w, *t.free)
                    m.free = [v]
                    a_tok[j], _ = hilo(Ahi[:, j, :], Alo[:, j, :], t.ap, v)
                    t.free = [a_tok[j]]
                    return [v]

                lin(Hhi, Hlo, h_tok, ev_g)
                lin(Hhi, Hlo, h_tok, ev_u)
            for n in range(KT):
                def ev_d(ps, tok, n=n, last=(gi == len(FG) - 1)):
                    x_tok[n] = v = V(lambda e: e.scalar_tensor_tensor(
                        out=X[:, n, :], in0=ps, scalar=0.5, in1=X[:, n, :], op0=ALU.mult, op1=ALU.add),
                        tok, x_tok[n])
                    if last:
                        nxt(n)
                    return [v]
                lin(Ahi, Alo, a_tok, ev_d)

    load(0)
    for n in range(KT):
        x_tok[n] = DMA("A" if n < 4 else "S", f"dx{n}", X[:, n, :], dr["xt"][n])
    for u in range(1, NRAW):
        load(u)
    c_tok = DMA("A", "dc", ident[:, :], dr["ident"])
    for n in range(KT):
        if n < 4:
            split_first(n)
        to_h(n, "g1", x_tok[n])
    load(NRAW)
    for u in range(1, NW - 1):
        split(u)
    for n in range(KT):
        square_into(SS, ss_tok, n, X[:, n, :], x_tok[n])
    norm_side()
    side.insert(0, lambda: None)

    def after_ffn1(n):
        to_h(n, "gm", x_tok[n])
        square_into(SS, ss_tok, n, X[:, n, :], x_tok[n])
        if n == KT - 1:
            norm_side()

    ffn(after_ffn1)

    mix_c = [DMA("A", "dm", KR[0:16, 2, :], dr["gup"]), DMA("A", "dm", SCM[:, :], dr["scm"]), DMA("A", "dm", CAU[:, :], dr["cau"])][-1]
    st_tok = V(lambda e: e.memset(ST[:, :], 0.0))
    gl = {}

    def ev_glr(ps, tok):
        gl["v"] = V(lambda e: e.tensor_tensor(KR[0:16, 3, :], ps[0:16, :], R[0:16, :], ALU.mult), tok, R_tok[0])
        return [gl["v"]]

    b_tok = [None] * 4

    def gate(h):
        def go():
            b = sbank_small()
            p = PE(lambda e: e.matmul(BK[b][:, :], KR[0:16, 2, h * P:h * P + P], KR[0:16, 3, :],
                                      start=True, stop=True), gl["v"], mix_c, *bfree[b], sig=True)
            z, e1, m = tmp(), tmp(), tmp()
            v = V(lambda e: e.tensor_scalar(z.ap, BK[b][:, :], vc("gb", h), None, ALU.add), p, vec_tok, *z.free)
            bfree[b] = [v]
            a = A(lambda e: e.activation(e1.ap, z.ap, ACT.Abs), v, *e1.free)
            a = A(lambda e: e.activation(e1.ap, e1.ap, ACT.Exp, scale=-1.0), a)
            a = A(lambda e: e.activation(e1.ap, e1.ap, ACT.Ln, bias=1.0), a)
            v = V(lambda e: e.scalar_tensor_tensor(out=m.ap, in0=z.ap, scalar=0.0, in1=e1.ap,
                                                   op0=ALU.min, op1=ALU.subtract), a, *m.free)
            z.free = e1.free = [v]
            b_tok[h] = V(lambda e: e.tensor_tensor_scan(KS[:, h, :], SCM[:, :], m.ap, 0.0, ALU.mult, ALU.add),
                         v, mix_c)
            m.free = [b_tok[h]]
        return go

    def sbank_small():
        return 7

    C64 = 64
    eb_tok = [None] * 4
    E = {}

    def chunks(ap):
        return ap.rearrange("p (c t) -> p c t", t=C64)

    def decays(h):
        def go():
            b3 = chunks(KS[:, h, :])
            ref = b3[:, :, 31:32].broadcast_to([P, 8, C64])
            lst = b3[:, :, 63:64].broadcast_to([P, 8, C64])
            d1, e1, e2, e3 = tmp(), tmp(), tmp(), tmp()
            v = V(lambda e: e.tensor_tensor(chunks(d1.ap), b3, ref, ALU.subtract), b_tok[h], *d1.free)
            v2 = V(lambda e: e.tensor_tensor(chunks(e3.ap), lst, b3, ALU.subtract), b_tok[h], *e3.free)
            a1 = A(lambda e: e.activation(e1.ap, d1.ap, ACT.Exp, scale=1 / 16), v, *e1.free)
            a2 = A(lambda e: e.activation(e2.ap, d1.ap, ACT.Exp, scale=-1 / 16), v, *e2.free)
            a3 = A(lambda e: e.activation(e3.ap, e3.ap, ACT.Exp, scale=1 / 16), v2)
            a4 = A(lambda e: e.activation(EBD[:, h, 0, :], b3[:, :, 31], ACT.Exp, scale=1 / 16), b_tok[h])
            a5 = A(lambda e: e.activation(EBD[:, h, 1, :], b3[:, :, 63], ACT.Exp, scale=1 / 16), b_tok[h])
            d1.free = [a2]
            E[h] = (e1, e2, e3, a1, a2, a3, a4, a5)
        return go

    q_tok = [None] * 4
    k_tok = [None] * 4

    def ev_q(h):
        def ev(ps, tok):
            e1, a1, a4 = E[h][0], E[h][3], E[h][6]
            t = tmp()
            v = V(lambda e: e.scalar_tensor_tensor(out=t.ap, in0=ps, scalar=P ** -0.5, in1=R[:, :],
                                                   op0=ALU.mult, op1=ALU.mult), tok, R_tok[0], *t.free)
            w = V(lambda e: e.tensor_tensor(QR[:, h, :], t.ap, e1.ap, ALU.mult), v, a1)
            e1.free = t.free = [w]
            q_tok[h] = V(lambda e: e.tensor_tensor(chunks(QI[:, h, :]), chunks(QR[:, h, :]),
                                                   EBD[:, h, 0, :].unsqueeze(2).broadcast_to([P, 8, C64]),
                                                   ALU.mult), w, a4)
            return [v]
        return ev

    def ev_k(h):
        def ev(ps, tok):
            _, e2, e3, _, a2, a3, a4, a5 = E[h]
            t = tmp()
            v = V(lambda e: e.tensor_tensor(t.ap, ps, R[:, :], ALU.mult), tok, R_tok[0], *t.free)
            w = V(lambda e: e.tensor_tensor(KR[:, h, :], t.ap, e2.ap, ALU.mult), v, a2)
            k_tok[h] = V(lambda e: e.tensor_tensor(KS[:, h, :], t.ap, e3.ap, ALU.mult), v, a3, a5)
            e2.free, e3.free = [w], [k_tok[h]]
            t.free = [k_tok[h]]
            gla(h)
            return [v]
        return ev

    gk = {"kst": None, "st": st_tok, "state": None, "kstfree": [], "stfree": [], "statefree": []}
    o_tok = [None] * KT
    os_tok = [None]

    def osl(i):
        return 4 * (i % 2) + i // 2

    def gla(h):
        L = {}

        def turn():
            b = sbank()
            for t in range(4):
                p = PE(lambda e, t=t: e.transpose(BK[b][:, t * P:t * P + P], KS[:, h, t * P:t * P + P], ident[:, :]),
                       k_tok[h], c_tok, *bfree[b], sig=(t == 3))
            L["kst"] = A(lambda e: e.activation(KST[:, :], BK[b][:, :], ACT.Copy), p, *gk["kstfree"])
            bfree[b] = [L["kst"]]

        def scores():
            b = sbank()
            for t in range(4):
                tc = slice(t * P, t * P + P)
                p = PE(lambda e, tc=tc: e.matmul(BK[b][:, tc], KR[:, h, tc], QR[:, h, tc], start=True, stop=True),
                       k_tok[h], q_tok[h], *bfree[b], sig=(t == 3))
            L["sp"] = p
            L["st"] = V(lambda e: e.copy_predicated(ST[:, :], CAU[:, :].bitcast(I32), BK[b][:, :]),
                        p, st_tok, mix_c, *gk["stfree"])
            bfree[b] = [L["st"]]

        def kv(cs):
            def go():
                if cs[0] == 0:
                    L["v"] = V(lambda e: e.memset(STATE[:, 0, :], 0.0), *gk["statefree"])
                bs = [sbank(), sbank()]
                for c in cs:
                    b = bs[c % 2]
                    pt = slice(64 * (c % 2), 64 * (c % 2) + 64)
                    cc = slice(256 * (c // 2 % 2), 256 * (c // 2 % 2) + 256)
                    p = PE(lambda e, c=c, pt=pt, cc=cc, b=b: e.matmul(
                        BK[b][:, cc], KST[pt, (c // 2) * P:(c // 2) * P + P],
                        VT[pt, c // 2, 256 * h:256 * h + 256], start=True, stop=True),
                        L["kst"], vt_tok[h // 2, c // 2], *bfree[b], sig=(c == cs[-1]))
                for c in cs:
                    cc = slice(256 * (c // 2 % 2), 256 * (c // 2 % 2) + 256)
                    L["v"] = V(lambda e, c=c, cc=cc, b=bs[c % 2]: e.scalar_tensor_tensor(
                        out=STATE[:, c + 1, :], in0=STATE[:, c, :], scalar=EBD[:, h, 1, c:c + 1],
                        in1=BK[b][:, cc], op0=ALU.mult, op1=ALU.add), p, L["v"], E[h][7])
                for b in bs:
                    bfree[b] = [L["v"]]
                gk["kstfree"] = [p]
            return go

        def outs():
            sq = []
            for d in range(2):
                b = sbank()
                vcs = slice(256 * h + 128 * d, 256 * h + 128 * d + 128)
                for t in range(4):
                    tc = slice(t * P, t * P + P)
                    PE(lambda e, t=t, tc=tc, b=b, vcs=vcs: e.matmul(
                        BK[b][:, tc], VT[:, t, vcs], ST[:, tc], start=(t == 0), stop=False, skip_group_check=True),
                        L["st"], *[vt_tok[h // 2, i] for i in range(4)], *bfree[b])
                for c in range(1, 8):
                    tc = slice(c * C64, c * C64 + C64)
                    p = PE(lambda e, c=c, tc=tc, b=b, d=d: e.matmul(
                        BK[b][:, tc], STATE[:, c, 128 * d:128 * d + 128], QI[:, h, tc], start=False, stop=(c == 7),
                        skip_group_check=True), L["v"], sig=(c == 7))
                i = 2 * h + d
                o_tok[i] = V(lambda e, i=i, b=b: e.tensor_copy(O[:, osl(i), :], BK[b][:, :]), p)
                bfree[b] = [o_tok[i]]
                s = tmp()
                a = A(lambda e, i=i, s=s: e.activation(s.ap, O[:, osl(i), :], ACT.Square), o_tok[i], *s.free)
                sq.append((s, a))
            L["sq"] = sq
            gk["stfree"] = [p]
            gk["statefree"] = [p]
            gk["last"] = p

        def sums():
            (s0, a0), (s1, a1) = L["sq"]
            p = token_sums(16 + h, [s0.ap, s1.ap], [a0, a1], n=4)
            s0.free = s1.free = [p]
            os_tok[0] = p

        side.extend([turn, scores, kv([0, 1, 2, 3]), kv([4, 5, 6]), outs, sums])

    def gla_norm():
        def stats():
            ot["v"] = rsq(rt2[:, 0:16], BK[7][:, 16:32], 16, 1.0 / 256, os_tok[0])
            bfree[7] = [ot["v"]]

        def scale(h):
            def go():
                b, p = rows(rt2[:, h:16], 4, ot["v"])
                for i in (2 * h, 2 * h + 1):
                    o_tok[i] = V(lambda e, i=i: e.tensor_tensor(O[:, osl(i), :], O[:, osl(i), :], BK[b][:, :], ALU.mult),
                                 p, o_tok[i])
                bfree[b] = [o_tok[2 * h + 1]]
            return go
        ot = {}
        side.extend([stats] + [scale(h) for h in range(4)])

    mset[0] = [0, 1, 2]
    lin(Hhi, Hlo, h_tok, ev_glr)
    pr.put("A", lambda e: e.preload_act_table_set("natural_log_exp_and_others"), [])
    flush_side = lambda: [side.pop(0)() for _ in range(len(side))]
    for half in range(2):
        if half == 1:
            side.extend([gate(h) for h in range(4)])
        linv(Hhi, Hlo, h_tok, lambda t, half=half: VT[:, t, 512 * half:512 * half + 512], half)
    for h in range(4):
        side.insert(0, decays(h))
        lin(Hhi, Hlo, h_tok, ev_q(h))
        lin(Hhi, Hlo, h_tok, ev_k(h))
    cv = {}
    pad = {}

    def ev_cc(ps, tok):
        t = tmp()
        v = V(lambda e: e.tensor_tensor(t.ap, ps, R[:, :], ALU.mult), tok, R_tok[0], *t.free)
        cv["cc"] = (t, v)
        return [v]

    def ev_cu(i):
        def ev(ps, tok):
            c, cw = cv["cc"]
            t, u, y = tmp(), tmp(), tmp()
            v = V(lambda e: e.tensor_tensor(t.ap, ps, R[:, :], ALU.mult), tok, R_tok[0], *t.free)
            z = V(lambda e: e.memset(u.t[:, 0:2], 0.0), *u.free)
            w = V(lambda e: e.tensor_tensor(u.t[:, 2:T + 2], t.ap, c.ap, ALU.mult), v, cw, *u.free)
            t.free = c.free = [w]
            a = A(lambda e: e.activation(y.ap, u.t[:, 0:T], ACT.Copy, scale=vc("cw0", i)), z, w, vec_tok, *y.free)
            w = V(lambda e: e.scalar_tensor_tensor(out=y.ap, in0=u.t[:, 1:T + 1], scalar=vc("cw1", i), in1=y.ap,
                                                   op0=ALU.mult, op1=ALU.add), a)
            w = V(lambda e: e.scalar_tensor_tensor(out=y.ap, in0=u.t[:, 2:T + 2], scalar=vc("cw2", i), in1=y.ap,
                                                   op0=ALU.mult, op1=ALU.add), w)
            u.free = [w]
            cv["y"] = (y, w)
            return [v]
        return ev

    def ev_cb(i):
        def ev(ps, tok):
            y, yw = cv["y"]
            t, r = tmp(), tmp()
            v = V(lambda e: e.tensor_tensor(t.ap, ps, R[:, :], ALU.mult), tok, R_tok[0], *t.free)
            w = V(lambda e: e.tensor_tensor(r.ap, t.ap, y.ap, ALU.mult), v, yw, *r.free)
            t.free = y.free = [w]
            a_tok[i], _ = hilo(Ahi[:, i, :], Alo[:, i, :], r.ap, w)
            r.free = [a_tok[i]]
            return [v]
        return ev

    for i in range(8):
        lin(Hhi, Hlo, h_tok, ev_cc)
        lin(Hhi, Hlo, h_tok, ev_cu(i))
        lin(Hhi, Hlo, h_tok, ev_cb(i))
    flush_side()

    def gated(func, dst=None):
        hold = {}

        def ev(ps, tok):
            t = tmp()
            v = V(lambda e: e.tensor_tensor(t.ap, ps, R[:, :], ALU.mult), tok, R_tok[0], *t.free)
            if dst is None:
                s = tmp()
                a = A(lambda e: e.activation(s.ap, t.ap, func), v, *s.free)
                hold["s"] = s
            else:
                a = A(lambda e: e.activation(dst, t.ap, func), v, gk["last"])
            t.free = [a]
            hold["a"] = a
            return [v]
        return ev, hold

    m_tok = [None] * KT
    gla_norm()
    for i in range(8):
        ev, hold = gated(ACT.Sigmoid)
        lin(Hhi, Hlo, h_tok, ev)

        def ev_oc(ps, tok, i=i, hold=hold):
            s = hold["s"]
            m_tok[i] = V(lambda e: e.tensor_tensor(MC[:, i, :], ps, s.ap, ALU.mult), tok, hold["a"], gk["last"])
            s.free = [m_tok[i]]
            return [m_tok[i]]
        lin(Ahi, Alo, a_tok, ev_oc)
    flush_side()
    for i in range(8):
        def ev_r(ps, tok, i=i):
            t, s, g = tmp(), tmp(), tmp()
            v = V(lambda e: e.tensor_tensor(t.ap, ps, R[:, :], ALU.mult), tok, R_tok[0], *t.free)
            a = A(lambda e: e.activation(s.ap, t.ap, ACT.Silu), v, *s.free)
            t.free = [a]
            w = V(lambda e: e.scalar_tensor_tensor(out=g.ap, in0=O[:, osl(i), :], scalar=vc("gla", i), in1=s.ap,
                                                   op0=ALU.mult, op1=ALU.mult), a, o_tok[i], vec_tok, *g.free)
            s.free = [w]
            a_tok[i], _ = hilo(Ahi[:, i, :], Alo[:, i, :], g.ap, w)
            g.free = [a_tok[i]]
            return [v]
        lin(Hhi, Hlo, h_tok, ev_r)
    sg = []
    for i in range(8):
        ev, hold = gated(ACT.Sigmoid, SG[:, i, :])
        sg.append(hold)
        lin(Hhi, Hlo, h_tok, ev)
    mg_tok = [None] * KT
    for i in range(8):
        def ev_og(ps, tok, i=i):
            t, m = tmp(), tmp()
            v = V(lambda e: e.tensor_tensor(t.ap, ps, SG[:, i, :], ALU.mult), tok, sg[i]["a"], *t.free)
            w = V(lambda e: e.tensor_tensor(m.ap, t.ap, MC[:, i, :], ALU.add), v, m_tok[i], *m.free)
            t.free = [w]
            mg_tok[i], _ = hilo(MGhi[:, i, :], MGlo[:, i, :], m.ap, w, a_tok[7])
            m.free = [mg_tok[i]]
            return [v]
        lin(Ahi, Alo, a_tok, ev_og)
    for n in range(8):
        def ev_o(ps, tok, n=n):
            x_tok[n] = v = V(lambda e: e.tensor_tensor(X[:, n, :], ps, X[:, n, :], ALU.add), tok, x_tok[n])
            to_h(n, "g2", v)
            square_into(SS, ss_tok, n, X[:, n, :], v)
            if n == KT - 1:
                norm_side()
            return [v]
        lin(MGhi, MGlo, mg_tok, ev_o)

    g_tok = V(lambda e: e.tensor_tensor(gfm[:, :], vc("gf", 0, 8), vc("gm2", 0, 8), ALU.mult), vec_tok)
    ss2_tok = [None]

    def after_ffn2(n):
        to_h(n, None, x_tok[n], garr=gfm)
        square_into(SS, ss_tok, n, X[:, n, :], x_tok[n])
        square_into(SS2, ss2_tok, n, X[:, n, :], x_tok[n], scale=vc("gf", n))
        if n < KT - 1:
            return
        L = {}

        def one():
            token_sums(0, [SS], [ss_tok[0]])
            p = token_sums(4, [SS2], [ss2_tok[0]])
            r1, r2, q, m = rt2[:, 0:4], rt2[:, 4:8], rt2[:, 8:12], rt2[:, 12:16]
            v = rsq(r1, BK[7][:, 0:4], 4, 1.0 / D, p)
            L["r1"] = v
            w = V(lambda e: e.tensor_tensor(q, r1, r1, ALU.mult), v)
            w = V(lambda e: e.tensor_tensor(m, q, BK[7][:, 4:8], ALU.mult), w)
            bfree[7] = [w]
            w = rsq(r2, m, 4, 1.0 / D, w)
            L["v"] = V(lambda e: e.tensor_tensor(rt[:, 0:4], r1, r2, ALU.mult), w)
            rt_tok[0] = L["v"]

        def two():
            b, p = rows(rt, 1, L["v"], 7)
            R_tok[0] = V(lambda e: e.tensor_copy(R[:, :], BK[b][:, :]), p)
            bfree[b] = [R_tok[0]]
            b2, p2 = rows(rt2, 1, L["r1"], 7)
            L["w"] = V(lambda e: e.tensor_copy(SS2[:, :], BK[b2][:, :]), p2)
            bfree[b2] = [L["w"]]
            late[0] = False

        def x2(n):
            def go():
                x_tok[n] = V(lambda e: e.scalar_tensor_tensor(
                    out=X[:, n, :], in0=X[:, n, :], scalar=vc("gf", n), in1=SS2[:, :], op0=ALU.mult, op1=ALU.mult),
                    L["w"], x_tok[n], h_tok[n], ss_tok[0], ss2_tok[0])
            return go
        late[0] = True
        side[0:0] = [one, two] + [(lambda n=n: (x2(2 * n)(), x2(2 * n + 1)())) for n in range(4)]

    mset[0] = list(range(7))
    ffn(after_ffn2)

    mset[0] = [0, 1]
    m_end = ptok[cur[0] - 1]
    gd_tok = DMA("A", "dg", GD[:, :], dr["gd"], m_end)
    rope_tok = DMA("A", "dr", ROPE[:, :, :], dr["rope"], m_end)
    nam_tok = DMA("A", "dn", NAM[:, :, :], dr["nam"], m_end)
    nq_tok = [None] * 4
    nk_tok = [None] * 4
    BS = [0, 8, 24, 32]
    vb_tok = {}

    def bands():
        for cb in range(4):
            for i in range(8):
                vb_tok[cb] = DMA("G", f"vb{cb}", VB[32 * (i % 4):32 * (i % 4) + 32, 2 * cb + i // 4, :],
                                 NV[64 * (i % 2) + BS[cb]:64 * (i % 2) + BS[cb] + 32, i // 2, :],
                                 vt_tok["n", i // 2])

    rbt = {}
    rb_free = [[m_end], [m_end]]

    def raw_bias(hp):
        for j in range(2):
            rbt[hp] = DMA("G", f"rb{hp % 2}", RB[hp % 2][:, j, :], dr["rpb"][2 * hp + j], *rb_free[hp % 2])

    ge = [GE0[:, :], GE1[:, :], GE2[:, :], GE0[:, :]]
    ge_tok = [None] * 4
    ge_free = [[m_end], [m_end], [], []]
    lg = small[:, 32:40]
    l1, l2, l3 = small[:, 40:48], small[:, 48:56], small[:, 56:64]
    lgt = {}

    def log_gamma():
        a = A(lambda e: e.activation(l1, vc("dec", 0, 8), ACT.Exp), vec_tok)
        v = V(lambda e: e.tensor_scalar(l2, l1, -1.0, 1.0, ALU.mult, ALU.add), a)
        a = A(lambda e: e.activation(lg, l2, ACT.Ln), v)
        v = V(lambda e: e.tensor_scalar(l3, l2, -1.0, 1.0, ALU.mult, ALU.add), v)
        v = V(lambda e: e.tensor_scalar(l3, l3, 1e-30, None, ALU.max), v)
        v = V(lambda e: e.reciprocal(l3, l3), v)
        v = V(lambda e: e.tensor_tensor(l3, l3, l1, ALU.mult), v)
        lgt["t"] = V(lambda e: e.tensor_tensor(lg, lg, l3, ALU.mult), v, a)

    def strip(h):
        def go():
            v = V(lambda e: e.tensor_scalar(ge[h], GD[:, :], 0.0, lg[:, h:h + 1], ALU.max, ALU.mult),
                  gd_tok, lgt["t"], *ge_free[h])
            t0, t1 = tmp(), tmp()
            for t, c0, c1 in ((t0, 0, 448), (t1, 448, 896)):
                w = V(lambda e, t=t, c0=c0, c1=c1: e.tensor_scalar(
                    t.ap[:, 0:c1 - c0], GD[:, c0:c1], 0.0, lg[:, 4 + h:5 + h], ALU.min, ALU.mult),
                    gd_tok, *t.free)
                v = V(lambda e, t=t, c0=c0, c1=c1: e.tensor_tensor(
                    ge[h][:, c0:c1], ge[h][:, c0:c1], t.ap[:, 0:c1 - c0], ALU.subtract), v, w)
                t.free = [v]
            ge_tok[h] = A(lambda e: e.activation(ge[h], ge[h], ACT.Exp), v)
        return go

    dst_free[0] = [m_end]
    raw_bias(0)
    raw_bias(1)
    side.extend([log_gamma, strip(0), strip(1)])
    linv(Hhi, Hlo, h_tok, lambda t: NV[:, t, :], "n")
    linv(Hhi, Hlo, h_tok, lambda t: RV[:, t, :], "r")
    bands()

    PAT = [0, 1, 1, 2]
    OFF = [0, -8, -8, -16]
    na = {}
    ob = {}
    na_tok = [None] * 4

    def na_s(p):
        hp, cb = p // 4, p % 4
        k3 = NK[:, hp, :].rearrange("p (r c) -> p r c", c=64)
        bm = tmp()
        g = G(lambda e: e.tensor_tensor(
            bm.ap.rearrange("p (h i j) -> p h i j", h=2, j=32),
            RB[hp % 2][:, :, 16 + OFF[cb]:16 + OFF[cb] + 256].rearrange("p h (i j) -> p h i j", j=32),
            NAM[:, PAT[cb], :].unsqueeze(1).unsqueeze(1).broadcast_to([P, 2, 8, 32]), ALU.add),
            rbt[hp], nam_tok, *bm.free)
        if cb == 3:
            rb_free[hp % 2] = [g]
            if hp + 2 < 4:
                raw_bias(hp + 2)
        for j in range(2):
            hs = slice(64 * j, 64 * j + 64)
            pt = PE(lambda e, j=j, hs=hs: e.matmul(
                BK[3 + j][:, 0:256], NQ[hs, hp, cb * P:cb * P + P], k3[hs, :, BS[cb]:BS[cb] + 32],
                start=True, stop=True), nq_tok[hp], nk_tok[hp], *bfree[3 + j], sig=(j == 1))
        s, mx = tmp(), 4 * (p % 2)
        v = V(lambda e: e.tensor_tensor(s.ap.rearrange("p (h k) -> p h k", h=2), PS[:, 3:5, 0:256],
                                        bm.ap.rearrange("p (h k) -> p h k", h=2), ALU.add), pt, g, *s.free)
        bfree[3] = bfree[4] = [v]
        bm.free = [v]
        s3 = s.ap.rearrange("p (h k) -> p h k", h=2)
        nm, rs, ri = (small[:, 8 * i + mx:8 * i + mx + 2] for i in range(3))
        v = V(lambda e: e.tensor_reduce(nm, s3, AX_X, ALU.max, negate=True), v, *na.get(("free", p % 2), []))
        for j in range(2):
            a = A(lambda e, j=j: e.activation(s3[:, j, :], s3[:, j, :], ACT.Exp, bias=nm[:, j:j + 1],
                                              accum_out=rs[:, j:j + 1]), v)
        v = V(lambda e: e.reciprocal(ri, rs), a)
        for j in range(2):
            w = V(lambda e, j=j: e.tensor_scalar(s3[:, j, :], s3[:, j, :], ri[:, j:j + 1], None, ALU.mult), v)
        na["free", p % 2] = [w]
        na[p] = (s, w)

    def na_t(p):
        s, w = na[p]
        b = 5
        for i in range(4):
            pt = PE(lambda e, i=i: e.transpose(BK[b][:, i * P:i * P + P], s.ap[:, i * P:i * P + P], ident[:, :]),
                    w, *bfree[b], sig=(i == 3))
        s.free = [pt]
        t = tmp()
        a = A(lambda e: e.activation(t.ap, BK[b][:, :], ACT.Copy), pt, *t.free)
        bfree[b] = [a]
        na[p] = (t, a)

    def na_o(p):
        hp, cb = p // 4, p % 4
        t, a = na.pop(p)
        b = 6
        for j in range(2):
            for i in range(2):
                pt = PE(lambda e, j=j, i=i: e.matmul(
                    BK[b][64 * j:64 * j + 64, cb * P:cb * P + P],
                    VB[:, 2 * cb + i, (2 * hp + j) * 64:(2 * hp + j) * 64 + 64],
                    t.ap[:, (2 * j + i) * P:(2 * j + i) * P + P], start=(i == 0), stop=(i == 1)),
                    a, vb_tok[cb], *(bfree[b] if cb == 0 else []), sig=(i == 1 and j == 1))
        t.free = [pt]
        if cb == 3:
            src = BK[b][:, :].rearrange("p (c r q) -> p r c q", c=4, q=16)
            hi = Ahi[:, hp, :].rearrange("p (r c q) -> p r c q", r=8, q=16)
            lo = Alo[:, hp, :].rearrange("p (r c q) -> p r c q", r=8, q=16)
            o = tmp()
            o4 = o.ap.rearrange("p (r c q) -> p r c q", r=8, q=16)
            v = V(lambda e: e.tensor_copy(o4, src), pt, *o.free)
            bfree[b] = [v]
            na_tok[hp], _ = hilo(Ahi[:, hp, :], Alo[:, hp, :], o.ap, v)
            o.free = [na_tok[hp]]

    def na_task(t):
        def go():
            if t < 16:
                na_s(t)
            if 0 <= t - 1 < 16:
                na_t(t - 1)
            if 0 <= t - 2 < 16:
                na_o(t - 2)
        return go

    rot_tok = {}

    def ev_rot(dst, key, sc):
        def ev(ps, tok):
            t, s = tmp(), tmp()
            v = V(lambda e: e.scalar_tensor_tensor(out=t.ap, in0=ps, scalar=sc, in1=R[:, :], op0=ALU.mult,
                                                   op1=ALU.mult), tok, R_tok[0], *t.free)
            for q in range(4):
                o = q ^ 1
                a = A(lambda e, q=q, o=o: e.activation(s.ap[32 * q:32 * q + 32, :], t.ap[32 * o:32 * o + 32, :],
                                                       ACT.Copy), v, *s.free)
            w = V(lambda e: e.tensor_tensor(t.ap, t.ap, ROPE[:, 0, :], ALU.mult), a, rope_tok)
            w2 = V(lambda e: e.tensor_tensor(s.ap, s.ap, ROPE[:, 1, :], ALU.mult), a)
            rot_tok[key] = V(lambda e: e.tensor_tensor(dst, t.ap, s.ap, ALU.add), w, w2, m_end)
            t.free = s.free = [rot_tok[key]]
            return [v]
        return ev

    y_tok = [None] * 4
    rs_ = {}
    rg_free = [None]
    rring = [Slot(t) for t in (SS, SS2, RS)]
    for s_ in rring:
        s_.ap = s_.t[:, :]
        s_.free = [m_end, R_tok[0], *x_tok]

    def ret_s(i):
        h, jt = i // 4, i % 4
        b = 7
        hs = slice(64 * (h % 2), 64 * (h % 2) + 64)
        pt = PE(lambda e: e.matmul(BK[b][:, :], RK[hs, h // 2, jt * P:jt * P + P], RQ[hs, h // 2, :],
                                   start=True, stop=True),
                rot_tok["q", h // 2], rot_tok["k", h // 2], *bfree[b], sig=True)
        if i == 7:
            rs_["h1"] = pt
        t = rring[i % 3]
        v = V(lambda e: e.tensor_tensor(t.ap, BK[b][:, :], ge[h][:, 384 - 128 * jt:896 - 128 * jt], ALU.mult),
              pt, ge_tok[h], *t.free)
        bfree[b] = [v]
        rs_[i] = (t, v)
        if i == 3:
            ge_free[3] = [v]
        if i == 15:
            rg_free[0] = v

    def ret_o(i):
        h, jt = i // 4, i % 4
        t, v = rs_.pop(i)
        b = 2
        p = PE(lambda e: e.matmul(BK[b][:, :], RV[:, jt, h * P:h * P + P], t.ap, start=(jt == 0), stop=(jt == 3)),
               v, vt_tok["r", jt], *(bfree[b] if jt == 0 else []), sig=True)
        t.free = [p]
        if jt == 3:
            y_tok[h] = A(lambda e: e.activation(YH[:, h, :], BK[b][:, :], ACT.Copy), p, *vb_tok.values())
            bfree[b] = [y_tok[h]]

    yc_tok = [None] * 4
    sq_ = {}

    def ret_m(h):
        b = 7
        p = PE(lambda e: e.matmul(BK[b][:, :], ones[:, :], YH[:, h, :], start=True, stop=True),
               y_tok[h], *bfree[b], sig=True)
        yc_tok[h] = V(lambda e: e.scalar_tensor_tensor(out=YH[:, h, :], in0=BK[b][:, :], scalar=-1.0 / P,
                                                       in1=YH[:, h, :], op0=ALU.mult, op1=ALU.add), p)
        bfree[b] = [yc_tok[h]]
        s = (RQ if h % 2 else RK)[:, 0, :]
        a = A(lambda e: e.activation(s, YH[:, h, :], ACT.Square), yc_tok[h], rs_["h1"], sq_.get("p"))
        sq_[h] = (s, a)

    def ret_v(h):
        s, a = sq_[h]
        p = sq_["p"] = token_sums(16 + h, [s], [a], n=4)
        sq_["v"] = V(lambda e: e.tensor_copy(st[:, 5, h:16:4], BK[7][:, 16 + h:32:4]), p)
        bfree[7] = [sq_["v"]]

    mix_tok = [None] * KT

    def ret_task(i):
        def go():
            if i < 16:
                ret_s(i)
            if i >= 2:
                ret_o(i - 2)
        return go

    def gn_stats():
        sq_["v"] = rsq(rt2[:, 0:16], st[:, 5, :], 16, 1.0 / P, sq_["v"], R_tok[0])

    def gn_scale(h):
        def go():
            b, p = rows(rt2[:, h:16], 4, sq_["v"], 7 if h % 2 else 2)
            t, s = tmp(), tmp()
            v = V(lambda e: e.tensor_tensor(t.ap, YH[:, h, :], BK[b][:, :], ALU.mult), p, yc_tok[h], *t.free)
            bfree[b] = [v]
            v = V(lambda e: e.scalar_tensor_tensor(out=s.ap, in0=t.ap, scalar=vc("rg", h), in1=RG[:, h, :],
                                                   op0=ALU.mult, op1=ALU.mult), v, rg_tok[h], *s.free)
            t.free = [v]
            mix_tok[4 + h], _ = hilo(Ahi[:, 4 + h, :], Alo[:, 4 + h, :], s.ap, v)
            s.free = [mix_tok[4 + h]]
        return go

    lin(Hhi, Hlo, h_tok, ev_rot(RQ[:, 0, :], ("q", 0), 1.0))
    lin(Hhi, Hlo, h_tok, ev_rot(RK[:, 0, :], ("k", 0), 0.125))
    flush_side()
    rets = []
    for i in range(18):
        rets.append(ret_task(i))
        if i == 6:
            rets += [strip(2), strip(3)]
        if i in (10, 11, 14):
            rets.append(lambda h={10: 0, 11: 1, 14: 2}[i]: ret_m(h))
        if i in (12, 13, 16):
            rets.append(lambda h={12: 0, 13: 1, 16: 2}[i]: ret_v(h))
    rets += [lambda: ret_m(3), lambda: ret_v(3), gn_stats]
    nas = [na_task(t) for t in range(18)]
    for ev in (ev_rot(RQ[:, 1, :], ("q", 1), 1.0), ev_rot(RK[:, 1, :], ("k", 1), 0.125)):
        side.extend(rets[0:3])
        del rets[0:3]
        lin(Hhi, Hlo, h_tok, ev, 3)
    ge_free[2] = [m_end]
    for i in range(4):
        def ev_nq(ps, tok, i=i):
            nq_tok[i] = V(lambda e: e.tensor_tensor(
                NQ[:, i, :].rearrange("p (c r q) -> p r c q", c=4, q=16),
                ps.rearrange("p (r c q) -> p r c q", r=8, q=16),
                R[:, :].rearrange("p (r c q) -> p r c q", r=8, q=16), ALU.mult), tok, R_tok[0], m_end)
            return [nq_tok[i]]

        def ev_nk(ps, tok, i=i):
            nk_tok[i] = V(lambda e: e.scalar_tensor_tensor(out=NK[:, i, :], in0=ps, scalar=0.125, in1=R[:, :],
                                                           op0=ALU.mult, op1=ALU.mult), tok, R_tok[0], m_end)
            return [nk_tok[i]]
        for ev in (ev_nq, ev_nk):
            side.extend(rets[0:2])
            del rets[0:2]
            if i:
                side[1:1] = [nas.pop(0)]
                side.append(nas.pop(0))
            lin(Hhi, Hlo, h_tok, ev, len(side))
    rg_tok = [None] * 4
    for i in range(4):
        def ev_rg(ps, tok, i=i):
            t = tmp()
            v = V(lambda e: e.tensor_tensor(t.ap, ps, R[:, :], ALU.mult), tok, R_tok[0], *t.free)
            rg_tok[i] = A(lambda e: e.activation(RG[:, i, :], t.ap, ACT.Silu), v, rg_free[0])
            t.free = [rg_tok[i]]
            return [v]
        side.extend(rets[0:2])
        del rets[0:2]
        if nas:
            side[1:1] = [nas.pop(0)]
        if nas:
            side.append(nas.pop(0))
        lin(Hhi, Hlo, h_tok, ev_rg, len(side))
    flush()
    side.extend(rets + nas + [gn_scale(h) for h in range(4)])
    flush_side()
    for h in range(4):
        mix_tok[h] = na_tok[h]
    mset[0] = list(range(7))
    for n in range(8):
        def ev_o2(ps, tok, n=n):
            x_tok[n] = v = V(lambda e: e.tensor_tensor(X[:, n, :], ps, X[:, n, :], ALU.add), tok, x_tok[n])
            to_h(n, "gl2", v)
            square_into(SS, ss_tok, n, X[:, n, :], v)
            if n == KT - 1:
                norm_side()
            return [v]
        lin(Ahi, Alo, mix_tok, ev_o2)

    fin = {}
    for g in range(4):
        for j in range(8):
            def ev_up(ps, tok, j=j):
                t, m = tmp(), tmp()
                v = V(lambda e: e.tensor_tensor(t.ap, ps, R[:, :], ALU.mult), tok, R_tok[0], *t.free)
                w = V(lambda e: e.scalar_tensor_tensor(out=m.ap, in0=t.ap, scalar=0.0, in1=t.ap, op0=ALU.max,
                                                       op1=ALU.mult), v, *m.free)
                t.free = [w]
                a_tok[j], _ = hilo(Ahi[:, j, :], Alo[:, j, :], m.ap, w)
                m.free = [a_tok[j]]
                return [v]
            lin(Hhi, Hlo, h_tok, ev_up)
        for n in range(8):
            def ev_dn(ps, tok, n=n, last=(g == 3)):
                x_tok[n] = v = V(lambda e: e.tensor_tensor(X[:, n, :], ps, X[:, n, :], ALU.add), tok, x_tok[n])
                if last and n < KT - 1:
                    square_into(SS, ss_tok, n, X[:, n, :], v)
                elif last:
                    fin["s"] = tmp()
                    fin["a"] = A(lambda e: e.activation(fin["s"].ap, X[:, n, :], ACT.Square), v, *fin["s"].free)
                if last:
                    x_tok[n] = A(lambda e: e.activation(X[:, n, :], X[:, n, :], ACT.Copy, scale=vc("gf2", n)), v)
                return [v]
            lin(Ahi, Alo, a_tok, ev_dn)
    flush()
    p = token_sums(0, [SS, fin["s"].ap], [ss_tok[0], fin["a"]])
    v = rsq(rt[:, 0:4], BK[7][:, 0:4], 4, 1.0 / D, p)
    _, p = rows(rt, 1, v, 6)
    for n in range(8):
        v = V(lambda e, n=n: e.tensor_tensor(X[:, n, :], X[:, n, :], BK[6][:, :], ALU.mult), p, x_tok[n])
        o = DMA("S", "do", out[n], X[:, n, :], v)
    pr.put("S", None, [o])
    assert cur[0] == NU, (cur[0], NU)

    with ExitStack() as ctx:
        sems = {s: ctx.enter_context(nc.semaphore(f"s_{s}")) for s in pr.n}
        block = ctx.enter_context(nc.Block())

        @block.sync
        def _(e):
            pr.run("S", e, sems)

        @block.scalar
        def _(e):
            pr.run("A", e, sems)

        @block.vector
        def _(e):
            pr.run("V", e, sems)

        @block.gpsimd
        def _(e):
            pr.run("G", e, sems)

        @block.tensor
        def _(e):
            pr.run("P", e, sems)


def _tiles(w):
    k, n = w.shape
    return np.ascontiguousarray(w.reshape(k // P, P, n // P, P).transpose(2, 1, 0, 3))


def _wide(w):
    k, n = w.shape
    return np.ascontiguousarray(w.reshape(k // P, P, n // 512, 512).transpose(2, 1, 0, 3))


def _col(v):
    return v.reshape(-1, P).T


def _layout(a):
    f = np.float32
    m = {}
    m["xt"] = np.ascontiguousarray(a["x"][0].T).reshape(KT, P, T)
    m["w_gu1"] = _tiles(a["ffn1_w_gu"][0])
    m["w_d1"] = _tiles(a["ffn1_w_down"][0])
    m["w_gu2"] = _tiles(a["ffn2_w_gu"][0])
    m["w_d2"] = _tiles(a["ffn2_w_down"][0])
    w = a["w_in"][0]
    sizes = [("cb", D), ("cc", D), ("cu", D), ("q", 512), ("k", 512), ("v", D), ("glr", 16), ("r", D), ("ga", D),
             ("gb", D)]
    o = 0
    for name, n in sizes:
        part = w[:, o:o + n]
        o += n
        if name == "glr":
            part = np.concatenate([part, np.zeros((D, P - n), f)], axis=1)
        m["w_" + name] = _wide(part) if name == "v" else _tiles(part)
    m["w_oc"] = _tiles(a["w_out_conv"][0])
    m["w_og"] = _tiles(a["w_out_gla"][0])
    m["w_o"] = _tiles(a["w_o"][0])
    w = a["w_in_2"][0]
    o = 0
    for name, n in [("nq", 512), ("nk", 512), ("nv", 512), ("rq", 256), ("rk", 256), ("rv", 512), ("rg", 512)]:
        part = w[:, o:o + n]
        o += n
        m["w_" + name] = _wide(part) if name in ("nv", "rv") else _tiles(part)
    m["w_out2"] = _tiles(a["w_out_2"][0])
    m["w_up"] = _tiles(a["w_up_2"][0])
    m["w_dn"] = _tiles(a["w_down_2"][0])
    m["gup"] = np.ascontiguousarray(a["gate_w_up"][0])
    dec = np.concatenate([a["ret_decay_fwd_2"][0], a["ret_decay_bwd_2"][0]])
    parts = dict(g1=_col(a["norm_ffn1_g"][0]), gm=_col(a["norm_mix_g"][0]), g2=_col(a["norm_ffn2_g"][0]),
                 gf=_col(a["final_norm_g"]), gm2=_col(a["norm_mix_2"][0]), gl2=_col(a["norm_mlp_2"][0]),
                 gf2=_col(a["norm_final_2"]), gla=_col(a["gla_norm_g"][0]), gb=_col(a["gate_b"][0]),
                 cw0=_col(a["conv_w"][0, 0]), cw1=_col(a["conv_w"][0, 1]), cw2=_col(a["conv_w"][0, 2]),
                 rg=_col(a["ret_norm_gain_2"][0]), dec=np.broadcast_to(dec, (P, 8)))
    m["vec"] = np.ascontiguousarray(np.concatenate([parts[n] for n in VEC], axis=1))
    rpb = a["na_rpb_2"][0]
    flat = np.concatenate([np.zeros((8, 32), f), np.concatenate([rpb, np.zeros((8, 15, 1), f)], axis=2).reshape(8, 480),
                           np.zeros((8, 32), f)], axis=1)
    r, q, n = np.meshgrid(np.arange(8), np.arange(16), np.arange(BW), indexing="ij")
    at = 32 + (7 - r) * 32 + 15 - q - 16 + n
    m["rpb"] = np.ascontiguousarray(flat[:, at.reshape(P, BW)])
    return m


def _constants():
    f = np.float32
    m = {}
    m["ident"] = np.eye(P, dtype=f)
    t = np.arange(T)
    m["scm"] = np.ascontiguousarray(np.broadcast_to((t % 64 != 0).astype(f), (P, T)))
    j, i = np.arange(P)[:, None], (t % P)[None, :]
    m["cau"] = ((i // 64 == j // 64) & (i >= j)).astype(f)
    qj, kj = np.arange(16)[:, None], np.arange(32)[None, :]
    nam = np.zeros((3, 16, 32), f)
    for p, cb in enumerate((0, 1, 3)):
        col = 16 * cb + qj
        key = [0, 8, 24, 32][cb] + kj
        lo = np.clip(col - 8, 0, 48)
        nam[p] = np.where((key >= lo) & (key < lo + 16), 0.0, -1e30)
    m["nam"] = np.ascontiguousarray(np.tile(nam.transpose(1, 0, 2), (8, 1, 1)))
    inv = (f(1.0) / (f(10000.0) ** (np.arange(0, 64, 2, dtype=f) / f(64)))).astype(f)
    ang = (t.astype(f)[None, :] * inv[:, None]).astype(f).astype(np.float64)
    cos, sin = np.cos(ang).astype(f), np.sin(ang).astype(f)
    m["rope"] = np.ascontiguousarray(np.stack([np.concatenate([cos, cos, cos, cos]),
                                               np.concatenate([-sin, sin, -sin, sin])], axis=1))
    m["gd"] = (np.arange(GW)[None, :] - np.arange(P)[:, None] - 384).astype(f)
    return m


def kernel(**inputs):
    import concourse.bacc as _bacc
    from concourse.bass_utils import run_bass_kernel_spmd as _run

    arrays = {**_layout({k: np.asarray(v) for k, v in inputs.items()}), **_constants()}
    nc = _bacc.Bacc("TRN2", target_bir_lowering=False, num_devices=1)
    dr = {n: nc.dram_tensor(f"in_{n}", v.shape, F32, kind="ExternalInput").ap() for n, v in arrays.items()}
    out = nc.dram_tensor("out_0", (KT, P, T), F32, kind="ExternalOutput").ap()
    build(nc, dr, out)
    r = _run(nc, [{f"in_{n}": v for n, v in arrays.items()}], core_ids=[0])
    got = r.results[0]["out_0"]
    return np.ascontiguousarray(got.reshape(D, T).T).reshape(1, T, D)
```

```python
from contextlib import ExitStack

import numpy as np

import concourse.bass as bass
from concourse import mybir

ALU = mybir.AluOpType
ACT = mybir.ActivationFunctionType
AX_X = mybir.AxisListType.X
F32 = mybir.dt.float32
F32R = mybir.dt.float32r
I32 = mybir.dt.int32

P = 128
T = 512
D = 1024
KT = D // P
FF = 2816
FT = FF // P
FF2 = 4096
EPS = 1e-6
NRAW = 3
NW = 3
NTMP = 9

VEC = ["g1", "gm", "g2", "gf", "gm2", "gl2", "gf2", "gla", "gb", "cw0", "cw1", "cw2", "rg", "dec"]
VECN = dict(g1=8, gm=8, g2=8, gf=8, gm2=8, gl2=8, gf2=8, gla=8, gb=4, cw0=8, cw1=8, cw2=8, rg=4, dec=8)
VECO = {}
_o = 0
for _n in VEC:
    VECO[_n] = _o
    _o += VECN[_n]
NVEC = _o
GW = 896
BW = 272


class Prog:

    def __init__(self):
        self.q = {e: [] for e in "PAVGS"}
        self.n = {}
        self.seen = {e: {} for e in "PAVGS"}

    def put(self, eng, fn, waits, sem=None, by=1):
        need = {}
        for w in waits:
            if w is not None:
                need[w[0]] = max(need.get(w[0], 0), w[1])
        todo = []
        for s, v in need.items():
            if self.seen[eng].get(s, 0) < v:
                self.seen[eng][s] = v
                todo.append((s, v))
        tok = None
        if sem is not None:
            self.n[sem] = self.n.get(sem, 0) + by
            tok = (sem, self.n[sem])
        self.q[eng].append((todo, fn, sem, by))
        return tok

    def run(self, eng, e, sems):
        for todo, fn, sem, by in self.q[eng]:
            for s, v in todo:
                e.wait_ge(sems[s], v)
            if fn is None:
                continue
            ins = fn(e)
            if sem is not None:
                ins.then_inc(sems[sem], by)


def build(nc, dr, out):
    pr = Prog()

    def V(fn, *waits):
        return pr.put("V", fn, waits, "V")

    def A(fn, *waits):
        return pr.put("A", fn, waits, "A")

    def G(fn, *waits):
        return pr.put("G", fn, waits, "G")

    def PE(fn, *waits, sig=False):
        return pr.put("P", fn, waits, "P" if sig else None)

    def DMA(q, sem, dst, src, *waits):
        return pr.put(q, lambda e: e.dma_start(dst, src), waits, sem, 16)

    at = [int(nc.sbuf_base)]

    def sb(name, shape, dt=F32, off=None):
        nb = 4 * int(np.prod(shape[1:]))
        if off is None:
            off = (at[0] + 31) // 32 * 32
            at[0] = off + nb
        t = nc.alloc_sbuf_tensor_at(name, list(shape), dt, offset=off)
        return t, off

    X, _ = sb("X", [P, KT, T])
    Hhi, oHhi = sb("Hhi", [P, KT, T], F32R)
    Hlo, oHlo = sb("Hlo", [P, KT, T], F32R)
    Ahi, oAhi = sb("Ahi", [P, KT, T], F32R)
    Alo, oAlo = sb("Alo", [P, KT, T], F32R)
    RAW = [sb(f"raw{i}", [P, 1024])[0] for i in range(NRAW)]
    WH = [sb(f"wh{i}", [P, 1024], F32R)[0] for i in range(NW)]
    WL = [sb(f"wl{i}", [P, 1024], F32R)[0] for i in range(NW)]
    R, _ = sb("R", [P, T])
    SS, _ = sb("SS", [P, T])
    SS2, _ = sb("SS2", [P, T])
    TM = [sb(f"tm{i}", [P, T + 2])[0] for i in range(NTMP)]
    vec, _ = sb("vec", [P, NVEC])
    gfm, _ = sb("gfm", [P, 8])
    ident, _ = sb("ident", [P, P])
    ones, _ = sb("ones", [P, P])
    st, _ = sb("st", [P, 8, 16])
    rt, _ = sb("rt", [P, 16])
    rt2, _ = sb("rt2", [P, 16])
    small, _ = sb("small", [P, 80])
    M = (at[0] + 31) // 32 * 32
    KB = 1024
    VT, _ = sb("VT", [P, 4, D], off=M)
    MC, _ = sb("MC", [P, KT, T], off=M)
    QR, _ = sb("QR", [P, 4, T], off=M + 16 * KB)
    KR, _ = sb("KR", [P, 4, T], off=M + 24 * KB)
    O, _ = sb("O", [P, KT, T], off=M + 16 * KB)
    MGhi, _ = sb("MGhi", [P, KT, T], F32R, off=M + 16 * KB)
    QI, _ = sb("QI", [P, 4, T], off=M + 32 * KB)
    KS, _ = sb("KS", [P, 4, T], off=M + 40 * KB)
    SG, _ = sb("SG", [P, KT, T], off=M + 32 * KB)
    MGlo, _ = sb("MGlo", [P, KT, T], F32R, off=M + 32 * KB)
    KST, _ = sb("KST", [P, T], off=M + 48 * KB)
    ST, _ = sb("ST", [P, T], off=M + 50 * KB)
    STATE, _ = sb("STATE", [P, 4, 256], off=M + 52 * KB)
    QO, _ = sb("QO", [P, 2, 256], off=M + 56 * KB)
    KE, _ = sb("KE", [P, 2, 256], off=M + 58 * KB)
    SCM, _ = sb("SCM", [P, T], off=M + 60 * KB)
    CAU, _ = sb("CAU", [P, T], off=M + 62 * KB)
    EBD, _ = sb("EBD", [P, 4, 4, 8], off=M + 64 * KB)
    NQ, _ = sb("NQ", [P, 4, T], off=M)
    NK, _ = sb("NK", [P, 4, T], off=M + 8 * KB)
    VB, _ = sb("VB", [P, 8, T], off=M + 16 * KB)
    RB = [sb(f"RB{i}", [P, 2, BW], off=M + 32 * KB + 2304 * i)[0] for i in range(2)]
    NAM, _ = sb("NAM", [P, 3, 32], off=M + 37 * KB)
    RQ, _ = sb("RQ", [P, 2, T], off=M + 38 * KB)
    RK, _ = sb("RK", [P, 2, T], off=M + 42 * KB)
    RV, _ = sb("RV", [P, 4, T], off=M + 46 * KB)
    NV, _ = sb("NV", [P, 4, T], off=oAhi + 8 * KB)
    ROPE, _ = sb("ROPE", [P, 2, T], off=oAlo + 8 * KB)
    GD, _ = sb("GD", [P, GW], off=oAlo + 12 * KB)
    GE0, _ = sb("GE0", [P, GW], off=M + 54 * KB)
    GE1, _ = sb("GE1", [P, GW], off=M + 54 * KB + 4 * GW)
    RS, _ = sb("RS", [P, T], off=M + 62 * KB)
    GE2, _ = sb("GE2", [P, GW], off=oAlo + 8 * KB)
    YH, _ = sb("YH", [P, 4, T], off=oAhi + 8 * KB)
    assert M + 64 * KB + 512 <= 229376, M
    PS = nc.alloc_psum_tensor("ps", [P, 8, 512], F32)
    BK = [PS[:, i, :] for i in range(8)]

    def f32(ap):
        return ap.bitcast(F32)

    def vc(name, i=0, n=1):
        return vec[:, VECO[name] + i:VECO[name] + i + n]

    class Slot:
        def __init__(self, t):
            self.t = t
            self.free = []

    tring = [Slot(t) for t in TM]
    tpos = [0]

    def tmp():
        s = tring[tpos[0] % NTMP]
        tpos[0] += 1
        s.ap = s.t[:, 0:T]
        return s

    bfree = [[] for _ in range(8)]
    mpos = [0]
    spos = [0]

    mset = [list(range(7))]

    def mbank():
        b = mset[0][mpos[0] % len(mset[0])]
        mpos[0] += 1
        return b

    def sbank():
        b = 3 + spos[0] % 4
        spos[0] += 1
        return b

    vec_tok = DMA("A", "dv", vec[:, :], dr["vec"])
    on_tok = V(lambda e: e.memset(ones[:, :], 1.0))

    units = []

    def add(name, n, k0=0, k1=8):
        units.append((dr[name][n, :, k0:k1, :], (k1 - k0)))

    def addv(name, half):
        for kk in range(4):
            units.append((dr[name][half, :, 2 * kk:2 * kk + 2, :], 8))

    FG = [(0, 8), (8, 16), (16, 22)]

    def add_ffn(gu, dn):
        for a, b in FG:
            for j in range(a, b):
                add(gu, j)
                add(gu, FT + j)
            for n in range(KT):
                add(dn, n, a, b)

    add_ffn("w_gu1", "w_d1")
    add("w_glr", 0)
    addv("w_v", 0)
    addv("w_v", 1)
    for h in range(4):
        add("w_q", h)
        add("w_k", h)
    for i in range(8):
        add("w_cc", i)
        add("w_cu", i)
        add("w_cb", i)
    for i in range(8):
        add("w_ga", i)
        add("w_oc", i)
    for i in range(8):
        add("w_r", i)
    for i in range(8):
        add("w_gb", i)
    for i in range(8):
        add("w_og", i)
    for i in range(8):
        add("w_o", i)
    add_ffn("w_gu2", "w_d2")
    addv("w_nv", 0)
    addv("w_rv", 0)
    for i in range(2):
        add("w_rq", i)
        add("w_rk", i)
    for i in range(4):
        add("w_nq", i)
        add("w_nk", i)
    for i in range(4):
        add("w_rg", i)
    for i in range(8):
        add("w_out2", i)
    for g in range(4):
        for j in range(8):
            add("w_up", 8 * g + j)
        for n in range(KT):
            add("w_dn", n, 8 * g, 8 * g + 8)
    NU = len(units)

    dtok = [None] * NU
    htok = [None] * NU
    ltok = [None] * NU
    ptok = [None] * NU

    def load(u):
        if u >= NU:
            return
        src, nb = units[u]
        if u == 0:
            for i in range(4):
                first_d[i] = DMA("S", f"df{i}", RAW[0][:, 256 * i:256 * i + 256].rearrange("p (k n) -> p k n", k=2),
                                 src[:, 2 * i:2 * i + 2, :])
            return
        w = [htok[u - NRAW], ltok[u - NRAW]] if u >= NRAW else []
        shape = [int(s) for s in src.shape]
        dst = RAW[u % NRAW][:, 0:128 * nb].rearrange("p (k n) -> p k n", k=shape[1])
        dtok[u] = DMA("S", f"dw{u % NRAW}", dst, src, *w)

    first_d, first_l = [None] * 4, [None] * 4

    def split_first(i):
        c = slice(256 * i, 256 * i + 256)
        htok[0] = A(lambda e: e.activation(WH[0][:, c], RAW[0][:, c], ACT.Copy), first_d[i])
        ltok[0] = first_l[i] = V(lambda e: e.tensor_tensor(WL[0][:, c], RAW[0][:, c], f32(WH[0][:, c]), ALU.subtract),
                                 htok[0])

    def split(u):
        if u >= NU:
            return
        n = 128 * units[u][1]
        raw, wh, wl = RAW[u % NRAW][:, 0:n], WH[u % NW][:, 0:n], WL[u % NW][:, 0:n]
        w = ptok[u - NW] if u >= NW else None
        htok[u] = A(lambda e: e.activation(wh, raw, ACT.Copy), dtok[u], w)
        ltok[u] = V(lambda e: e.tensor_tensor(wl, raw, f32(wh), ALU.subtract), htok[u])
        load(u + NRAW)

    cur = [0]
    pend = []
    late = [False]
    side = []

    mids = []

    def step(pe, evac, nside=1, mid=(), end=(), pre=()):
        u = cur[0]
        cur[0] += 1
        mids[:] = mid
        for f in pre:
            f()
        split(u + NW - 1)
        tok = pe(u)
        ptok[u] = tok[-1] if isinstance(tok, list) else tok
        pend.append(lambda: evac(tok))
        todo = [side.pop(0) for _ in range(min(nside, len(side)))]
        if not late[0]:
            flush()
        for f in todo:
            f()
        for f in end:
            f()
        if not late[0]:
            flush()

    def flush():
        while pend:
            pend.pop(0)()

    def lin(rhi, rlo, rtok, evac, nside=1, mid=(), end=(), pre=()):
        b = mbank()
        ps = BK[b][:, :]

        def pe(u):
            nb = units[u][1]
            wh, wl = WH[u % NW], WL[u % NW]
            tok = None
            for k in range(nb):
                while k == nb // 2 and mids:
                    mids.pop(0)()
                kc = slice(k * P, k * P + P)
                first = [ltok[u], *bfree[b]] if k == 0 else []
                if u == 0:
                    first = [first_l[k // 2]]
                PE(lambda e, k=k, kc=kc: e.matmul(ps, wh[:, kc], rhi[:, k, :], start=(k == 0), stop=False),
                   rtok[k], *first)
                PE(lambda e, k=k, kc=kc: e.matmul(ps, wh[:, kc], rlo[:, k, :], start=False, stop=False))
                tok = PE(lambda e, k=k, kc=kc: e.matmul(ps, wl[:, kc], rhi[:, k, :], start=False, stop=(k == nb - 1)),
                         sig=(k == nb - 1))
            return tok

        def ev(tok):
            bfree[b] = evac(ps, tok)

        step(pe, ev, nside, mid, end, pre)

    def linv(rhi, rlo, rtok, dst, htag, sums=None):
        bs = [sbank() for _ in range(4)]
        for kk in range(4):
            def pe(u, kk=kk):
                wh, wl = WH[u % NW], WL[u % NW]
                toks = []
                for t in range(4):
                    ps = BK[bs[t]][:, :]
                    tc = slice(t * P, t * P + P)
                    for j in range(2):
                        k = 2 * kk + j
                        wc = slice(j * 512, j * 512 + 512)
                        first = [ltok[u], rtok[k], *(bfree[bs[t]] if kk == 0 else [])]
                        PE(lambda e, ps=ps, k=k, tc=tc, wc=wc: e.matmul(
                            ps, rhi[:, k, tc], wh[:, wc], start=(k == 0), stop=False), *first)
                        PE(lambda e, ps=ps, k=k, tc=tc, wc=wc: e.matmul(
                            ps, rlo[:, k, tc], wh[:, wc], start=False, stop=False))
                        tok = PE(lambda e, ps=ps, k=k, tc=tc, wc=wc: e.matmul(
                            ps, rhi[:, k, tc], wl[:, wc], start=False, stop=(k == 7)), sig=(j == 1))
                    toks.append(tok)
                return toks

            def ev(toks, kk=kk):
                if kk < 3:
                    return
                for t in range(4):
                    for c in range(0, 512, 512 if sums is None else P):
                        kw = {} if sums is None else {"accum_out": sums(t, c // P)}
                        a = A(lambda e, t=t, c=c, kw=kw: e.activation(
                            dst(t) if sums is None else dst(t)[:, c:c + P],
                            BK[bs[t]][:, :] if sums is None else BK[bs[t]][:, c:c + P], ACT.Copy,
                            scale=rt[:, t:t + 1], **kw), toks[t], rt_tok[0], *dst_free[0])
                    bfree[bs[t]] = [a]
                    vt_tok[htag, t] = a

            step(pe, ev)

    vt_tok = {}
    dst_free = [[]]

    R_tok = [None]
    rt_tok = [None]
    x_tok = [None] * KT
    h_tok = [None] * KT
    a_tok = [None] * KT

    def rsq(dst, src, n, sc, *waits):
        m, s, y, t = (st[:, i, 0:n] for i in range(4))
        return newton(dst, m, s, y, t, src, sc, *waits)

    def newton(dst, m, s, y, t, src, sc, *waits):
        v = V(lambda e: e.tensor_scalar(m, src, sc, EPS, ALU.mult, ALU.add), *waits)
        a = A(lambda e: e.activation(s, m, ACT.Sqrt), v)
        v = V(lambda e: e.reciprocal(y, s), a)
        v = V(lambda e: e.scalar_tensor_tensor(out=t, in0=y, scalar=-0.5, in1=y, op0=ALU.mult, op1=ALU.mult), v)
        v = V(lambda e: e.tensor_tensor(t, t, m, ALU.mult), v)
        return V(lambda e: e.scalar_tensor_tensor(out=dst, in0=t, scalar=1.5, in1=y, op0=ALU.add, op1=ALU.mult), v)

    def rsq_rows(dst, b, srcs, n, toks, *waits):
        for i, x in enumerate(srcs):
            p = PE(lambda e, i=i, x=x: e.matmul(BK[b][:, :], ones[:, :], x, start=(i == 0), stop=(i == len(srcs) - 1)),
                   *toks, on_tok, *bfree[b], sig=(i == len(srcs) - 1))
        m, y, t = tmp(), tmp(), tmp()
        v = V(lambda e: e.tensor_scalar(m.ap, BK[b][:, :], 1.0 / n, EPS, ALU.mult, ALU.add), p, *m.free)
        bfree[b] = [v]
        a = A(lambda e: e.activation(y.ap, m.ap, ACT.Ln), v, *y.free)
        a = A(lambda e: e.activation(y.ap, y.ap, ACT.Exp, scale=-0.5), a)
        a = A(lambda e: e.activation(t.ap, y.ap, ACT.Square), a, *t.free)

        def newton_step():
            v = V(lambda e: e.scalar_tensor_tensor(out=m.ap, in0=t.ap, scalar=-0.5, in1=m.ap, op0=ALU.mult,
                                                   op1=ALU.mult), a)
            v = V(lambda e: e.scalar_tensor_tensor(out=m.ap if dst is None else dst, in0=m.ap, scalar=1.5, in1=y.ap,
                                                   op0=ALU.add, op1=ALU.mult), v, *waits)
            m.free = y.free = t.free = [v]
            return v, m
        return newton_step, p

    def token_sums(col, srcs, toks, n=1):
        tok = None
        for t in range(4):
            for i, s in enumerate(srcs):
                tok = PE(lambda e, t=t, i=i, s=s: e.matmul(
                    BK[7][:, col + t * n:col + t * n + 1], s[:, t * P:t * P + P], ones[:, 0:1],
                    start=(i == 0), stop=(i == len(srcs) - 1)), *toks, on_tok, *bfree[7], sig=(t == 3))
        return tok

    def rows(src, n, tok, b=None):
        b = sbank() if b is None else b
        for t in range(4):
            p = PE(lambda e, t=t: e.matmul(BK[b][:, t * P:t * P + P], src[:, t * n:t * n + 1].broadcast_to([P, P]),
                                           ident[:, :], start=True, stop=True), tok, c_tok, *bfree[b], sig=(t == 3))
        return b, p

    ss_tok = [None]

    def square_into(acc, key, n, src, tok, scale=None):
        kw = {} if scale is None else {"scale": scale}
        if n == 0:
            key[0] = A(lambda e: e.activation(acc[:, :], src, ACT.Square, **kw), tok, *key[1:])
        else:
            q = tmp()
            a = A(lambda e: e.activation(q.ap, src, ACT.Square, **kw), tok, *q.free)
            key[0] = V(lambda e: e.tensor_tensor(acc[:, :], acc[:, :], q.ap, ALU.add), a, key[0])
            q.free = [key[0]]

    def to_h(n, gname, tok, garr=None):
        g = garr[:, n:n + 1] if garr is not None else vc(gname, n)
        a = A(lambda e: e.activation(Hhi[:, n, :], X[:, n, :], ACT.Copy, scale=g), tok, vec_tok)
        h_tok[n] = V(lambda e: e.scalar_tensor_tensor(out=Hlo[:, n, :], in0=X[:, n, :], scalar=g,
                                                      in1=f32(Hhi[:, n, :]), op0=ALU.mult, op1=ALU.subtract), a)

    def norm_side():
        keep = {}

        def one():
            keep["p"] = token_sums(0, [SS], [ss_tok[0]])
            keep["v"] = rsq(rt[:, 0:4], BK[7][:, 0:4], 4, 1.0 / D, keep["p"], *rt_free)
            bfree[7] = [keep["v"]]
            rt_tok[0] = keep["v"]

        def two():
            b, p = rows(rt, 1, keep["v"], 7)
            R_tok[0] = V(lambda e: e.tensor_copy(R[:, :], BK[b][:, :]), p)
            bfree[b] = [R_tok[0]]
            late[0] = False

        late[0] = True
        side.insert(0, two)
        side.insert(0, one)

    def ln_table():
        pr.put("A", lambda e: e.preload_act_table_set("natural_log_exp_and_others"), [])

    def norm_rows():
        def one():
            ln_table()
            R_tok[0], _ = rsq_rows(R[:, :], 7, [SS[:, :]], D, [ss_tok[0]])[0]()
            late[0] = False

        late[0] = True
        side.insert(0, one)

    rt_free = []

    def hilo(hi, lo, src, tok, *waits):
        a = A(lambda e: e.activation(hi, src, ACT.Copy), tok, *waits)
        return V(lambda e: e.tensor_tensor(lo, src, f32(hi), ALU.subtract), a), a

    def ffn(nxt):
        for gi, (a, b) in enumerate(FG):
            keep = {}
            for j in range(a, b):
                def ev_g(ps, tok):
                    t, s, m = tmp(), tmp(), tmp()
                    v = V(lambda e: e.tensor_tensor(t.ap, ps, R[:, :], ALU.mult), tok, R_tok[0], *t.free)
                    q = A(lambda e: e.activation(s.ap, t.ap, ACT.Silu), v, *s.free)
                    w = V(lambda e: e.tensor_tensor(m.ap, s.ap, R[:, :], ALU.mult), q, *m.free)
                    t.free, s.free = [q], [w]
                    keep["m"] = (m, w)
                    return [v]

                def ev_u(ps, tok, j=j - a):
                    m, w = keep["m"]
                    t = tmp()
                    v = V(lambda e: e.tensor_tensor(t.ap, ps, m.ap, ALU.mult), tok, w, *t.free)
                    m.free = [v]
                    a_tok[j], _ = hilo(Ahi[:, j, :], Alo[:, j, :], t.ap, v)
                    t.free = [a_tok[j]]
                    return [v]

                lin(Hhi, Hlo, h_tok, ev_g)
                lin(Hhi, Hlo, h_tok, ev_u)
            for n in range(KT):
                def ev_d(ps, tok, n=n, last=(gi == len(FG) - 1)):
                    x_tok[n] = v = V(lambda e: e.scalar_tensor_tensor(
                        out=X[:, n, :], in0=ps, scalar=0.5, in1=X[:, n, :], op0=ALU.mult, op1=ALU.add),
                        tok, x_tok[n])
                    if last:
                        nxt(n)
                    return [v]
                lin(Ahi, Alo, a_tok, ev_d)

    load(0)
    for n in range(KT):
        x_tok[n] = DMA("A" if n < 4 else "S", f"dx{n}", X[:, n, :], dr["xt"][n])
    for u in range(1, NRAW):
        load(u)
    c_tok = DMA("A", "dc", ident[:, :], dr["ident"])
    for n in range(KT):
        if n < 4:
            split_first(n)
        to_h(n, "g1", x_tok[n])
    load(NRAW)
    split(1)
    for n in range(KT):
        square_into(SS, ss_tok, n, X[:, n, :], x_tok[n])
    norm_rows()
    side.insert(0, lambda: None)

    def after_ffn1(n):
        to_h(n, "gm", x_tok[n])
        square_into(SS, ss_tok, n, X[:, n, :], x_tok[n])
        if n == KT - 1:
            norm_side()

    ffn(after_ffn1)

    mix_c = [DMA("A", "dm", KR[0:16, 2, :], dr["gup"]), DMA("A", "dm", SCM[:, :], dr["scm"]), DMA("A", "dm", CAU[:, :], dr["cau"])][-1]
    st_tok = V(lambda e: e.memset(ST[:, :], 0.0))
    gl = {}

    def ev_glr(ps, tok):
        gl["v"] = V(lambda e: e.tensor_tensor(KR[0:16, 3, :], ps[0:16, :], R[0:16, :], ALU.mult), tok, R_tok[0])
        return [gl["v"]]

    b_tok = [None] * 4

    def gate(h):
        def go():
            b = sbank_small()
            p = PE(lambda e: e.matmul(BK[b][:, :], KR[0:16, 2, h * P:h * P + P], KR[0:16, 3, :],
                                      start=True, stop=True), gl["v"], mix_c, *bfree[b], sig=True)
            z, e1, m = tmp(), tmp(), tmp()
            v = V(lambda e: e.tensor_scalar(z.ap, BK[b][:, :], vc("gb", h), None, ALU.add), p, vec_tok, *z.free)
            bfree[b] = [v]
            a = A(lambda e: e.activation(e1.ap, z.ap, ACT.Abs), v, *e1.free)
            a = A(lambda e: e.activation(e1.ap, e1.ap, ACT.Exp, scale=-1.0), a)
            a = A(lambda e: e.activation(e1.ap, e1.ap, ACT.Ln, bias=1.0), a)
            v = V(lambda e: e.scalar_tensor_tensor(out=m.ap, in0=z.ap, scalar=0.0, in1=e1.ap,
                                                   op0=ALU.min, op1=ALU.subtract), a, *m.free)
            z.free = e1.free = [v]
            b_tok[h] = V(lambda e: e.tensor_tensor_scan(KS[:, h, :], SCM[:, :], m.ap, 0.0, ALU.mult, ALU.add),
                         v, mix_c)
            m.free = [b_tok[h]]
        return go

    def sbank_small():
        return 7

    C64 = 64
    eb_tok = [None] * 4
    E = {}

    def chunks(ap):
        return ap.rearrange("p (c t) -> p c t", t=C64)

    def decays(h):
        def go():
            b3 = chunks(KS[:, h, :])
            ref = b3[:, :, 31:32].broadcast_to([P, 8, C64])
            lst = b3[:, :, 63:64].broadcast_to([P, 8, C64])
            d1, e1, e2, e3 = tmp(), tmp(), tmp(), tmp()
            v = V(lambda e: e.tensor_tensor(chunks(d1.ap), b3, ref, ALU.subtract), b_tok[h], *d1.free)
            v2 = V(lambda e: e.tensor_tensor(chunks(e3.ap), lst, b3, ALU.subtract), b_tok[h], *e3.free)
            a1 = A(lambda e: e.activation(e1.ap, d1.ap, ACT.Exp, scale=1 / 16), v, *e1.free)
            a2 = A(lambda e: e.activation(e2.ap, d1.ap, ACT.Exp, scale=-1 / 16), v, *e2.free)
            a3 = A(lambda e: e.activation(e3.ap, e3.ap, ACT.Exp, scale=1 / 16), v2)
            a4 = A(lambda e: e.activation(EBD[:, h, 0, :], b3[:, :, 31], ACT.Exp, scale=1 / 16), b_tok[h])
            a5 = A(lambda e: e.activation(EBD[:, h, 1, :], b3[:, :, 63], ACT.Exp, scale=1 / 16), b_tok[h])
            V(lambda e: e.tensor_copy(EBD[:, h, 2, 0:8:2], EBD[:, h, 0, 0:8:2]), a4)
            V(lambda e: e.tensor_tensor(EBD[:, h, 2, 1:8:2], EBD[:, h, 0, 1:8:2], EBD[:, h, 1, 0:8:2], ALU.mult), a5)
            v3 = V(lambda e: e.tensor_tensor(EBD[:, h, 3, 0:4], EBD[:, h, 1, 0:8:2], EBD[:, h, 1, 1:8:2], ALU.mult), a5)
            d1.free = [a2]
            E[h] = (e1, e2, e3, a1, a2, a3, v3, a5)
        return go

    q_tok = [None] * 4
    k_tok = [None] * 4

    def ev_q(h):
        def ev(ps, tok):
            e1, a1, a4 = E[h][0], E[h][3], E[h][6]
            t = tmp()
            v = V(lambda e: e.scalar_tensor_tensor(out=t.ap, in0=ps, scalar=P ** -0.5, in1=R[:, :],
                                                   op0=ALU.mult, op1=ALU.mult), tok, R_tok[0], *t.free)
            w = V(lambda e: e.tensor_tensor(QR[:, h, :], t.ap, e1.ap, ALU.mult), v, a1)
            e1.free = t.free = [w]
            V(lambda e: e.tensor_tensor(chunks(QO[:, h % 2, :]), chunks(QR[:, h, :])[:, 1:8:2, :],
                                        EBD[:, h, 0, 1:8:2].unsqueeze(2).broadcast_to([P, 4, C64]),
                                        ALU.mult), w, a4, s_tok.get(h - 2))
            q_tok[h] = V(lambda e: e.tensor_tensor(chunks(QI[:, h, :]), chunks(QR[:, h, :]),
                                                   EBD[:, h, 2, :].unsqueeze(2).broadcast_to([P, 8, C64]),
                                                   ALU.mult), w)
            return [v]
        return ev

    def ev_k(h):
        def ev(ps, tok):
            _, e2, e3, _, a2, a3, a4, a5 = E[h]
            t = tmp()
            v = V(lambda e: e.tensor_tensor(t.ap, ps, R[:, :], ALU.mult), tok, R_tok[0], *t.free)
            w = V(lambda e: e.tensor_tensor(KR[:, h, :], t.ap, e2.ap, ALU.mult), v, a2)
            k2 = V(lambda e: e.tensor_tensor(chunks(KE[:, h % 2, :]), chunks(t.ap)[:, 0:8:2, :],
                                             chunks(e3.ap)[:, 0:8:2, :], ALU.mult), v, a3, s_tok.get(h - 2))
            V(lambda e: e.tensor_tensor(chunks(KS[:, h, :])[:, 1:8:2, :], chunks(t.ap)[:, 1:8:2, :],
                                        chunks(e3.ap)[:, 1:8:2, :], ALU.mult), a5)
            k_tok[h] = V(lambda e: e.tensor_tensor(chunks(KS[:, h, :])[:, 0:8:2, :], chunks(KE[:, h % 2, :]),
                                                   EBD[:, h, 1, 1:8:2].unsqueeze(2).broadcast_to([P, 4, C64]),
                                                   ALU.mult), k2)
            e2.free, e3.free = [w], [k_tok[h]]
            t.free = [k_tok[h]]
            return [v]
        return ev

    gk = {"kstfree": [], "stfree": [], "statefree": []}
    s_tok = {}
    o_tok = [None] * KT
    os_tok = [None]

    def osl(i):
        return 4 * (i % 2) + i // 2

    def gla(h):
        L = {}

        def scores():
            b = sbank()
            for t in range(3):
                p = PE(lambda e, t=t: e.transpose(BK[b][:, t * P:t * P + P], KS[:, h, t * P:t * P + P], ident[:, :]),
                       k_tok[h], c_tok, *bfree[b], sig=(t == 2))
            L["kst"] = A(lambda e: e.activation(KST[:, 0:3 * P], BK[b][:, 0:3 * P], ACT.Copy), p, *gk["kstfree"])
            bfree[b] = [L["kst"]]
            b2 = sbank()
            for t in range(4):
                tc = slice(t * P, t * P + P)
                PE(lambda e, tc=tc: e.matmul(BK[b2][:, tc], KR[:, h, tc], QR[:, h, tc], start=True, stop=True),
                   k_tok[h], q_tok[h], *bfree[b2])
            for t in range(4):
                p = PE(lambda e, t=t: e.matmul(BK[b2][0:64, t * P + 64:t * P + P], KE[:, h % 2, 64 * t:64 * t + 64],
                                               QO[:, h % 2, 64 * t:64 * t + 64], start=True, stop=True), sig=(t == 3))
            s_tok[h] = p
            L["st"] = V(lambda e: e.copy_predicated(ST[:, :], CAU[:, :].bitcast(I32), BK[b2][:, :]),
                        p, st_tok, mix_c, *gk["stfree"])
            bfree[b2] = [L["st"]]

        def kv():
            bs = [sbank(), sbank()]
            for t in range(3):
                cc = slice(256 * (t % 2), 256 * (t % 2) + 256)
                p = PE(lambda e, t=t, cc=cc: e.matmul(
                    BK[bs[t // 2]][:, cc], KST[:, t * P:t * P + P], VT[:, t, 256 * h:256 * h + 256],
                    start=True, stop=True), L["kst"], vt_tok[h // 2, t], *bfree[bs[t // 2]], sig=(t > 0))
                if t == 1:
                    L["v"] = V(lambda e: e.tensor_copy(STATE[:, 1, :], BK[bs[0]][:, 0:256]), p, *gk["statefree"])
                if t > 0:
                    L["v"] = V(lambda e, t=t, cc=cc: e.scalar_tensor_tensor(
                        out=STATE[:, t + 1, :], in0=STATE[:, t, :], scalar=EBD[:, h, 3, t:t + 1],
                        in1=BK[bs[t // 2]][:, cc], op0=ALU.mult, op1=ALU.add), p, L["v"])
            bfree[bs[0]] = bfree[bs[1]] = [L["v"]]
            gk["kstfree"] = [p]

        def outs():
            sq = []
            for d in range(2):
                b = sbank()
                vcs = slice(256 * h + 128 * d, 256 * h + 128 * d + 128)
                for t in range(4):
                    tc = slice(t * P, t * P + P)
                    p = PE(lambda e, t=t, tc=tc, b=b, vcs=vcs: e.matmul(
                        BK[b][:, tc], VT[:, t, vcs], ST[:, tc], start=True, stop=(t == 0)),
                        L["st"], L["v"], vt_tok[h // 2, t], *bfree[b])
                    if t > 0:
                        p = PE(lambda e, t=t, tc=tc, b=b, d=d: e.matmul(
                            BK[b][:, tc], STATE[:, t, 128 * d:128 * d + 128], QI[:, h, tc], start=False, stop=True),
                            sig=(t == 3))
                i = 2 * h + d
                o_tok[i] = V(lambda e, i=i, b=b: e.tensor_copy(O[:, osl(i), :], BK[b][:, :]), p)
                bfree[b] = [o_tok[i]]
                s = tmp()
                a = A(lambda e, i=i, s=s: e.activation(s.ap, O[:, osl(i), :], ACT.Square), o_tok[i], *s.free)
                sq.append((s, a))
            (s0, a0), (s1, a1) = sq
            v = V(lambda e: e.tensor_tensor(s0.ap, s0.ap, s1.ap, ALU.add), a0, a1)
            s1.free = [v]
            L["sq"] = (s0, v)
            gk["stfree"] = [p]
            gk["statefree"] = [p]
            gk["last"] = p

        def sums():
            s, v = L["sq"]
            L["n"], p = rsq_rows(None, 7, [s.ap], 256, [v])
            s.free = [p]

        def scale():
            v, n = L["n"]()
            for i in (2 * h, 2 * h + 1):
                o_tok[i] = V(lambda e, i=i: e.tensor_tensor(O[:, osl(i), :], O[:, osl(i), :], n.ap, ALU.mult), v, o_tok[i])
            n.free = [o_tok[2 * h + 1]]

        return scores, kv, outs, sums, scale

    mset[0] = [0, 1, 2]
    lin(Hhi, Hlo, h_tok, ev_glr)
    ln_table()
    flush_side = lambda: [side.pop(0)() for _ in range(len(side))]
    for half in range(2):
        if half == 1:
            side.extend([gate(h) for h in range(4)])
        linv(Hhi, Hlo, h_tok, lambda t, half=half: VT[:, t, 512 * half:512 * half + 512], half)
    heads = [gla(h) for h in range(4)]
    mids_, ends_ = [[] for _ in range(12)], [[] for _ in range(12)]
    for h in range(4):
        mids_[2 * h].append(decays(h))
        for k, f in ((2, 0), (3, 1), (4, 2), (5, 4)):
            ends_[2 * h + k].append(heads[h][f])
        mids_[2 * h + 5].append(heads[h][3])
    for h in range(4):
        lin(Hhi, Hlo, h_tok, ev_q(h), 0, mids_[2 * h], ends_[2 * h])
        lin(Hhi, Hlo, h_tok, ev_k(h), 0, mids_[2 * h + 1], ends_[2 * h + 1])
    cv = {}
    pad = {}

    def ev_cc(ps, tok):
        t = tmp()
        v = V(lambda e: e.tensor_tensor(t.ap, ps, R[:, :], ALU.mult), tok, R_tok[0], *t.free)
        cv["cc"] = (t, v)
        return [v]

    def ev_cu(i):
        def ev(ps, tok):
            c, cw = cv["cc"]
            t, u, y = tmp(), tmp(), tmp()
            v = V(lambda e: e.tensor_tensor(t.ap, ps, R[:, :], ALU.mult), tok, R_tok[0], *t.free)
            z = V(lambda e: e.memset(u.t[:, 0:2], 0.0), *u.free)
            w = V(lambda e: e.tensor_tensor(u.t[:, 2:T + 2], t.ap, c.ap, ALU.mult), v, cw, *u.free)
            t.free = c.free = [w]
            a = A(lambda e: e.activation(y.ap, u.t[:, 0:T], ACT.Copy, scale=vc("cw0", i)), z, w, vec_tok, *y.free)
            w = V(lambda e: e.scalar_tensor_tensor(out=y.ap, in0=u.t[:, 1:T + 1], scalar=vc("cw1", i), in1=y.ap,
                                                   op0=ALU.mult, op1=ALU.add), a)
            w = V(lambda e: e.scalar_tensor_tensor(out=y.ap, in0=u.t[:, 2:T + 2], scalar=vc("cw2", i), in1=y.ap,
                                                   op0=ALU.mult, op1=ALU.add), w)
            u.free = [w]
            cv["y"] = (y, w)
            return [v]
        return ev

    def ev_cb(i):
        def ev(ps, tok):
            y, yw = cv["y"]
            t, r = tmp(), tmp()
            v = V(lambda e: e.tensor_tensor(t.ap, ps, R[:, :], ALU.mult), tok, R_tok[0], *t.free)
            w = V(lambda e: e.tensor_tensor(r.ap, t.ap, y.ap, ALU.mult), v, yw, *r.free)
            t.free = y.free = [w]
            a_tok[i], _ = hilo(Ahi[:, i, :], Alo[:, i, :], r.ap, w)
            r.free = [a_tok[i]]
            return [v]
        return ev

    for i in range(8):
        for j, ev in enumerate((ev_cc, ev_cu(i), ev_cb(i))):
            n = 8 + 3 * i + j
            lin(Hhi, Hlo, h_tok, ev, 0, mids_[n] if n < 12 else (), ends_[n] if n < 12 else ())

    def gated(func, dst=None):
        hold = {}

        def ev(ps, tok):
            t = tmp()
            v = V(lambda e: e.tensor_tensor(t.ap, ps, R[:, :], ALU.mult), tok, R_tok[0], *t.free)
            if dst is None:
                s = tmp()
                a = A(lambda e: e.activation(s.ap, t.ap, func), v, *s.free)
                hold["s"] = s
            else:
                a = A(lambda e: e.activation(dst, t.ap, func), v, gk["last"])
            t.free = [a]
            hold["a"] = a
            return [v]
        return ev, hold

    m_tok = [None] * KT
    for i in range(8):
        ev, hold = gated(ACT.Sigmoid)
        lin(Hhi, Hlo, h_tok, ev)

        def ev_oc(ps, tok, i=i, hold=hold):
            s = hold["s"]
            m_tok[i] = V(lambda e: e.tensor_tensor(MC[:, i, :], ps, s.ap, ALU.mult), tok, hold["a"], gk["last"])
            s.free = [m_tok[i]]
            return [m_tok[i]]
        lin(Ahi, Alo, a_tok, ev_oc)
    flush_side()
    for i in range(8):
        def ev_r(ps, tok, i=i):
            t, s, g = tmp(), tmp(), tmp()
            v = V(lambda e: e.tensor_tensor(t.ap, ps, R[:, :], ALU.mult), tok, R_tok[0], *t.free)
            a = A(lambda e: e.activation(s.ap, t.ap, ACT.Silu), v, *s.free)
            t.free = [a]
            w = V(lambda e: e.scalar_tensor_tensor(out=g.ap, in0=O[:, osl(i), :], scalar=vc("gla", i), in1=s.ap,
                                                   op0=ALU.mult, op1=ALU.mult), a, o_tok[i], vec_tok, *g.free)
            s.free = [w]
            a_tok[i], _ = hilo(Ahi[:, i, :], Alo[:, i, :], g.ap, w)
            g.free = [a_tok[i]]
            return [v]
        lin(Hhi, Hlo, h_tok, ev_r)
    sg = []
    for i in range(8):
        ev, hold = gated(ACT.Sigmoid, SG[:, i, :])
        sg.append(hold)
        lin(Hhi, Hlo, h_tok, ev)
    mg_tok = [None] * KT
    for i in range(8):
        def ev_og(ps, tok, i=i):
            t, m = tmp(), tmp()
            v = V(lambda e: e.tensor_tensor(t.ap, ps, SG[:, i, :], ALU.mult), tok, sg[i]["a"], *t.free)
            w = V(lambda e: e.tensor_tensor(m.ap, t.ap, MC[:, i, :], ALU.add), v, m_tok[i], *m.free)
            t.free = [w]
            mg_tok[i], _ = hilo(MGhi[:, i, :], MGlo[:, i, :], m.ap, w, a_tok[7])
            m.free = [mg_tok[i]]
            return [v]
        lin(Ahi, Alo, a_tok, ev_og)
    for n in range(8):
        def ev_o(ps, tok, n=n):
            x_tok[n] = v = V(lambda e: e.tensor_tensor(X[:, n, :], ps, X[:, n, :], ALU.add), tok, x_tok[n])
            to_h(n, "g2", v)
            square_into(SS, ss_tok, n, X[:, n, :], v)
            if n == KT - 1:
                norm_rows()
            return [v]
        lin(MGhi, MGlo, mg_tok, ev_o)

    g_tok = V(lambda e: e.tensor_tensor(gfm[:, :], vc("gf", 0, 8), vc("gm2", 0, 8), ALU.mult), vec_tok)
    ss2_tok = [None]

    def after_ffn2(n):
        to_h(n, None, x_tok[n], garr=gfm)
        square_into(SS, ss_tok, n, X[:, n, :], x_tok[n])
        square_into(SS2, ss2_tok, n, X[:, n, :], x_tok[n], scale=vc("gf", n))
        if n < KT - 1:
            return
        L = {}

        def one():
            token_sums(0, [SS], [ss_tok[0]])
            p = token_sums(4, [SS2], [ss2_tok[0]])
            r1, r2, q, m = rt2[:, 0:4], rt2[:, 4:8], rt2[:, 8:12], rt2[:, 12:16]
            v = rsq(r1, BK[7][:, 0:4], 4, 1.0 / D, p)
            L["r1"] = v
            w = V(lambda e: e.tensor_tensor(q, r1, r1, ALU.mult), v)
            w = V(lambda e: e.tensor_tensor(m, q, BK[7][:, 4:8], ALU.mult), w)
            bfree[7] = [w]
            w = rsq(r2, m, 4, 1.0 / D, w)
            L["v"] = V(lambda e: e.tensor_tensor(rt[:, 0:4], r1, r2, ALU.mult), w)
            rt_tok[0] = L["v"]

        def two():
            b, p = rows(rt, 1, L["v"], 7)
            R_tok[0] = V(lambda e: e.tensor_copy(R[:, :], BK[b][:, :]), p)
            bfree[b] = [R_tok[0]]
            b2, p2 = rows(rt2, 1, L["r1"], 7)
            L["w"] = V(lambda e: e.tensor_copy(SS2[:, :], BK[b2][:, :]), p2)
            bfree[b2] = [L["w"]]
            late[0] = False

        def x2(n):
            def go():
                x_tok[n] = V(lambda e: e.scalar_tensor_tensor(
                    out=X[:, n, :], in0=X[:, n, :], scalar=vc("gf", n), in1=SS2[:, :], op0=ALU.mult, op1=ALU.mult),
                    L["w"], x_tok[n], h_tok[n], ss_tok[0], ss2_tok[0])
            return go
        late[0] = True
        side[0:0] = [one, two] + [(lambda n=n: (x2(2 * n)(), x2(2 * n + 1)())) for n in range(4)]

    mset[0] = list(range(7))
    ffn(after_ffn2)

    mset[0] = [0, 1]
    m_end = ptok[cur[0] - 1]
    gd_tok = DMA("A", "dg", GD[:, :], dr["gd"], m_end)
    rope_tok = DMA("A", "dr", ROPE[:, :, :], dr["rope"], m_end)
    nam_tok = DMA("A", "dn", NAM[:, :, :], dr["nam"], m_end)
    nq_tok = [None] * 4
    nk_tok = [None] * 4
    BS = [0, 8, 24, 32]
    vb_tok = {}

    def bands():
        for cb in range(4):
            for i in range(8):
                vb_tok[cb] = DMA("S", f"vb{cb}", VB[32 * (i % 4):32 * (i % 4) + 32, 2 * cb + i // 4, :],
                                 NV[64 * (i % 2) + BS[cb]:64 * (i % 2) + BS[cb] + 32, i // 2, :],
                                 vt_tok["n", i // 2])

    rbt = {}
    rb_free = [[m_end], [m_end]]

    def raw_bias(hp):
        for j in range(2):
            rbt[hp] = DMA("G", f"rb{hp % 2}", RB[hp % 2][:, j, :], dr["rpb"][2 * hp + j], *rb_free[hp % 2])

    ge = [GE0[:, :], GE1[:, :], GE2[:, :], GE0[:, :]]
    ge_tok = [None] * 4
    ge_free = [[m_end], [m_end], [], []]
    lg = small[:, 40:48]
    l1, l2, l3 = small[:, 48:56], small[:, 56:64], small[:, 64:72]
    lgt = {}

    def log_gamma():
        ln_table()
        a = A(lambda e: e.activation(l1, vc("dec", 0, 8), ACT.Exp), vec_tok)
        v = V(lambda e: e.tensor_scalar(l2, l1, -1.0, 1.0, ALU.mult, ALU.add), a)
        a = A(lambda e: e.activation(lg, l2, ACT.Ln), v)
        v = V(lambda e: e.tensor_scalar(l3, l2, -1.0, 1.0, ALU.mult, ALU.add), v)
        v = V(lambda e: e.tensor_scalar(l3, l3, 1e-30, None, ALU.max), v)
        v = V(lambda e: e.reciprocal(l3, l3), v)
        v = V(lambda e: e.tensor_tensor(l3, l3, l1, ALU.mult), v)
        lgt["t"] = V(lambda e: e.tensor_tensor(lg, lg, l3, ALU.mult), v, a)

    def strip(h):
        def go():
            v = V(lambda e: e.tensor_scalar(ge[h], GD[:, :], 0.0, lg[:, h:h + 1], ALU.max, ALU.mult),
                  gd_tok, lgt["t"], *ge_free[h])
            t0, t1 = tmp(), tmp()
            for t, c0, c1 in ((t0, 0, 448), (t1, 448, 896)):
                w = V(lambda e, t=t, c0=c0, c1=c1: e.tensor_scalar(
                    t.ap[:, 0:c1 - c0], GD[:, c0:c1], 0.0, lg[:, 4 + h:5 + h], ALU.min, ALU.mult),
                    gd_tok, *t.free)
                v = V(lambda e, t=t, c0=c0, c1=c1: e.tensor_tensor(
                    ge[h][:, c0:c1], ge[h][:, c0:c1], t.ap[:, 0:c1 - c0], ALU.subtract), v, w)
                t.free = [v]
            ge_tok[h] = A(lambda e: e.activation(ge[h], ge[h], ACT.Exp), v)
        return go

    dst_free[0] = [m_end]
    raw_bias(0)
    raw_bias(1)
    side.extend([log_gamma, strip(0), strip(1)])
    linv(Hhi, Hlo, h_tok, lambda t: NV[:, t, :], "n")
    linv(Hhi, Hlo, h_tok, lambda t: RV[:, t, :], "r", lambda t, h: small[:, 24 + 4 * t + h:25 + 4 * t + h])
    v = V(lambda e: e.tensor_scalar(small[:, 24:40], small[:, 24:40], 1.0 / P, None, ALU.mult), vt_tok["r", 3])
    for t in range(4):
        vt_tok["r", t] = G(lambda e, t=t: e.tensor_tensor(
            RV[:, t, :].rearrange("p (h d) -> p h d", h=4), RV[:, t, :].rearrange("p (h d) -> p h d", h=4),
            small[:, 24 + 4 * t:28 + 4 * t].unsqueeze(2).broadcast_to([P, 4, P]), ALU.subtract), v)

    PAT = [0, 1, 1, 2]
    OFF = [0, -8, -8, -16]
    na = {}
    ob = {}
    na_tok = [None] * 4

    def na_g(p):
        hp = p // 4
        ss = []
        for q in range(2):
            cb = (p + q) % 4
            s = tmp()
            g = G(lambda e, s=s, cb=cb: e.tensor_tensor(
                s.ap.rearrange("p (h i j) -> p h i j", h=2, j=32),
                RB[hp % 2][:, :, 16 + OFF[cb]:16 + OFF[cb] + 256].rearrange("p h (i j) -> p h i j", j=32),
                NAM[:, PAT[cb], :].unsqueeze(1).unsqueeze(1).broadcast_to([P, 2, 8, 32]), ALU.add),
                rbt[hp], nam_tok, *s.free)
            ss.append((s, g))
        if p % 4 == 2:
            rb_free[hp % 2] = [g]
            if hp + 2 < 4:
                raw_bias(hp + 2)
        na["g"] = ss

    def na_s(p):
        hp = p // 4
        k3 = NK[:, hp, :].rearrange("p (r c) -> p r c", c=64)
        ss = na["g"]
        for q in range(2):
            cb = (p + q) % 4
            for j in range(2):
                hs = slice(64 * j, 64 * j + 64)
                pt = PE(lambda e, j=j, hs=hs, q=q, cb=cb: e.matmul(
                    BK[3 + j][:, 256 * q:256 * q + 256], NQ[hs, hp, cb * P:cb * P + P], k3[hs, :, BS[cb]:BS[cb] + 32],
                    start=True, stop=True), nq_tok[hp], nk_tok[hp], *bfree[3 + j], sig=(q == 1 and j == 1))
        for q, (s, g) in enumerate(ss):
            ss[q] = (s, V(lambda e, s=s, q=q: e.tensor_tensor(
                s.ap.rearrange("p (h k) -> p h k", h=2), PS[:, 3:5, 256 * q:256 * q + 256],
                s.ap.rearrange("p (h k) -> p h k", h=2), ALU.add), pt, g))
        bfree[3] = bfree[4] = [ss[1][1]]
        for q, (s, v) in enumerate(ss):
            s3 = s.ap.rearrange("p (h k) -> p h k", h=2)
            mx = 4 * q
            nm, rs, ri = (small[:, 8 * i + mx:8 * i + mx + 2] for i in range(3))
            v = V(lambda e, nm=nm, s3=s3: e.tensor_reduce(nm, s3, AX_X, ALU.max, negate=True), v,
                  *na.get(("free", q), []))
            for j in range(2):
                a = A(lambda e, j=j, s3=s3, nm=nm, rs=rs: e.activation(
                    s3[:, j, :], s3[:, j, :], ACT.Exp, bias=nm[:, j:j + 1], accum_out=rs[:, j:j + 1]), v)
            ss[q] = (s, s3, rs, ri, a)
        na["x"] = ss

    def na_x(p):
        for q, (s, s3, rs, ri, a) in enumerate(na["x"]):
            v = V(lambda e, rs=rs, ri=ri: e.reciprocal(ri, rs), a)
            for j in range(2):
                w = V(lambda e, j=j, s3=s3, ri=ri: e.tensor_scalar(s3[:, j, :], s3[:, j, :], ri[:, j:j + 1], None,
                                                                   ALU.mult), v)
            na["free", q] = [w]
            na[p + q] = (s, w)

    def na_t(p):
        s, w = na[p]
        b = 5 if p < 10 or p % 2 == 0 else 2
        for i in range(4):
            pt = PE(lambda e, i=i: e.transpose(BK[b][:, i * P:i * P + P], s.ap[:, i * P:i * P + P], ident[:, :]),
                    w, *bfree[b], sig=(i == 3))
        s.free = [pt]
        t = tmp()
        a = A(lambda e: e.activation(t.ap, BK[b][:, :], ACT.Copy), pt, *t.free)
        bfree[b] = [a]
        na[p] = (t, a)

    def na_o(p):
        hp, cb = p // 4, p % 4
        t, a = na.pop(p)
        b = 6
        for j in range(2):
            for i in range(2):
                pt = PE(lambda e, j=j, i=i: e.matmul(
                    BK[b][64 * j:64 * j + 64, cb * P:cb * P + P],
                    VB[:, 2 * cb + i, (2 * hp + j) * 64:(2 * hp + j) * 64 + 64],
                    t.ap[:, (2 * j + i) * P:(2 * j + i) * P + P], start=(i == 0), stop=(i == 1)),
                    a, vb_tok[cb], *(bfree[b] if cb == 0 else []), sig=(i == 1 and j == 1))
        t.free = [pt]
        if cb == 3:
            src = BK[b][:, :].rearrange("p (c r q) -> p r c q", c=4, q=16)
            hi = Ahi[:, hp, :].rearrange("p (r c q) -> p r c q", r=8, q=16)
            lo = Alo[:, hp, :].rearrange("p (r c q) -> p r c q", r=8, q=16)
            o = tmp()
            o4 = o.ap.rearrange("p (r c q) -> p r c q", r=8, q=16)
            v = V(lambda e: e.tensor_copy(o4, src), pt, *o.free)
            bfree[b] = [v]
            na_tok[hp], _ = hilo(Ahi[:, hp, :], Alo[:, hp, :], o.ap, v)
            o.free = [na_tok[hp]]

    rot_tok = {}

    def ev_rot(dst, key, sc):
        def ev(ps, tok):
            t, s = tmp(), tmp()
            v = V(lambda e: e.scalar_tensor_tensor(out=t.ap, in0=ps, scalar=sc, in1=R[:, :], op0=ALU.mult,
                                                   op1=ALU.mult), tok, R_tok[0], *t.free)
            L = {}

            def swap():
                for q in range(4):
                    o = q ^ 1
                    L["a"] = A(lambda e, q=q, o=o: e.activation(s.ap[32 * q:32 * q + 32, :],
                                                                t.ap[32 * o:32 * o + 32, :], ACT.Copy), v, *s.free)

            def turn():
                w = V(lambda e: e.tensor_tensor(t.ap, t.ap, ROPE[:, 0, :], ALU.mult), L["a"], rope_tok)
                w2 = V(lambda e: e.tensor_tensor(s.ap, s.ap, ROPE[:, 1, :], ALU.mult))
                rot_tok[key] = V(lambda e: e.tensor_tensor(dst, t.ap, s.ap, ALU.add), w, w2, m_end)
                t.free = s.free = [rot_tok[key]]
                if key == ("k", 1):
                    ge_free[2] = [rot_tok["q", 1], rot_tok["k", 1]]
            rot.extend([swap, turn])
            return [v]
        return ev

    rot = []

    y_tok = [None] * 4
    rs_ = {}
    rpos = [0]

    def rtmp():
        rpos[0] += 1
        return rring[rpos[0] % 3]

    rring = [Slot(t) for t in (SS, SS2, RS)]
    for s_ in rring:
        s_.ap = s_.t[:, :]
        s_.free = [m_end, R_tok[0], *x_tok]

    def ret_s(i):
        h, jt = i // 4, i % 4
        b = 7
        hs = slice(64 * (h % 2), 64 * (h % 2) + 64)
        pt = PE(lambda e: e.matmul(BK[b][:, :], RK[hs, h // 2, jt * P:jt * P + P], RQ[hs, h // 2, :],
                                   start=True, stop=True),
                rot_tok["q", h // 2], rot_tok["k", h // 2], *bfree[b], sig=True)
        t = rtmp()
        v = V(lambda e: e.tensor_tensor(t.ap, BK[b][:, :], ge[h][:, 384 - 128 * jt:896 - 128 * jt], ALU.mult),
              pt, ge_tok[h], *t.free)
        bfree[b] = [v]
        rs_[i] = (t, v)
        if i == 3:
            ge_free[3] = [v]

    def ret_o(i):
        h, jt = i // 4, i % 4
        t, v = rs_.pop(i)
        b = 2
        p = PE(lambda e: e.matmul(BK[b][:, :], RV[:, jt, h * P:h * P + P], t.ap, start=(jt == 0), stop=(jt == 3)),
               v, vt_tok["r", jt], *(bfree[b] if jt == 0 else []), sig=True)
        t.free = [p]
        if jt == 3:
            y_tok[h] = A(lambda e: e.activation(YH[:, h, :], BK[b][:, :], ACT.Copy), p, *vb_tok.values())
            s = rtmp()
            a = A(lambda e: e.activation(s.ap, BK[b][:, :], ACT.Square), *s.free)
            bfree[b] = [a]
            sq_[h] = (s, a)

    sq_ = {}

    def ret_n(h):
        s, a = sq_[h]
        sq_[h], p = rsq_rows(None, 7, [s.ap], P, [a])
        s.free = [p]

    def ret_y(h):
        v, n = sq_[h]()
        y_tok[h] = V(lambda e: e.tensor_tensor(YH[:, h, :], YH[:, h, :], n.ap, ALU.mult), v, y_tok[h])
        n.free = [y_tok[h]]

    mix_tok = [None] * KT

    def ev_nq(i):
        def ev(ps, tok):
            nq_tok[i] = V(lambda e: e.tensor_tensor(
                NQ[:, i, :].rearrange("p (c r q) -> p r c q", c=4, q=16),
                ps.rearrange("p (r c q) -> p r c q", r=8, q=16),
                R[:, :].rearrange("p (r c q) -> p r c q", r=8, q=16), ALU.mult), tok, R_tok[0], m_end)
            return [nq_tok[i]]
        return ev

    def ev_nk(i):
        def ev(ps, tok):
            nk_tok[i] = V(lambda e: e.scalar_tensor_tensor(out=NK[:, i, :], in0=ps, scalar=0.125, in1=R[:, :],
                                                           op0=ALU.mult, op1=ALU.mult), tok, R_tok[0], m_end)
            return [nk_tok[i]]
        return ev

    def ev_rg(i):
        def ev(ps, tok):
            t = rtmp()
            v = V(lambda e: e.tensor_tensor(t.ap, ps, R[:, :], ALU.mult), tok, R_tok[0], *t.free)
            rg_[i] = (t, v)
            return [v]
        return ev

    rg_ = {}

    def rg_silu(i):
        t, v = rg_[i]
        rg_[i] = (t, A(lambda e: e.activation(t.ap, t.ap, ACT.Silu), v))

    def rg_out(i):
        g, a = rg_[i]
        s = rtmp()
        w = V(lambda e: e.scalar_tensor_tensor(out=s.ap, in0=YH[:, i, :], scalar=vc("rg", i), in1=g.ap,
                                               op0=ALU.mult, op1=ALU.mult), a, y_tok[i], *s.free)
        g.free = [w]
        mix_tok[4 + i], _ = hilo(Ahi[:, 4 + i, :], Alo[:, 4 + i, :], s.ap, w, *ge_tok)
        s.free = [mix_tok[4 + i]]

    evs = [ev_rot(RQ[:, 0, :], ("q", 0), 1.0), ev_rot(RK[:, 0, :], ("k", 0), 0.125),
           ev_rot(RQ[:, 1, :], ("q", 1), 1.0), ev_rot(RK[:, 1, :], ("k", 1), 0.125)]
    for i in range(4):
        evs += [ev_nq(i), ev_nk(i)]
    evs += [ev_rg(i) for i in range(4)]
    for n, ev in enumerate(evs):
        pre, mid, end = [], [], []
        i, p = 2 * (n - 3), 2 * (n - 7)
        if 0 < n <= 4:
            mid.append(lambda: rot.pop(0)())
            end.append(lambda: rot.pop(0)())
        if 0 < i <= 16:
            mid.append(lambda i=i: ret_o(i - 1))
        if 0 <= i < 16:
            mid.append(lambda i=i: ret_s(i))
        if 4 < i <= 18 and i % 4 == 2:
            mid.append(lambda h=(i - 2) // 4 - 1: ret_y(h))
        if 0 <= p < 16:
            pre.append(lambda p=p: na_x(p))
            end.append(lambda p=p: na_t(p))
        if 0 <= p + 2 < 16:
            mid.append(lambda p=p: na_g(p + 2))
        if n > 12:
            mid.append(lambda h=n - 13: rg_silu(h))
        if 0 <= i < 16:
            end.append(lambda i=i: ret_o(i))
        if 0 <= p < 16:
            end.append(lambda p=p: na_t(p + 1))
        if 0 <= i < 16:
            end.append(lambda i=i: ret_s(i + 1))
        if 0 <= p < 16:
            end += [lambda p=p: na_o(p), lambda p=p: na_o(p + 1)]
        if 0 <= p + 2 < 16:
            end.append(lambda p=p: na_s(p + 2))
        if 0 < i <= 16 and i % 4 == 0:
            end.append(lambda h=i // 4 - 1: ret_n(h))
        if n > 12:
            end.append(lambda h=n - 13: rg_out(h))
        if n == 0:
            end.append(bands)
        if n in (4, 5):
            end.append(strip(n - 2))
        lin(Hhi, Hlo, h_tok, ev, 1, mid, end, pre)
    flush()
    rg_silu(3)
    rg_out(3)
    for h in range(4):
        mix_tok[h] = na_tok[h]
    mset[0] = list(range(7))
    for n in range(8):
        def ev_o2(ps, tok, n=n):
            x_tok[n] = v = V(lambda e: e.tensor_tensor(X[:, n, :], ps, X[:, n, :], ALU.add), tok, x_tok[n])
            to_h(n, "gl2", v)
            square_into(SS, ss_tok, n, X[:, n, :], v)
            if n == KT - 1:
                norm_rows()
            return [v]
        lin(Ahi, Alo, mix_tok, ev_o2)

    fin = {}
    for g in range(4):
        for j in range(8):
            def ev_up(ps, tok, j=j):
                t, m = tmp(), tmp()
                v = V(lambda e: e.tensor_tensor(t.ap, ps, R[:, :], ALU.mult), tok, R_tok[0], *t.free)
                w = V(lambda e: e.scalar_tensor_tensor(out=m.ap, in0=t.ap, scalar=0.0, in1=t.ap, op0=ALU.max,
                                                       op1=ALU.mult), v, *m.free)
                t.free = [w]
                a_tok[j], _ = hilo(Ahi[:, j, :], Alo[:, j, :], m.ap, w)
                m.free = [a_tok[j]]
                return [v]
            lin(Hhi, Hlo, h_tok, ev_up)
        for n in range(8):
            def ev_dn(ps, tok, n=n, last=(g == 3)):
                x_tok[n] = v = V(lambda e: e.tensor_tensor(X[:, n, :], ps, X[:, n, :], ALU.add), tok, x_tok[n])
                if last and n < KT - 1:
                    square_into(SS, ss_tok, n, X[:, n, :], v)
                elif last:
                    fin["s"] = tmp()
                    fin["a"] = A(lambda e: e.activation(fin["s"].ap, X[:, n, :], ACT.Square), v, *fin["s"].free)
                if last:
                    x_tok[n] = A(lambda e: e.activation(X[:, n, :], X[:, n, :], ACT.Copy, scale=vc("gf2", n)), v)
                return [v]
            lin(Ahi, Alo, a_tok, ev_dn)
    flush()
    p = token_sums(0, [SS, fin["s"].ap], [ss_tok[0], fin["a"]])
    v = rsq(rt[:, 0:4], BK[7][:, 0:4], 4, 1.0 / D, p)
    _, p = rows(rt, 1, v, 6)
    for n in range(8):
        v = V(lambda e, n=n: e.tensor_tensor(X[:, n, :], X[:, n, :], BK[6][:, :], ALU.mult), p, x_tok[n])
        o = DMA("S", "do", out[n], X[:, n, :], v)
    pr.put("S", None, [o])
    assert cur[0] == NU, (cur[0], NU)

    with ExitStack() as ctx:
        sems = {s: ctx.enter_context(nc.semaphore(f"s_{s}")) for s in pr.n}
        block = ctx.enter_context(nc.Block())

        @block.sync
        def _(e):
            pr.run("S", e, sems)

        @block.scalar
        def _(e):
            pr.run("A", e, sems)

        @block.vector
        def _(e):
            pr.run("V", e, sems)

        @block.gpsimd
        def _(e):
            pr.run("G", e, sems)

        @block.tensor
        def _(e):
            pr.run("P", e, sems)


def _tiles(w):
    k, n = w.shape
    return np.ascontiguousarray(w.reshape(k // P, P, n // P, P).transpose(2, 1, 0, 3))


def _wide(w):
    k, n = w.shape
    return np.ascontiguousarray(w.reshape(k // P, P, n // 512, 512).transpose(2, 1, 0, 3))


def _col(v):
    return v.reshape(-1, P).T


def _layout(a):
    f = np.float32
    m = {}
    m["xt"] = np.ascontiguousarray(a["x"][0].T).reshape(KT, P, T)
    m["w_gu1"] = _tiles(a["ffn1_w_gu"][0])
    m["w_d1"] = _tiles(a["ffn1_w_down"][0])
    m["w_gu2"] = _tiles(a["ffn2_w_gu"][0])
    m["w_d2"] = _tiles(a["ffn2_w_down"][0])
    w = a["w_in"][0]
    sizes = [("cb", D), ("cc", D), ("cu", D), ("q", 512), ("k", 512), ("v", D), ("glr", 16), ("r", D), ("ga", D),
             ("gb", D)]
    o = 0
    for name, n in sizes:
        part = w[:, o:o + n]
        o += n
        if name == "glr":
            part = np.concatenate([part, np.zeros((D, P - n), f)], axis=1)
        m["w_" + name] = _wide(part) if name == "v" else _tiles(part)
    m["w_oc"] = _tiles(a["w_out_conv"][0])
    m["w_og"] = _tiles(a["w_out_gla"][0])
    m["w_o"] = _tiles(a["w_o"][0])
    w = a["w_in_2"][0]
    o = 0
    for name, n in [("nq", 512), ("nk", 512), ("nv", 512), ("rq", 256), ("rk", 256), ("rv", 512), ("rg", 512)]:
        part = w[:, o:o + n]
        o += n
        m["w_" + name] = _wide(part) if name in ("nv", "rv") else _tiles(part)
    m["w_out2"] = _tiles(a["w_out_2"][0])
    m["w_up"] = _tiles(a["w_up_2"][0])
    m["w_dn"] = _tiles(a["w_down_2"][0])
    m["gup"] = np.ascontiguousarray(a["gate_w_up"][0])
    dec = np.concatenate([a["ret_decay_fwd_2"][0], a["ret_decay_bwd_2"][0]])
    parts = dict(g1=_col(a["norm_ffn1_g"][0]), gm=_col(a["norm_mix_g"][0]), g2=_col(a["norm_ffn2_g"][0]),
                 gf=_col(a["final_norm_g"]), gm2=_col(a["norm_mix_2"][0]), gl2=_col(a["norm_mlp_2"][0]),
                 gf2=_col(a["norm_final_2"]), gla=_col(a["gla_norm_g"][0]), gb=_col(a["gate_b"][0]),
                 cw0=_col(a["conv_w"][0, 0]), cw1=_col(a["conv_w"][0, 1]), cw2=_col(a["conv_w"][0, 2]),
                 rg=_col(a["ret_norm_gain_2"][0]), dec=np.broadcast_to(dec, (P, 8)))
    m["vec"] = np.ascontiguousarray(np.concatenate([parts[n] for n in VEC], axis=1))
    rpb = a["na_rpb_2"][0]
    flat = np.concatenate([np.zeros((8, 32), f), np.concatenate([rpb, np.zeros((8, 15, 1), f)], axis=2).reshape(8, 480),
                           np.zeros((8, 32), f)], axis=1)
    r, q, n = np.meshgrid(np.arange(8), np.arange(16), np.arange(BW), indexing="ij")
    at = 32 + (7 - r) * 32 + 15 - q - 16 + n
    m["rpb"] = np.ascontiguousarray(flat[:, at.reshape(P, BW)])
    return m


def _constants():
    f = np.float32
    m = {}
    m["ident"] = np.eye(P, dtype=f)
    t = np.arange(T)
    m["scm"] = np.ascontiguousarray(np.broadcast_to((t % 64 != 0).astype(f), (P, T)))
    j, i = np.arange(P)[:, None], (t % P)[None, :]
    m["cau"] = (i >= j).astype(f)
    qj, kj = np.arange(16)[:, None], np.arange(32)[None, :]
    nam = np.zeros((3, 16, 32), f)
    for p, cb in enumerate((0, 1, 3)):
        col = 16 * cb + qj
        key = [0, 8, 24, 32][cb] + kj
        lo = np.clip(col - 8, 0, 48)
        nam[p] = np.where((key >= lo) & (key < lo + 16), 0.0, -1e30)
    m["nam"] = np.ascontiguousarray(np.tile(nam.transpose(1, 0, 2), (8, 1, 1)))
    inv = (f(1.0) / (f(10000.0) ** (np.arange(0, 64, 2, dtype=f) / f(64)))).astype(f)
    ang = (t.astype(f)[None, :] * inv[:, None]).astype(f).astype(np.float64)
    cos, sin = np.cos(ang).astype(f), np.sin(ang).astype(f)
    m["rope"] = np.ascontiguousarray(np.stack([np.concatenate([cos, cos, cos, cos]),
                                               np.concatenate([-sin, sin, -sin, sin])], axis=1))
    m["gd"] = (np.arange(GW)[None, :] - np.arange(P)[:, None] - 384).astype(f)
    return m


def kernel(**inputs):
    import concourse.bacc as _bacc
    from concourse.bass_utils import run_bass_kernel_spmd as _run

    arrays = {**_layout({k: np.asarray(v) for k, v in inputs.items()}), **_constants()}
    nc = _bacc.Bacc("TRN2", target_bir_lowering=False, num_devices=1)
    dr = {n: nc.dram_tensor(f"in_{n}", v.shape, F32, kind="ExternalInput").ap() for n, v in arrays.items()}
    out = nc.dram_tensor("out_0", (KT, P, T), F32, kind="ExternalOutput").ap()
    build(nc, dr, out)
    r = _run(nc, [{f"in_{n}": v for n, v in arrays.items()}], core_ids=[0])
    got = r.results[0]["out_0"]
    return np.ascontiguousarray(got.reshape(D, T).T).reshape(1, T, D)
```

```python
from contextlib import ExitStack

import numpy as np

import concourse.bass as bass
from concourse import mybir

ALU = mybir.AluOpType
ACT = mybir.ActivationFunctionType
AX_X = mybir.AxisListType.X
F32 = mybir.dt.float32
F32R = mybir.dt.float32r
I32 = mybir.dt.int32

P = 128
T = 512
D = 1024
KT = D // P
FF = 2816
FT = FF // P
FF2 = 4096
EPS = 1e-6
NRAW = 3
NW = 3
NTMP = 9

VEC = ["g1", "gm", "g2", "gf", "gm2", "gl2", "gf2", "gla", "gb", "cw0", "cw1", "cw2", "rg", "dec"]
VECN = dict(g1=8, gm=8, g2=8, gf=8, gm2=8, gl2=8, gf2=8, gla=8, gb=4, cw0=8, cw1=8, cw2=8, rg=4, dec=12)
VECO = {}
_o = 0
for _n in VEC:
    VECO[_n] = _o
    _o += VECN[_n]
NVEC = _o
GW = 384
BW = 272


class Prog:

    def __init__(self):
        self.q = {e: [] for e in "PAVGS"}
        self.n = {}
        self.seen = {e: {} for e in "PAVGS"}

    def put(self, eng, fn, waits, sem=None, by=1):
        need = {}
        for w in waits:
            if w is not None:
                need[w[0]] = max(need.get(w[0], 0), w[1])
        todo = []
        for s, v in need.items():
            if self.seen[eng].get(s, 0) < v:
                self.seen[eng][s] = v
                todo.append((s, v))
        tok = None
        if sem is not None:
            self.n[sem] = self.n.get(sem, 0) + by
            tok = (sem, self.n[sem])
        self.q[eng].append((todo, fn, sem, by))
        return tok

    def run(self, eng, e, sems):
        for todo, fn, sem, by in self.q[eng]:
            for s, v in todo:
                e.wait_ge(sems[s], v)
            if fn is None:
                continue
            ins = fn(e)
            if sem is not None:
                ins.then_inc(sems[sem], by)


def build(nc, dr, out):
    pr = Prog()

    def V(fn, *waits):
        return pr.put("V", fn, waits, "V")

    def A(fn, *waits):
        return pr.put("A", fn, waits, "A")

    def G(fn, *waits):
        return pr.put("G", fn, waits, "G")

    def PE(fn, *waits, sig=False):
        return pr.put("P", fn, waits, "P" if sig else None)

    def DMA(q, sem, dst, src, *waits):
        return pr.put(q, lambda e: e.dma_start(dst, src), waits, sem, 16)

    at = [int(nc.sbuf_base)]

    def sb(name, shape, dt=F32, off=None):
        nb = 4 * int(np.prod(shape[1:]))
        if off is None:
            off = (at[0] + 31) // 32 * 32
            at[0] = off + nb
        t = nc.alloc_sbuf_tensor_at(name, list(shape), dt, offset=off)
        return t, off

    X, _ = sb("X", [P, KT, T])
    Hhi, oHhi = sb("Hhi", [P, KT, T], F32R)
    Hlo, oHlo = sb("Hlo", [P, KT, T], F32R)
    Ahi, oAhi = sb("Ahi", [P, KT, T], F32R)
    Alo, oAlo = sb("Alo", [P, KT, T], F32R)
    RAW = [sb(f"raw{i}", [P, 1024])[0] for i in range(NRAW)]
    WH = [sb(f"wh{i}", [P, 1024], F32R)[0] for i in range(NW)]
    WL = [sb(f"wl{i}", [P, 1024], F32R)[0] for i in range(NW)]
    R, _ = sb("R", [P, T])
    SS, _ = sb("SS", [P, T])
    SS2, _ = sb("SS2", [P, T])
    TM = [sb(f"tm{i}", [P, T + 2])[0] for i in range(NTMP)]
    vec, _ = sb("vec", [P, NVEC])
    gfm, _ = sb("gfm", [P, 8])
    ident, _ = sb("ident", [P, P])
    ones, _ = sb("ones", [P, P])
    st, _ = sb("st", [P, 8, 16])
    rt, _ = sb("rt", [P, 16])
    rt2, _ = sb("rt2", [P, 16])
    small, _ = sb("small", [P, 96])
    M = (at[0] + 31) // 32 * 32
    KB = 1024
    VT, _ = sb("VT", [P, 4, D], off=M)
    MC, _ = sb("MC", [P, KT, T], off=M)
    QR, _ = sb("QR", [P, 4, T], off=M + 16 * KB)
    KR, _ = sb("KR", [P, 4, T], off=M + 24 * KB)
    O, _ = sb("O", [P, KT, T], off=M + 16 * KB)
    MGhi, _ = sb("MGhi", [P, KT, T], F32R, off=M + 16 * KB)
    QI, _ = sb("QI", [P, 4, T], off=M + 32 * KB)
    KS, _ = sb("KS", [P, 4, T], off=M + 40 * KB)
    SG, _ = sb("SG", [P, KT, T], off=M + 32 * KB)
    MGlo, _ = sb("MGlo", [P, KT, T], F32R, off=M + 32 * KB)
    KST, _ = sb("KST", [P, T], off=M + 48 * KB)
    ST, _ = sb("ST", [P, T], off=M + 50 * KB)
    STATE, _ = sb("STATE", [P, 4, 256], off=M + 52 * KB)
    QO, _ = sb("QO", [P, 2, 256], off=M + 56 * KB)
    KE, _ = sb("KE", [P, 2, 256], off=M + 58 * KB)
    SCM, _ = sb("SCM", [P, T], off=M + 60 * KB)
    CAU, _ = sb("CAU", [P, T], off=M + 62 * KB)
    EBD, _ = sb("EBD", [P, 4, 4, 8], off=M + 64 * KB)
    NQ, _ = sb("NQ", [P, 4, T], off=M)
    NK, _ = sb("NK", [P, 4, T], off=M + 8 * KB)
    VB, _ = sb("VB", [P, 8, T], off=M + 16 * KB)
    RB = [sb(f"RB{i}", [P, 2, BW], off=M + 32 * KB + 2304 * i)[0] for i in range(2)]
    NAM, _ = sb("NAM", [P, 3, 32], off=M + 37 * KB)
    RQ, _ = sb("RQ", [P, 2, T], off=M + 38 * KB)
    RK, _ = sb("RK", [P, 2, T], off=M + 42 * KB)
    RV, _ = sb("RV", [P, 4, T], off=M + 46 * KB)
    NV, _ = sb("NV", [P, 4, T], off=oAhi + 8 * KB)
    ROPE, _ = sb("ROPE", [P, 2, T], off=oAlo + 8 * KB)
    GD, _ = sb("GD", [P, GW], off=oAlo + 12 * KB)
    DG, _ = sb("DG", [P, 4, P], off=M + 54 * KB)
    KF, _ = sb("KF", [P, 4, P], off=M + 56 * KB)
    KB_, _ = sb("KB", [P, 4, P], off=M + 58 * KB)
    SF, _ = sb("SF", [P, 4, P], off=M + 60 * KB)
    RS, _ = sb("RS", [P, T], off=M + 62 * KB)
    QF, _ = sb("QF", [P, T], off=oAlo + 8 * KB)
    QB, _ = sb("QB", [P, T], off=oAlo + 10 * KB)
    SB, _ = sb("SB", [P, 3, P], off=oAlo + 13 * KB + 512)
    XF, _ = sb("XF", [P, P], off=oAlo + 15 * KB)
    XB, _ = sb("XB", [P, P], off=oAlo + 15 * KB + 512)
    YH, _ = sb("YH", [P, 4, T], off=oAhi + 8 * KB)
    assert M + 64 * KB + 512 <= 229376, M
    PS = nc.alloc_psum_tensor("ps", [P, 8, 512], F32)
    BK = [PS[:, i, :] for i in range(8)]

    def f32(ap):
        return ap.bitcast(F32)

    def vc(name, i=0, n=1):
        return vec[:, VECO[name] + i:VECO[name] + i + n]

    class Slot:
        def __init__(self, t):
            self.t = t
            self.free = []

    tring = [Slot(t) for t in TM]
    tpos = [0]

    def tmp():
        s = tring[tpos[0] % NTMP]
        tpos[0] += 1
        s.ap = s.t[:, 0:T]
        return s

    bfree = [[] for _ in range(8)]
    mpos = [0]
    spos = [0]

    mset = [list(range(7))]

    def mbank():
        b = mset[0][mpos[0] % len(mset[0])]
        mpos[0] += 1
        return b

    def sbank():
        b = 3 + spos[0] % 4
        spos[0] += 1
        return b

    vec_tok = DMA("G", "dv", vec[:, :], dr["vec"])
    on_tok = V(lambda e: e.memset(ones[:, :], 1.0))

    units = []

    def add(name, n, k0=0, k1=8):
        units.append((dr[name][n, :, k0:k1, :], (k1 - k0)))

    def addv(name, half):
        for kk in range(4):
            units.append((dr[name][half, :, 2 * kk:2 * kk + 2, :], 8))

    FG = [(0, 8), (8, 16), (16, 22)]

    def add_ffn(gu, dn):
        for a, b in FG:
            for j in range(a, b):
                add(gu, j)
                add(gu, FT + j)
            for n in range(KT):
                add(dn, n, a, b)

    add_ffn("w_gu1", "w_d1")
    add("w_glr", 0)
    addv("w_v", 0)
    addv("w_v", 1)
    for h in range(4):
        add("w_q", h)
        add("w_k", h)
    for i in range(8):
        add("w_cc", i)
        add("w_cu", i)
        add("w_cb", i)
    for i in range(8):
        add("w_ga", i)
        add("w_oc", i)
    for i in range(8):
        add("w_r", i)
    for i in range(8):
        add("w_gb", i)
    for i in range(8):
        add("w_og", i)
    for i in range(8):
        add("w_o", i)
    add_ffn("w_gu2", "w_d2")
    addv("w_nv", 0)
    addv("w_rv", 0)
    for i in range(2):
        add("w_rq", i)
        add("w_rk", i)
    for i in range(4):
        add("w_nq", i)
        add("w_nk", i)
    for i in range(4):
        add("w_rg", i)
    for i in range(8):
        add("w_out2", i)
    for g in range(4):
        for j in range(8):
            add("w_up", 8 * g + j)
        for n in range(KT):
            add("w_dn", n, 8 * g, 8 * g + 8)
    NU = len(units)

    dtok = [None] * NU
    htok = [None] * NU
    ltok = [None] * NU
    ptok = [None] * NU

    def load(u, i=None):
        if u >= NU:
            return
        src, nb = units[u]
        if u == 0:
            first_d[i] = DMA("S", f"df{i}", RAW[0][:, 256 * i:256 * i + 256].rearrange("p (k n) -> p k n", k=2),
                             src[:, 2 * i:2 * i + 2, :])
            return
        w = [htok[u - NRAW], ltok[u - NRAW]] if u >= NRAW else []
        shape = [int(s) for s in src.shape]
        dst = RAW[u % NRAW][:, 0:128 * nb].rearrange("p (k n) -> p k n", k=shape[1])
        dtok[u] = DMA("S", f"dw{u % NRAW}", dst, src, *w)

    first_d, first_l = [None] * 4, [None] * 4

    def split_first(i):
        c = slice(256 * i, 256 * i + 256)
        htok[0] = A(lambda e: e.activation(WH[0][:, c], RAW[0][:, c], ACT.Copy), first_d[i])
        ltok[0] = first_l[i] = V(lambda e: e.tensor_tensor(WL[0][:, c], RAW[0][:, c], f32(WH[0][:, c]), ALU.subtract),
                                 htok[0])

    def split(u):
        if u >= NU:
            return
        n = 128 * units[u][1]
        raw, wh, wl = RAW[u % NRAW][:, 0:n], WH[u % NW][:, 0:n], WL[u % NW][:, 0:n]
        w = ptok[u - NW] if u >= NW else None
        htok[u] = A(lambda e: e.activation(wh, raw, ACT.Copy), dtok[u], w)
        ltok[u] = V(lambda e: e.tensor_tensor(wl, raw, f32(wh), ALU.subtract), htok[u])
        load(u + NRAW)

    cur = [0]
    pend = []
    late = [False]
    side = []

    mids = []

    def step(pe, evac, nside=1, mid=(), end=(), pre=()):
        u = cur[0]
        cur[0] += 1
        mids[:] = mid
        for f in pre:
            f()
        split(u + NW - 1)
        tok = pe(u)
        ptok[u] = tok[-1] if isinstance(tok, list) else tok
        pend.append(lambda: evac(tok))
        todo = [side.pop(0) for _ in range(min(nside, len(side)))]
        if not late[0]:
            flush()
        for f in todo:
            f()
        for f in end:
            f()
        if not late[0]:
            flush()

    def flush():
        while pend:
            pend.pop(0)()

    def lin(rhi, rlo, rtok, evac, nside=1, mid=(), end=(), pre=()):
        b = mbank()
        ps = BK[b][:, :]

        def pe(u):
            nb = units[u][1]
            wh, wl = WH[u % NW], WL[u % NW]
            tok = None
            for k in range(nb):
                while k == nb // 2 and mids:
                    mids.pop(0)()
                kc = slice(k * P, k * P + P)
                first = [ltok[u], *bfree[b]] if k == 0 else []
                if u == 0:
                    first = [first_l[k // 2]]
                PE(lambda e, k=k, kc=kc: e.matmul(ps, wh[:, kc], rhi[:, k, :], start=(k == 0), stop=False),
                   rtok[k], *first)
                PE(lambda e, k=k, kc=kc: e.matmul(ps, wh[:, kc], rlo[:, k, :], start=False, stop=False))
                tok = PE(lambda e, k=k, kc=kc: e.matmul(ps, wl[:, kc], rhi[:, k, :], start=False, stop=(k == nb - 1)),
                         sig=(k == nb - 1))
            return tok

        def ev(tok):
            bfree[b] = evac(ps, tok)

        step(pe, ev, nside, mid, end, pre)

    def linv(rhi, rlo, rtok, dst, htag, sums=None):
        bs = [sbank() for _ in range(4)]
        for kk in range(4):
            def pe(u, kk=kk):
                wh, wl = WH[u % NW], WL[u % NW]
                toks = []
                for t in range(4):
                    ps = BK[bs[t]][:, :]
                    tc = slice(t * P, t * P + P)
                    for j in range(2):
                        k = 2 * kk + j
                        wc = slice(j * 512, j * 512 + 512)
                        first = [ltok[u], rtok[k], *(bfree[bs[t]] if kk == 0 else [])]
                        PE(lambda e, ps=ps, k=k, tc=tc, wc=wc: e.matmul(
                            ps, rhi[:, k, tc], wh[:, wc], start=(k == 0), stop=False), *first)
                        PE(lambda e, ps=ps, k=k, tc=tc, wc=wc: e.matmul(
                            ps, rlo[:, k, tc], wh[:, wc], start=False, stop=False))
                        tok = PE(lambda e, ps=ps, k=k, tc=tc, wc=wc: e.matmul(
                            ps, rhi[:, k, tc], wl[:, wc], start=False, stop=(k == 7)), sig=(j == 1))
                    toks.append(tok)
                return toks

            def ev(toks, kk=kk):
                if kk < 3:
                    return
                for t in range(4):
                    for c in range(0, 512, 512 if sums is None else P):
                        kw = {} if sums is None else {"accum_out": sums(t, c // P)}
                        a = A(lambda e, t=t, c=c, kw=kw: e.activation(
                            dst(t) if sums is None else dst(t)[:, c:c + P],
                            BK[bs[t]][:, :] if sums is None else BK[bs[t]][:, c:c + P], ACT.Copy,
                            scale=rt[:, t:t + 1], **kw), toks[t], rt_tok[0], *dst_free[0])
                    bfree[bs[t]] = [a]
                    vt_tok[htag, t] = a

            step(pe, ev)

    vt_tok = {}
    dst_free = [[]]

    R_tok = [None]
    rt_tok = [None]
    x_tok = [None] * KT
    h_tok = [None] * KT
    a_tok = [None] * KT

    def rsq(dst, src, n, sc, *waits):
        m, s, y, t = (st[:, i, 0:n] for i in range(4))
        return newton(dst, m, s, y, t, src, sc, *waits)

    def newton(dst, m, s, y, t, src, sc, *waits):
        v = V(lambda e: e.tensor_scalar(m, src, sc, EPS, ALU.mult, ALU.add), *waits)
        a = A(lambda e: e.activation(s, m, ACT.Sqrt), v)
        v = V(lambda e: e.reciprocal(y, s), a)
        v = V(lambda e: e.scalar_tensor_tensor(out=t, in0=y, scalar=-0.5, in1=y, op0=ALU.mult, op1=ALU.mult), v)
        v = V(lambda e: e.tensor_tensor(t, t, m, ALU.mult), v)
        return V(lambda e: e.scalar_tensor_tensor(out=dst, in0=t, scalar=1.5, in1=y, op0=ALU.add, op1=ALU.mult), v)

    def rsq_rows(dst, b, srcs, n, toks, *waits):
        for i, x in enumerate(srcs):
            p = PE(lambda e, i=i, x=x: e.matmul(BK[b][:, :], ones[:, :], x, start=(i == 0), stop=(i == len(srcs) - 1)),
                   *toks, on_tok, *bfree[b], sig=(i == len(srcs) - 1))
        m, y, t = tmp(), tmp(), tmp()
        v = V(lambda e: e.tensor_scalar(m.ap, BK[b][:, :], 1.0 / n, EPS, ALU.mult, ALU.add), p, *m.free)
        bfree[b] = [v]
        a = A(lambda e: e.activation(y.ap, m.ap, ACT.Ln), v, *y.free)
        a = A(lambda e: e.activation(y.ap, y.ap, ACT.Exp, scale=-0.5), a)
        a = A(lambda e: e.activation(t.ap, y.ap, ACT.Square), a, *t.free)

        def newton_step():
            v = V(lambda e: e.scalar_tensor_tensor(out=m.ap, in0=t.ap, scalar=-0.5, in1=m.ap, op0=ALU.mult,
                                                   op1=ALU.mult), a)
            v = V(lambda e: e.scalar_tensor_tensor(out=m.ap if dst is None else dst, in0=m.ap, scalar=1.5, in1=y.ap,
                                                   op0=ALU.add, op1=ALU.mult), v, *waits)
            m.free = y.free = t.free = [v]
            return v, m
        return newton_step, p

    def token_sums(col, srcs, toks, n=1):
        tok = None
        for t in range(4):
            for i, s in enumerate(srcs):
                tok = PE(lambda e, t=t, i=i, s=s: e.matmul(
                    BK[7][:, col + t * n:col + t * n + 1], s[:, t * P:t * P + P], ones[:, 0:1],
                    start=(i == 0), stop=(i == len(srcs) - 1)), *toks, on_tok, *bfree[7], sig=(t == 3))
        return tok

    def rows(src, n, tok, b=None):
        b = sbank() if b is None else b
        for t in range(4):
            p = PE(lambda e, t=t: e.matmul(BK[b][:, t * P:t * P + P], src[:, t * n:t * n + 1].broadcast_to([P, P]),
                                           ident[:, :], start=True, stop=True), tok, c_tok, *bfree[b], sig=(t == 3))
        return b, p

    ss_tok = [None]

    def square_into(acc, key, n, src, tok, scale=None):
        kw = {} if scale is None else {"scale": scale}
        if n == 0:
            key[0] = A(lambda e: e.activation(acc[:, :], src, ACT.Square, **kw), tok, *key[1:])
        else:
            q = tmp()
            a = A(lambda e: e.activation(q.ap, src, ACT.Square, **kw), tok, *q.free)
            key[0] = V(lambda e: e.tensor_tensor(acc[:, :], acc[:, :], q.ap, ALU.add), a, key[0])
            q.free = [key[0]]

    def to_h(n, gname, tok, garr=None):
        g = garr[:, n:n + 1] if garr is not None else vc(gname, n)
        a = A(lambda e: e.activation(Hhi[:, n, :], X[:, n, :], ACT.Copy, scale=g), tok, vec_tok)
        h_tok[n] = V(lambda e: e.scalar_tensor_tensor(out=Hlo[:, n, :], in0=X[:, n, :], scalar=g,
                                                      in1=f32(Hhi[:, n, :]), op0=ALU.mult, op1=ALU.subtract), a)

    def norm_side():
        keep = {}

        def one():
            keep["p"] = token_sums(0, [SS], [ss_tok[0]])
            keep["v"] = rsq(rt[:, 0:4], BK[7][:, 0:4], 4, 1.0 / D, keep["p"])
            bfree[7] = [keep["v"]]
            rt_tok[0] = keep["v"]

        def two():
            b, p = rows(rt, 1, keep["v"], 7)
            R_tok[0] = V(lambda e: e.tensor_copy(R[:, :], BK[b][:, :]), p)
            bfree[b] = [R_tok[0]]
            late[0] = False

        late[0] = True
        side[0:0] = [lambda: None, one, two]

    def ln_table():
        pr.put("A", lambda e: e.preload_act_table_set("natural_log_exp_and_others"), [])

    def norm_rows():
        def one():
            ln_table()
            R_tok[0], _ = rsq_rows(R[:, :], 7, [SS[:, :]], D, [ss_tok[0]])[0]()
            late[0] = False

        late[0] = True
        side.insert(0, one)

    def hilo(hi, lo, src, tok, *waits):
        a = A(lambda e: e.activation(hi, src, ACT.Copy), tok, *waits)
        return V(lambda e: e.tensor_tensor(lo, src, f32(hi), ALU.subtract), a), a

    def ffn(nxt):
        for gi, (a, b) in enumerate(FG):
            keep = {}
            for j in range(a, b):
                def ev_g(ps, tok):
                    t, s, m = tmp(), tmp(), tmp()
                    v = V(lambda e: e.tensor_tensor(t.ap, ps, R[:, :], ALU.mult), tok, R_tok[0], *t.free)
                    q = A(lambda e: e.activation(s.ap, t.ap, ACT.Silu), v, *s.free)
                    w = V(lambda e: e.tensor_tensor(m.ap, s.ap, R[:, :], ALU.mult), q, *m.free)
                    t.free, s.free = [q], [w]
                    keep["m"] = (m, w)
                    return [v]

                def ev_u(ps, tok, j=j - a):
                    m, w = keep["m"]
                    t = tmp()
                    v = V(lambda e: e.tensor_tensor(t.ap, ps, m.ap, ALU.mult), tok, w, *t.free)
                    m.free = [v]
                    a_tok[j], _ = hilo(Ahi[:, j, :], Alo[:, j, :], t.ap, v)
                    t.free = [a_tok[j]]
                    return [v]

                lin(Hhi, Hlo, h_tok, ev_g)
                lin(Hhi, Hlo, h_tok, ev_u)
            for n in range(KT):
                def ev_d(ps, tok, n=n, last=(gi == len(FG) - 1)):
                    x_tok[n] = v = V(lambda e: e.scalar_tensor_tensor(
                        out=X[:, n, :], in0=ps, scalar=0.5, in1=X[:, n, :], op0=ALU.mult, op1=ALU.add),
                        tok, x_tok[n])
                    if last:
                        nxt(n)
                    return [v]
                lin(Ahi, Alo, a_tok, ev_d)

    for n in range(KT):
        x_tok[n] = DMA("S", f"dx{n}", X[:, n, :], dr["xt"][n])
        if n < 4:
            load(0, n)
    for u in range(1, NRAW):
        load(u)
    c_tok = DMA("G", "dc", ident[:, :], dr["ident"])
    for n in range(KT):
        if n < 4:
            split_first(n)
        to_h(n, "g1", x_tok[n])
    load(NRAW)
    split(1)
    for n in range(KT):
        square_into(SS, ss_tok, n, X[:, n, :], x_tok[n])
    norm_rows()
    side.insert(0, lambda: None)

    def after_ffn1(n):
        to_h(n, "gm", x_tok[n])
        square_into(SS, ss_tok, n, X[:, n, :], x_tok[n])
        if n == KT - 1:
            norm_side()

    ffn(after_ffn1)

    mix_c = [DMA("A", "dm", KR[0:16, 2, :], dr["gup"]), DMA("A", "dm", SCM[:, :], dr["scm"]), DMA("A", "dm", CAU[:, :], dr["cau"])][-1]
    st_tok = V(lambda e: e.memset(ST[:, :], 0.0))
    gl = {}

    def ev_glr(ps, tok):
        gl["v"] = V(lambda e: e.tensor_tensor(KR[0:16, 3, :], ps[0:16, :], R[0:16, :], ALU.mult), tok, R_tok[0])
        return [gl["v"]]

    b_tok = [None] * 4

    def gate(h):
        def go():
            b = 7
            p = PE(lambda e: e.matmul(BK[b][:, :], KR[0:16, 2, h * P:h * P + P], KR[0:16, 3, :],
                                      start=True, stop=True), gl["v"], mix_c, *bfree[b], sig=True)
            z, e1, m = tmp(), tmp(), tmp()
            v = V(lambda e: e.tensor_scalar(z.ap, BK[b][:, :], vc("gb", h), None, ALU.add), p, vec_tok, *z.free)
            bfree[b] = [v]
            a = A(lambda e: e.activation(e1.ap, z.ap, ACT.Abs), v, *e1.free)
            a = A(lambda e: e.activation(e1.ap, e1.ap, ACT.Exp, scale=-1.0), a)
            a = A(lambda e: e.activation(e1.ap, e1.ap, ACT.Ln, bias=1.0), a)
            v = V(lambda e: e.scalar_tensor_tensor(out=m.ap, in0=z.ap, scalar=0.0, in1=e1.ap,
                                                   op0=ALU.min, op1=ALU.subtract), a, *m.free)
            z.free = e1.free = [v]
            b_tok[h] = V(lambda e: e.tensor_tensor_scan(KS[:, h, :], SCM[:, :], m.ap, 0.0, ALU.mult, ALU.add),
                         v, mix_c)
            m.free = [b_tok[h]]
        return go

    C64 = 64
    eb_tok = [None] * 4
    E = {}

    def chunks(ap):
        return ap.rearrange("p (c t) -> p c t", t=C64)

    def decays(h):
        def go():
            b3 = chunks(KS[:, h, :])
            ref = b3[:, :, 31:32].broadcast_to([P, 8, C64])
            lst = b3[:, :, 63:64].broadcast_to([P, 8, C64])
            d1, e1, e2, e3 = tmp(), tmp(), tmp(), tmp()
            v = V(lambda e: e.tensor_tensor(chunks(d1.ap), b3, ref, ALU.subtract), b_tok[h], *d1.free)
            v2 = V(lambda e: e.tensor_tensor(chunks(e3.ap), lst, b3, ALU.subtract), b_tok[h], *e3.free)
            a1 = A(lambda e: e.activation(e1.ap, d1.ap, ACT.Exp, scale=1 / 16), v, *e1.free)
            a2 = A(lambda e: e.activation(e2.ap, d1.ap, ACT.Exp, scale=-1 / 16), v, *e2.free)
            a3 = A(lambda e: e.activation(e3.ap, e3.ap, ACT.Exp, scale=1 / 16), v2)
            a4 = A(lambda e: e.activation(EBD[:, h, 0, :], b3[:, :, 31], ACT.Exp, scale=1 / 16), b_tok[h])
            a5 = A(lambda e: e.activation(EBD[:, h, 1, :], b3[:, :, 63], ACT.Exp, scale=1 / 16), b_tok[h])
            V(lambda e: e.tensor_copy(EBD[:, h, 2, 0:8:2], EBD[:, h, 0, 0:8:2]), a4)
            V(lambda e: e.tensor_tensor(EBD[:, h, 2, 1:8:2], EBD[:, h, 0, 1:8:2], EBD[:, h, 1, 0:8:2], ALU.mult), a5)
            v3 = V(lambda e: e.tensor_tensor(EBD[:, h, 3, 0:4], EBD[:, h, 1, 0:8:2], EBD[:, h, 1, 1:8:2], ALU.mult), a5)
            d1.free = [a2]
            E[h] = (e1, e2, e3, a1, a2, a3, v3, a5)
        return go

    q_tok = [None] * 4
    k_tok = [None] * 4

    def ev_q(h):
        def ev(ps, tok):
            e1, a1, a4 = E[h][0], E[h][3], E[h][6]
            t = tmp()
            v = V(lambda e: e.scalar_tensor_tensor(out=t.ap, in0=ps, scalar=P ** -0.5, in1=R[:, :],
                                                   op0=ALU.mult, op1=ALU.mult), tok, R_tok[0], *t.free)
            w = V(lambda e: e.tensor_tensor(QR[:, h, :], t.ap, e1.ap, ALU.mult), v, a1)
            e1.free = t.free = [w]
            V(lambda e: e.tensor_tensor(chunks(QO[:, h % 2, :]), chunks(QR[:, h, :])[:, 1:8:2, :],
                                        EBD[:, h, 0, 1:8:2].unsqueeze(2).broadcast_to([P, 4, C64]),
                                        ALU.mult), w, a4, s_tok.get(h - 2))
            q_tok[h] = V(lambda e: e.tensor_tensor(chunks(QI[:, h, :]), chunks(QR[:, h, :]),
                                                   EBD[:, h, 2, :].unsqueeze(2).broadcast_to([P, 8, C64]),
                                                   ALU.mult), w)
            return [v]
        return ev

    def ev_k(h):
        def ev(ps, tok):
            _, e2, e3, _, a2, a3, a4, a5 = E[h]
            t = tmp()
            v = V(lambda e: e.tensor_tensor(t.ap, ps, R[:, :], ALU.mult), tok, R_tok[0], *t.free)
            w = V(lambda e: e.tensor_tensor(KR[:, h, :], t.ap, e2.ap, ALU.mult), v, a2)
            k2 = V(lambda e: e.tensor_tensor(chunks(KE[:, h % 2, :]), chunks(t.ap)[:, 0:8:2, :],
                                             chunks(e3.ap)[:, 0:8:2, :], ALU.mult), v, a3, s_tok.get(h - 2))
            V(lambda e: e.tensor_tensor(chunks(KS[:, h, :])[:, 1:8:2, :], chunks(t.ap)[:, 1:8:2, :],
                                        chunks(e3.ap)[:, 1:8:2, :], ALU.mult), a5)
            k_tok[h] = V(lambda e: e.tensor_tensor(chunks(KS[:, h, :])[:, 0:8:2, :], chunks(KE[:, h % 2, :]),
                                                   EBD[:, h, 1, 1:8:2].unsqueeze(2).broadcast_to([P, 4, C64]),
                                                   ALU.mult), k2)
            e2.free, e3.free = [w], [k_tok[h]]
            t.free = [k_tok[h]]
            return [v]
        return ev

    gk = {"kstfree": [], "stfree": [], "statefree": []}
    s_tok = {}
    o_tok = [None] * KT

    def osl(i):
        return 4 * (i % 2) + i // 2

    def gla(h):
        L = {}

        def scores():
            b = sbank()
            for t in range(3):
                p = PE(lambda e, t=t: e.transpose(BK[b][:, t * P:t * P + P], KS[:, h, t * P:t * P + P], ident[:, :]),
                       k_tok[h], c_tok, *bfree[b], sig=(t == 2))
            L["kst"] = A(lambda e: e.activation(KST[:, 0:3 * P], BK[b][:, 0:3 * P], ACT.Copy), p, *gk["kstfree"])
            bfree[b] = [L["kst"]]
            b2 = sbank()
            for t in range(4):
                tc = slice(t * P, t * P + P)
                PE(lambda e, tc=tc: e.matmul(BK[b2][:, tc], KR[:, h, tc], QR[:, h, tc], start=True, stop=True),
                   k_tok[h], q_tok[h], *bfree[b2])
            for t in range(4):
                p = PE(lambda e, t=t: e.matmul(BK[b2][0:64, t * P + 64:t * P + P], KE[:, h % 2, 64 * t:64 * t + 64],
                                               QO[:, h % 2, 64 * t:64 * t + 64], start=True, stop=True), sig=(t == 3))
            s_tok[h] = p
            L["st"] = V(lambda e: e.copy_predicated(ST[:, :], CAU[:, :].bitcast(I32), BK[b2][:, :]),
                        p, st_tok, mix_c, *gk["stfree"])
            bfree[b2] = [L["st"]]

        def kv():
            bs = [sbank(), sbank()]
            for t in range(3):
                cc = slice(256 * (t % 2), 256 * (t % 2) + 256)
                p = PE(lambda e, t=t, cc=cc: e.matmul(
                    BK[bs[t // 2]][:, cc], KST[:, t * P:t * P + P], VT[:, t, 256 * h:256 * h + 256],
                    start=True, stop=True), L["kst"], vt_tok[h // 2, t], *bfree[bs[t // 2]], sig=(t > 0))
                if t == 1:
                    L["v"] = V(lambda e: e.tensor_copy(STATE[:, 1, :], BK[bs[0]][:, 0:256]), p, *gk["statefree"])
                if t > 0:
                    L["v"] = V(lambda e, t=t, cc=cc: e.scalar_tensor_tensor(
                        out=STATE[:, t + 1, :], in0=STATE[:, t, :], scalar=EBD[:, h, 3, t:t + 1],
                        in1=BK[bs[t // 2]][:, cc], op0=ALU.mult, op1=ALU.add), p, L["v"])
            bfree[bs[0]] = bfree[bs[1]] = [L["v"]]
            gk["kstfree"] = [p]

        def outs():
            for d in range(2):
                b = sbank()
                vcs = slice(256 * h + 128 * d, 256 * h + 128 * d + 128)
                for t in range(4):
                    tc = slice(t * P, t * P + P)
                    p = PE(lambda e, t=t, tc=tc, b=b, vcs=vcs: e.matmul(
                        BK[b][:, tc], VT[:, t, vcs], ST[:, tc], start=True, stop=(t == 0)),
                        L["st"], L["v"], vt_tok[h // 2, t], *bfree[b])
                    if t > 0:
                        p = PE(lambda e, t=t, tc=tc, b=b, d=d: e.matmul(
                            BK[b][:, tc], STATE[:, t, 128 * d:128 * d + 128], QI[:, h, tc], start=False, stop=True),
                            sig=(t == 3))
                i = 2 * h + d
                o_tok[i] = V(lambda e, i=i, b=b: e.tensor_copy(O[:, osl(i), :], BK[b][:, :]), p)
                bfree[b] = [o_tok[i]]
            gk["stfree"] = [p]
            gk["statefree"] = [p]
            gk["last"] = p

        def squares():
            sq = []
            for i in (2 * h, 2 * h + 1):
                s = tmp()
                a = A(lambda e, i=i, s=s: e.activation(s.ap, O[:, osl(i), :], ACT.Square), o_tok[i], *s.free)
                sq.append((s, a))
            (s0, a0), (s1, a1) = sq
            L["sq"] = (s0, V(lambda e: e.tensor_tensor(s0.ap, s0.ap, s1.ap, ALU.add), a0, a1))
            s1.free = [L["sq"][1]]

        def sums():
            s, v = L["sq"]
            L["n"], p = rsq_rows(None, 7, [s.ap], 256, [v])
            s.free = [p]

        def scale():
            v, n = L["n"]()
            for i in (2 * h, 2 * h + 1):
                o_tok[i] = V(lambda e, i=i: e.tensor_tensor(O[:, osl(i), :], O[:, osl(i), :], n.ap, ALU.mult), v, o_tok[i])
            n.free = [o_tok[2 * h + 1]]

        return scores, kv, outs, squares, sums, scale

    mset[0] = [0, 1, 2]
    lin(Hhi, Hlo, h_tok, ev_glr)
    flush_side = lambda: [side.pop(0)() for _ in range(len(side))]
    for half in range(2):
        if half == 1:
            ln_table()
            side.extend([gate(h) for h in range(4)])
        linv(Hhi, Hlo, h_tok, lambda t, half=half: VT[:, t, 512 * half:512 * half + 512], half)
    heads = [gla(h) for h in range(4)]
    mids_, ends_ = [[] for _ in range(13)], [[] for _ in range(13)]
    for h in range(4):
        mids_[2 * h].append(decays(h))
        for k, f in ((2, 0), (3, 1), (4, 2)):
            ends_[2 * h + k].append(heads[h][f])
        mids_[2 * h + 5].append(heads[h][3])
        mids_[2 * h + 6].insert(0, heads[h][4])
        ends_[2 * h + 6].append(heads[h][5])
    for h in range(4):
        lin(Hhi, Hlo, h_tok, ev_q(h), 0, mids_[2 * h], ends_[2 * h])
        lin(Hhi, Hlo, h_tok, ev_k(h), 0, mids_[2 * h + 1], ends_[2 * h + 1])
    cv = {}
    pad = {}

    def ev_cc(ps, tok):
        t = tmp()
        v = V(lambda e: e.tensor_tensor(t.ap, ps, R[:, :], ALU.mult), tok, R_tok[0], *t.free)
        cv["cc"] = (t, v)
        return [v]

    def ev_cu(i):
        def ev(ps, tok):
            c, cw = cv["cc"]
            t, u, y = tmp(), tmp(), tmp()
            v = V(lambda e: e.tensor_tensor(t.ap, ps, R[:, :], ALU.mult), tok, R_tok[0], *t.free)
            z = V(lambda e: e.memset(u.t[:, 0:2], 0.0), *u.free)
            w = V(lambda e: e.tensor_tensor(u.t[:, 2:T + 2], t.ap, c.ap, ALU.mult), v, cw, *u.free)
            t.free = c.free = [w]
            a = A(lambda e: e.activation(y.ap, u.t[:, 0:T], ACT.Copy, scale=vc("cw0", i)), z, w, vec_tok, *y.free)
            w = V(lambda e: e.scalar_tensor_tensor(out=y.ap, in0=u.t[:, 1:T + 1], scalar=vc("cw1", i), in1=y.ap,
                                                   op0=ALU.mult, op1=ALU.add), a)
            w = V(lambda e: e.scalar_tensor_tensor(out=y.ap, in0=u.t[:, 2:T + 2], scalar=vc("cw2", i), in1=y.ap,
                                                   op0=ALU.mult, op1=ALU.add), w)
            u.free = [w]
            cv["y"] = (y, w)
            return [v]
        return ev

    def ev_cb(i):
        def ev(ps, tok):
            y, yw = cv["y"]
            t, r = tmp(), tmp()
            v = V(lambda e: e.tensor_tensor(t.ap, ps, R[:, :], ALU.mult), tok, R_tok[0], *t.free)
            w = V(lambda e: e.tensor_tensor(r.ap, t.ap, y.ap, ALU.mult), v, yw, *r.free)
            t.free = y.free = [w]
            a_tok[i], _ = hilo(Ahi[:, i, :], Alo[:, i, :], r.ap, w)
            r.free = [a_tok[i]]
            return [v]
        return ev

    for i in range(8):
        for j, ev in enumerate((ev_cc, ev_cu(i), ev_cb(i))):
            n = 8 + 3 * i + j
            lin(Hhi, Hlo, h_tok, ev, 0, mids_[n] if n < 13 else (), ends_[n] if n < 13 else ())

    def gated(func, dst=None):
        hold = {}

        def ev(ps, tok):
            t = tmp()
            v = V(lambda e: e.tensor_tensor(t.ap, ps, R[:, :], ALU.mult), tok, R_tok[0], *t.free)
            if dst is None:
                s = tmp()
                a = A(lambda e: e.activation(s.ap, t.ap, func), v, *s.free)
                hold["s"] = s
            else:
                a = A(lambda e: e.activation(dst, t.ap, func), v, gk["last"])
            t.free = [a]
            hold["a"] = a
            return [v]
        return ev, hold

    m_tok = [None] * KT
    for i in range(8):
        ev, hold = gated(ACT.Sigmoid)
        lin(Hhi, Hlo, h_tok, ev)

        def ev_oc(ps, tok, i=i, hold=hold):
            s = hold["s"]
            m_tok[i] = V(lambda e: e.tensor_tensor(MC[:, i, :], ps, s.ap, ALU.mult), tok, hold["a"], gk["last"])
            s.free = [m_tok[i]]
            return [m_tok[i]]
        lin(Ahi, Alo, a_tok, ev_oc)
    flush_side()
    for i in range(8):
        def ev_r(ps, tok, i=i):
            t, s, g = tmp(), tmp(), tmp()
            v = V(lambda e: e.tensor_tensor(t.ap, ps, R[:, :], ALU.mult), tok, R_tok[0], *t.free)
            a = A(lambda e: e.activation(s.ap, t.ap, ACT.Silu), v, *s.free)
            t.free = [a]
            w = V(lambda e: e.scalar_tensor_tensor(out=g.ap, in0=O[:, osl(i), :], scalar=vc("gla", i), in1=s.ap,
                                                   op0=ALU.mult, op1=ALU.mult), a, o_tok[i], vec_tok, *g.free)
            s.free = [w]
            a_tok[i], _ = hilo(Ahi[:, i, :], Alo[:, i, :], g.ap, w)
            g.free = [a_tok[i]]
            return [v]
        lin(Hhi, Hlo, h_tok, ev_r)
    sg = []
    for i in range(8):
        ev, hold = gated(ACT.Sigmoid, SG[:, i, :])
        sg.append(hold)
        lin(Hhi, Hlo, h_tok, ev)
    mg_tok = [None] * KT
    for i in range(8):
        def ev_og(ps, tok, i=i):
            t, m = tmp(), tmp()
            v = V(lambda e: e.tensor_tensor(t.ap, ps, SG[:, i, :], ALU.mult), tok, sg[i]["a"], *t.free)
            w = V(lambda e: e.tensor_tensor(m.ap, t.ap, MC[:, i, :], ALU.add), v, m_tok[i], *m.free)
            t.free = [w]
            mg_tok[i], _ = hilo(MGhi[:, i, :], MGlo[:, i, :], m.ap, w, a_tok[7])
            m.free = [mg_tok[i]]
            return [v]
        lin(Ahi, Alo, a_tok, ev_og)
    for n in range(8):
        def ev_o(ps, tok, n=n):
            x_tok[n] = v = V(lambda e: e.tensor_tensor(X[:, n, :], ps, X[:, n, :], ALU.add), tok, x_tok[n])
            to_h(n, "g2", v)
            square_into(SS, ss_tok, n, X[:, n, :], v)
            if n == KT - 1:
                norm_rows()
            return [v]
        lin(MGhi, MGlo, mg_tok, ev_o)

    g_tok = V(lambda e: e.tensor_tensor(gfm[:, :], vc("gf", 0, 8), vc("gm2", 0, 8), ALU.mult), vec_tok)
    ss2_tok = [None]

    def after_ffn2(n):
        to_h(n, None, x_tok[n], garr=gfm)
        square_into(SS, ss_tok, n, X[:, n, :], x_tok[n])
        square_into(SS2, ss2_tok, n, X[:, n, :], x_tok[n], scale=vc("gf", n))
        if n < KT - 1:
            return
        L = {}

        def one():
            token_sums(0, [SS], [ss_tok[0]])
            p = token_sums(4, [SS2], [ss2_tok[0]])
            r1, r2, q, m = rt2[:, 0:4], rt2[:, 4:8], rt2[:, 8:12], rt2[:, 12:16]
            v = rsq(r1, BK[7][:, 0:4], 4, 1.0 / D, p)
            L["r1"] = v
            w = V(lambda e: e.tensor_tensor(q, r1, r1, ALU.mult), v)
            w = V(lambda e: e.tensor_tensor(m, q, BK[7][:, 4:8], ALU.mult), w)
            bfree[7] = [w]
            w = rsq(r2, m, 4, 1.0 / D, w)
            L["v"] = V(lambda e: e.tensor_tensor(rt[:, 0:4], r1, r2, ALU.mult), w)
            rt_tok[0] = L["v"]

        def two():
            b, p = rows(rt, 1, L["v"], 7)
            R_tok[0] = V(lambda e: e.tensor_copy(R[:, :], BK[b][:, :]), p)
            bfree[b] = [R_tok[0]]
            b2, p2 = rows(rt2, 1, L["r1"], 2)
            L["w"] = V(lambda e: e.tensor_copy(SS2[:, :], BK[b2][:, :]), p2)
            bfree[b2] = [L["w"]]
            late[0] = False

        def x2(n):
            def go():
                x_tok[n] = V(lambda e: e.scalar_tensor_tensor(
                    out=X[:, n, :], in0=X[:, n, :], scalar=vc("gf", n), in1=SS2[:, :], op0=ALU.mult, op1=ALU.mult),
                    L["w"], x_tok[n], h_tok[n], ss_tok[0], ss2_tok[0])
            return go
        late[0] = True
        side[0:0] = [lambda: None, one, two] + [(lambda n=n: (x2(2 * n)(), x2(2 * n + 1)())) for n in range(4)]

    mset[0] = list(range(7))
    ffn(after_ffn2)

    mset[0] = [0, 1]
    m_end = ptok[cur[0] - 1]
    gd_tok = DMA("A", "dg", GD[:, :], dr["gd"], m_end)
    rope_tok = DMA("A", "dr", ROPE[:, :, :], dr["rope"], m_end)
    nam_tok = DMA("A", "dn", NAM[:, :, :], dr["nam"], m_end)
    nq_tok = [None] * 4
    nk_tok = [None] * 4
    BS = [0, 8, 24, 32]
    vb_tok = {}

    def bands(cb):
        for i in range(8):
            vb_tok[cb] = DMA("S", f"vb{cb}", VB[32 * (i % 4):32 * (i % 4) + 32, 2 * cb + i // 4, :],
                             NV[64 * (i % 2) + BS[cb]:64 * (i % 2) + BS[cb] + 32, i // 2, :],
                             vt_tok["n", i // 2])

    rbt = {}
    rb_free = [[m_end], [m_end]]

    def raw_bias(hp):
        for j in range(2):
            rbt[hp] = DMA("G", f"rb{hp % 2}", RB[hp % 2][:, j, :], dr["rpb"][2 * hp + j], *rb_free[hp % 2])

    lg, l1, l2, l3 = (small[:, 40 + 12 * i:52 + 12 * i] for i in range(4))
    e128 = small[:, 88:92]
    dg_tok = [None]
    def log_gamma():
        ln_table()
        a = A(lambda e: e.activation(l1, vc("dec", 0, 12), ACT.Exp), vec_tok)
        v = V(lambda e: e.tensor_scalar(l2, l1, -1.0, 1.0, ALU.mult, ALU.add), a)
        a = A(lambda e: e.activation(lg, l2, ACT.Ln), v)
        v = V(lambda e: e.tensor_scalar(l3, l2, -1.0, 1.0, ALU.mult, ALU.add), v)
        v = V(lambda e: e.tensor_scalar(l3, l3, 1e-30, None, ALU.max), v)
        v = V(lambda e: e.reciprocal(l3, l3), v)
        v = V(lambda e: e.tensor_tensor(l3, l3, l1, ALU.mult), v)
        v = V(lambda e: e.tensor_tensor(lg, lg, l3, ALU.mult), v, a)
        v = V(lambda e: e.tensor_scalar(l1, lg, -1.0, None, ALU.mult), v)
        a = A(lambda e: e.activation(e128, lg[:, 8:12], ACT.Exp, scale=128.0), v)
        for h in range(4):
            w = V(lambda e, h=h: e.tensor_scalar(DG[:, h, :], GD[:, 0:P], lg[:, h:h + 1], None, ALU.mult),
                  gd_tok, v, m_end)
            w = V(lambda e, h=h: e.scalar_tensor_tensor(out=DG[:, h, :], in0=GD[:, 0:P], scalar=l1[:, 4 + h:5 + h],
                                                        in1=DG[:, h, :], op0=ALU.mult, op1=ALU.min), w)
        dg_tok[0] = A(lambda e: e.activation(DG[:, :, :], DG[:, :, :], ACT.Exp), w)

    dst_free[0] = [m_end]
    raw_bias(0)
    raw_bias(1)
    side[3:3] = [log_gamma]
    linv(Hhi, Hlo, h_tok, lambda t: NV[:, t, :], "n")
    linv(Hhi, Hlo, h_tok, lambda t: RV[:, t, :], "r", lambda t, h: small[:, 24 + 4 * t + h:25 + 4 * t + h])
    v = V(lambda e: e.tensor_scalar(small[:, 24:40], small[:, 24:40], 1.0 / P, None, ALU.mult), vt_tok["r", 3])
    for t in range(4):
        vt_tok["r", t] = G(lambda e, t=t: e.tensor_tensor(
            RV[:, t, :].rearrange("p (h d) -> p h d", h=4), RV[:, t, :].rearrange("p (h d) -> p h d", h=4),
            small[:, 24 + 4 * t:28 + 4 * t].unsqueeze(2).broadcast_to([P, 4, P]), ALU.subtract), v)

    PAT = [0, 1, 1, 2]
    OFF = [0, -8, -8, -16]
    na = {}
    ob = {}
    na_tok = [None] * 4

    def na_g(p):
        hp = p // 4
        ss = []
        for q in range(2):
            cb = (p + q) % 4
            s = tmp()
            g = G(lambda e, s=s, cb=cb: e.tensor_tensor(
                s.ap.rearrange("p (h i j) -> p h i j", h=2, j=32),
                RB[hp % 2][:, :, 16 + OFF[cb]:16 + OFF[cb] + 256].rearrange("p h (i j) -> p h i j", j=32),
                NAM[:, PAT[cb], :].unsqueeze(1).unsqueeze(1).broadcast_to([P, 2, 8, 32]), ALU.add),
                rbt[hp], nam_tok, *s.free)
            ss.append((s, g))
        if p % 4 == 2:
            rb_free[hp % 2] = [g]
            if hp + 2 < 4:
                raw_bias(hp + 2)
        na["g"] = ss

    def na_s(p):
        hp = p // 4
        k3 = NK[:, hp, :].rearrange("p (r c) -> p r c", c=64)
        ss = na["g"]
        for j in (1, 0):
            hs = slice(64 * j, 64 * j + 64)
            for q in range(2):
                cb = (p + q) % 4
                pt = PE(lambda e, j=j, hs=hs, q=q, cb=cb: e.matmul(
                    BK[3 + j][:, 256 * q:256 * q + 256], NQ[hs, hp, cb * P:cb * P + P], k3[hs, :, BS[cb]:BS[cb] + 32],
                    start=True, stop=True), nq_tok[hp], nk_tok[hp], *bfree[3 + j], sig=(q == 1 and j == 0))
        for q, (s, g) in enumerate(ss):
            ss[q] = (s, V(lambda e, s=s, q=q: e.tensor_tensor(
                s.ap.rearrange("p (h k) -> p h k", h=2), PS[:, 3:5, 256 * q:256 * q + 256],
                s.ap.rearrange("p (h k) -> p h k", h=2), ALU.add), pt, g))
            v = ss[q][1]
            bfree[3] = bfree[4] = [v]
            s3 = s.ap.rearrange("p (h k) -> p h k", h=2)
            mx = 4 * q
            nm, rs, ri = (small[:, 8 * i + mx:8 * i + mx + 2] for i in range(3))
            v = V(lambda e, nm=nm, s3=s3: e.tensor_reduce(nm, s3, AX_X, ALU.max, negate=True), v,
                  *na.get(("free", q), []))
            ss[q] = (s, s3, nm, rs, ri, v)
        na["e"] = ss

    def na_e(p):
        ss = na["e"]
        for q, (s, s3, nm, rs, ri, v) in enumerate(ss):
            for j in range(2):
                a = A(lambda e, j=j, s3=s3, nm=nm, rs=rs: e.activation(
                    s3[:, j, :], s3[:, j, :], ACT.Exp, bias=nm[:, j:j + 1], accum_out=rs[:, j:j + 1]), v)
            ss[q] = (s, s3, rs, ri, a)
        na["x"] = ss

    def na_x(p):
        for q, (s, s3, rs, ri, a) in enumerate(na["x"]):
            v = V(lambda e, rs=rs, ri=ri: e.reciprocal(ri, rs), a)
            for j in range(2):
                w = V(lambda e, j=j, s3=s3, ri=ri: e.tensor_scalar(s3[:, j, :], s3[:, j, :], ri[:, j:j + 1], None,
                                                                   ALU.mult), v)
            na["free", q] = [w]
            na[p + q] = (s, w)

    def na_t(p):
        s, w = na[p]
        b = 3 if p % 2 else 5
        for i in range(4):
            pt = PE(lambda e, i=i: e.transpose(BK[b][:, i * P:i * P + P], s.ap[:, i * P:i * P + P], ident[:, :]),
                    w, *bfree[b], sig=(i == 3))
        s.free = [pt]
        t = tmp()
        a = A(lambda e: e.activation(t.ap, BK[b][:, :], ACT.Copy), pt, *t.free)
        bfree[b] = [a]
        na[p] = (t, a)

    def na_o(p):
        hp, cb = p // 4, p % 4
        t, a = na.pop(p)
        b = 6
        for j in range(2):
            for i in range(2):
                pt = PE(lambda e, j=j, i=i: e.matmul(
                    BK[b][64 * j:64 * j + 64, cb * P:cb * P + P],
                    VB[:, 2 * cb + i, (2 * hp + j) * 64:(2 * hp + j) * 64 + 64],
                    t.ap[:, (2 * j + i) * P:(2 * j + i) * P + P], start=(i == 0), stop=(i == 1)),
                    a, vb_tok[cb], *(bfree[b] if cb == 0 else []), sig=(i == 1 and j == 1))
        t.free = [pt]
        if cb == 3:
            src = BK[b][:, :].rearrange("p (c r q) -> p r c q", c=4, q=16)
            hi = Ahi[:, hp, :].rearrange("p (r c q) -> p r c q", r=8, q=16)
            lo = Alo[:, hp, :].rearrange("p (r c q) -> p r c q", r=8, q=16)
            ah = A(lambda e: e.activation(hi, src, ACT.Copy), pt)
            na_tok[hp] = V(lambda e: e.tensor_tensor(lo, src, f32(hi), ALU.subtract), ah)
            bfree[b] = [na_tok[hp]]

    rot_tok = {}

    def ev_rot(dst, key, sc):
        def ev(ps, tok):
            t, s = tmp(), tmp()
            v = V(lambda e: e.scalar_tensor_tensor(out=t.ap, in0=ps, scalar=sc, in1=R[:, :], op0=ALU.mult,
                                                   op1=ALU.mult), tok, R_tok[0], *t.free)
            L = {}

            def swap():
                for q in range(4):
                    o = q ^ 1
                    L["a"] = A(lambda e, q=q, o=o: e.activation(s.ap[32 * q:32 * q + 32, :],
                                                                t.ap[32 * o:32 * o + 32, :], ACT.Copy), v, *s.free)

            def turn():
                w = V(lambda e: e.tensor_tensor(t.ap, t.ap, ROPE[:, 0, :], ALU.mult), L["a"], rope_tok)
                w2 = V(lambda e: e.tensor_tensor(s.ap, s.ap, ROPE[:, 1, :], ALU.mult))
                rot_tok[key] = V(lambda e: e.tensor_tensor(dst, t.ap, s.ap, ALU.add), w, w2, m_end)
                t.free = s.free = [rot_tok[key]]
            rot.extend([swap, turn])
            return [v]
        return ev

    rot = []

    y_tok = [None] * 4
    rs_ = {}
    rpos = [0]

    def rtmp():
        rpos[0] += 1
        return rring[rpos[0] % 3]

    rring = [Slot(t) for t in (SS, SS2, RS)]
    for s_ in rring:
        s_.ap = s_.t[:, :]
        s_.free = [m_end, R_tok[0], *x_tok]

    def ret_k(hp):
        for c in range(4):
            p = PE(lambda e, c=c: e.transpose(BK[7][:, c * P:c * P + P], RK[:, hp, c * P:c * P + P], ident[:, :]),
                   rot_tok["k", hp], c_tok, *bfree[7], sig=(c == 3))
        ps = BK[7][:, :].rearrange("p (c d) -> p c d", c=4)
        for j in range(2):
            for dst, col in ((KF, 127), (KB_, 0)):
                a = A(lambda e, j=j, dst=dst, col=col: e.activation(
                    dst[:, :, 64 * j:64 * j + 64], ps[:, :, 64 * j:64 * j + 64], ACT.Copy,
                    scale=DG[:, 2 * hp + j, col:col + 1]), p, dg_tok[0], rs_.get("kv"))
        bfree[7] = [a]
        A(lambda e: e.activation(XF[:, :], GD[:, P:2 * P], ACT.Exp, scale=lg[:, 8 + hp:9 + hp]), rs_.get("q"))
        rs_["k"] = A(lambda e: e.activation(XB[:, :], GD[:, 2 * P:3 * P], ACT.Exp, scale=lg[:, 10 + hp:11 + hp]))

    def ret_q(hp):
        q3 = RQ[:, hp, :].rearrange("p (c t) -> p c t", c=4)
        for dst, x in ((QF, XF), (QB, XB)):
            rs_["q"] = V(lambda e, dst=dst, x=x: e.tensor_tensor(
                dst[:, :].rearrange("p (c t) -> p c t", c=4), q3, x[:, :].unsqueeze(1).broadcast_to([P, 4, P]),
                ALU.mult), rot_tok["q", hp], rs_["k"], *rot_tok.values(), rs_.get("o"))

    def ret_kv(hp):
        for b, kt, c0 in ((2, KF, 0), (7, KB_, 1)):
            for c in range(3):
                for j in range(2):
                    p = PE(lambda e, b=b, kt=kt, c=c, c0=c0, j=j: e.matmul(
                        BK[b][64 * j:64 * j + 64, c * P:c * P + P], kt[:, c0 + c, 64 * j:64 * j + 64],
                        RV[:, c0 + c, (2 * hp + j) * P:(2 * hp + j) * P + P], start=True, stop=True),
                        rs_["k"], vt_tok["r", c0 + c], *bfree[b], sig=(c == 2 and j == 1))
            v = rs_.get("o")
            for i in range(3):
                c = i if b == 2 else 2 - i
                dst, prev = (SF, c - 1) if b == 2 else (SB, c + 1)
                kv = BK[b][:, c * P:c * P + P]
                if i == 0:
                    v = V(lambda e, dst=dst, c=c, kv=kv: e.tensor_copy(dst[:, c, :], kv), p, v)
                else:
                    ec = e128[:, hp:hp + 1] if b == 2 else e128[:, 2 + hp:3 + hp]
                    v = V(lambda e, dst=dst, c=c, kv=kv, prev=prev, ec=ec: e.scalar_tensor_tensor(
                        out=dst[:, c, :], in0=dst[:, prev, :], scalar=ec, in1=kv, op0=ALU.mult, op1=ALU.add), v)
            bfree[b] = [v]
        rs_["kv"] = p
        rs_["s"] = v

    def ret_s(h):
        hs = slice(64 * (h % 2), 64 * (h % 2) + 64)
        for c in range(4):
            pt = PE(lambda e, c=c: e.matmul(BK[7][:, c * P:c * P + P], RK[hs, h // 2, c * P:c * P + P],
                                            RQ[hs, h // 2, c * P:c * P + P], start=True, stop=True),
                    rot_tok["q", h // 2], rot_tok["k", h // 2], *bfree[7], sig=(c == 3))
        t = rtmp()
        v = V(lambda e: e.tensor_tensor(t.ap.rearrange("p (c t) -> p c t", c=4),
                                        BK[7][:, :].rearrange("p (c t) -> p c t", c=4),
                                        DG[:, h, :].unsqueeze(1).broadcast_to([P, 4, P]), ALU.mult),
              pt, dg_tok[0], *t.free)
        bfree[7] = [v]
        rs_[h] = (t, v)

    def ret_o(h):
        hs = slice(64 * (h % 2), 64 * (h % 2) + 64)
        t, v = rs_.pop(h)
        b = 2
        for c in range(4):
            tc = slice(c * P, c * P + P)
            PE(lambda e, c=c, tc=tc: e.matmul(BK[b][:, tc], RV[:, c, h * P:h * P + P], t.ap[:, tc],
                                              start=True, stop=False), v, vt_tok["r", c], rs_["s"], rs_["q"], *bfree[b])
            if c > 0:
                p = PE(lambda e, c=c, tc=tc: e.matmul(BK[b][:, tc], SF[hs, c - 1, :], QF[hs, tc], start=False,
                                                      stop=(c == 3)), sig=(c == 3))
            if c < 3:
                PE(lambda e, c=c, tc=tc: e.matmul(BK[b][:, tc], SB[hs, c, :], QB[hs, tc], start=False, stop=True))
        t.free = [p]
        rs_["o"] = p
        y_tok[h] = A(lambda e: e.activation(YH[:, h, :], BK[b][:, :], ACT.Copy), p, *vb_tok.values())
        s = rtmp()
        a = A(lambda e: e.activation(s.ap, BK[b][:, :], ACT.Square), *s.free)
        bfree[b] = [a]
        sq_[h] = (s, a)

    sq_ = {}

    def ret_n(h):
        s, a = sq_[h]
        sq_[h], p = rsq_rows(None, 7, [s.ap], P, [a])
        s.free = [p]

    def ret_y(h):
        v, n = sq_[h]()
        y_tok[h] = V(lambda e: e.tensor_tensor(YH[:, h, :], YH[:, h, :], n.ap, ALU.mult), v, y_tok[h])
        n.free = [y_tok[h]]

    mix_tok = [None] * KT

    def ev_nq(i):
        def ev(ps, tok):
            nq_tok[i] = V(lambda e: e.tensor_tensor(
                NQ[:, i, :].rearrange("p (c r q) -> p r c q", c=4, q=16),
                ps.rearrange("p (r c q) -> p r c q", r=8, q=16),
                R[:, :].rearrange("p (r c q) -> p r c q", r=8, q=16), ALU.mult), tok, R_tok[0], m_end)
            return [nq_tok[i]]
        return ev

    def ev_nk(i):
        def ev(ps, tok):
            nk_tok[i] = V(lambda e: e.scalar_tensor_tensor(out=NK[:, i, :], in0=ps, scalar=0.125, in1=R[:, :],
                                                           op0=ALU.mult, op1=ALU.mult), tok, R_tok[0], m_end)
            return [nk_tok[i]]
        return ev

    def ev_rg(i):
        def ev(ps, tok):
            t = rtmp()
            v = V(lambda e: e.tensor_tensor(t.ap, ps, R[:, :], ALU.mult), tok, R_tok[0], *t.free)
            rg_[i] = (t, v)
            return [v]
        return ev

    rg_ = {}

    def rg_silu(i):
        t, v = rg_[i]
        rg_[i] = (t, A(lambda e: e.activation(t.ap, t.ap, ACT.Silu), v))

    def rg_out(i):
        g, a = rg_[i]
        s = rtmp()
        w = V(lambda e: e.scalar_tensor_tensor(out=s.ap, in0=YH[:, i, :], scalar=vc("rg", i), in1=g.ap,
                                               op0=ALU.mult, op1=ALU.mult), a, y_tok[i], *s.free)
        g.free = [w]
        mix_tok[4 + i], _ = hilo(Ahi[:, 4 + i, :], Alo[:, 4 + i, :], s.ap, w, *y_tok)
        s.free = [mix_tok[4 + i]]

    evs = [ev_rot(RQ[:, 0, :], ("q", 0), 1.0), ev_rot(RK[:, 0, :], ("k", 0), 0.125),
           ev_rot(RQ[:, 1, :], ("q", 1), 1.0), ev_rot(RK[:, 1, :], ("k", 1), 0.125)]
    for i in range(4):
        evs += [ev_nq(i), ev_nk(i)]
    evs += [ev_rg(i) for i in range(4)]
    for n, ev in enumerate(evs):
        pre, mid, end = [], [], []
        p = 2 * (n - 7)
        if n < 4:
            end.append(lambda n=n: bands(n))
        if 0 < n <= 4:
            mid.append(lambda: rot.pop(0)())
            end.append(lambda: rot.pop(0)())
        ret = []
        for hp, n0 in ((0, 4), (1, 7)):
            k = n - n0
            if k == 0:
                ret.append(lambda hp=hp: ret_k(hp))
            if k == 1:
                mid += [lambda hp=hp: ret_kv(hp), lambda hp=hp: ret_q(hp)]
                ret.append(lambda hp=hp: ret_s(2 * hp))
            if k == 2:
                mid += [lambda hp=hp: ret_o(2 * hp), lambda hp=hp: ret_s(2 * hp + 1)]
            if k == 3:
                mid += [lambda hp=hp: ret_o(2 * hp + 1), lambda hp=hp: ret_y(2 * hp)]
            if k == 4:
                (ret if hp == 0 else mid).append(lambda hp=hp: ret_y(2 * hp + 1))
        if 0 <= p < 16:
            pre.append(lambda p=p: na_x(p))
            end += [lambda p=p: na_t(p), lambda p=p: na_t(p + 1), lambda p=p: na_o(p), lambda p=p: na_o(p + 1)]
            if n > 11 and p + 2 < 16:
                end.insert(2, lambda p=p: na_e(p + 2))
        end += ret
        if 0 <= p + 2 < 16:
            (mid if n < 12 else pre).append(lambda p=p: na_g(p + 2))
        if n > 12:
            end.append(lambda h=n - 13: rg_silu(h))
        if 0 <= p + 2 < 16:
            if n < 12:
                end.insert(2 if n > 9 else len(end), lambda p=p: na_s(p + 2))
                end.append(lambda p=p: na_e(p + 2))
            else:
                mid.append(lambda p=p: na_s(p + 2))
        for hp, n0 in ((0, 4), (1, 7)):
            if n - n0 in (2, 3):
                end.append(lambda h=2 * hp + n - n0 - 2: ret_n(h))
        if n > 12:
            end.append(lambda h=n - 13: rg_out(h))
        lin(Hhi, Hlo, h_tok, ev, 1, mid, end, pre)
    flush()
    rg_silu(3)
    rg_out(3)
    for h in range(4):
        mix_tok[h] = na_tok[h]
    mset[0] = list(range(7))
    for n in range(8):
        def ev_o2(ps, tok, n=n):
            x_tok[n] = v = V(lambda e: e.tensor_tensor(X[:, n, :], ps, X[:, n, :], ALU.add), tok, x_tok[n])
            to_h(n, "gl2", v)
            square_into(SS, ss_tok, n, X[:, n, :], v)
            if n == KT - 1:
                norm_rows()
            return [v]
        lin(Ahi, Alo, mix_tok, ev_o2)

    for g in range(4):
        for j in range(8):
            def ev_up(ps, tok, j=j):
                t, m = tmp(), tmp()
                v = V(lambda e: e.tensor_tensor(t.ap, ps, R[:, :], ALU.mult), tok, R_tok[0], *t.free)
                w = V(lambda e: e.scalar_tensor_tensor(out=m.ap, in0=t.ap, scalar=0.0, in1=t.ap, op0=ALU.max,
                                                       op1=ALU.mult), v, *m.free)
                t.free = [w]
                a_tok[j], _ = hilo(Ahi[:, j, :], Alo[:, j, :], m.ap, w)
                m.free = [a_tok[j]]
                return [v]
            lin(Hhi, Hlo, h_tok, ev_up)
        for n in range(8):
            if g == 3 and n == KT - 1:
                break
            if g == 3 and n == 5:
                ln_table()

            def ev_dn(ps, tok, n=n, last=(g == 3)):
                x_tok[n] = v = V(lambda e: e.tensor_tensor(X[:, n, :], ps, X[:, n, :], ALU.add), tok, x_tok[n])
                if last:
                    square_into(SS, ss_tok, n, X[:, n, :], v)
                    x_tok[n] = A(lambda e: e.activation(X[:, n, :], X[:, n, :], ACT.Copy, scale=vc("gf2", n)), v)
                return [v]
            lin(Ahi, Alo, a_tok, ev_dn)
    flush()

    u, n = cur[0], KT - 1
    cur[0] += 1
    wh, wl = WH[u % NW], WL[u % NW]
    acc, sums, row = [[mbank() for _ in range(2)] for _ in range(3)]
    last_p, last_q = [None, None], [None, None]
    q7 = tmp()

    def products(h, k):
        ps, kc, tc = BK[acc[h]][:, 0:256], slice(k * P, k * P + P), slice(256 * h, 256 * h + 256)
        PE(lambda e: e.matmul(ps, wh[:, kc], Ahi[:, k, tc], start=(k == 0), stop=False), a_tok[k], ltok[u],
           *bfree[acc[h]])
        PE(lambda e: e.matmul(ps, wh[:, kc], Alo[:, k, tc], start=False, stop=False))
        last_p[h] = PE(lambda e: e.matmul(ps, wl[:, kc], Ahi[:, k, tc], start=False, stop=(k == 7)), sig=(k == 7))

    def close(h):
        tc = slice(256 * h, 256 * h + 256)
        v = V(lambda e: e.tensor_tensor(X[:, n, tc], BK[acc[h]][:, 0:256], X[:, n, tc], ALU.add), last_p[h], x_tok[n])
        last_q[h] = A(lambda e: e.activation(q7.ap[:, tc], X[:, n, tc], ACT.Square), v, *q7.free)
        last_p[h] = A(lambda e: e.activation(X[:, n, tc], X[:, n, tc], ACT.Copy, scale=vc("gf2", n)), v)

    def half_sums(h, col, src, tok):
        for t in range(2):
            p = PE(lambda e, t=t: e.matmul(BK[sums[h]][:, col + t:col + t + 1],
                                           src[:, 256 * h + t * P:256 * h + t * P + P], ones[:, 0:1],
                                           start=True, stop=True), tok, *bfree[sums[h]], sig=(t == 1))
        return p

    fin = {}

    def factor(h, p, between=()):
        sm, m, y, t = (st[:, i, 2 * h:2 * h + 2] for i in range(4))
        ps = BK[sums[h]]
        v = V(lambda e: e.tensor_copy(sm, ps[:, 0:2]), p)
        v = V(lambda e: e.tensor_tensor(sm, sm, ps[:, 2:4], ALU.add), v)
        v = V(lambda e: e.tensor_scalar(m, sm, 1.0 / D, EPS, ALU.mult, ALU.add), v)
        a = A(lambda e: e.activation(y, m, ACT.Ln), v)
        a = A(lambda e: e.activation(y, y, ACT.Exp, scale=-0.5), a)
        for i in between:
            store(0, i)
        v = V(lambda e: e.scalar_tensor_tensor(out=t, in0=y, scalar=-0.5, in1=y, op0=ALU.mult, op1=ALU.mult), a)
        v = V(lambda e: e.tensor_tensor(t, t, m, ALU.mult), v)
        v = V(lambda e: e.scalar_tensor_tensor(out=rt[:, 2 * h:2 * h + 2], in0=t, scalar=1.5, in1=y, op0=ALU.add,
                                               op1=ALU.mult), v)
        return v

    def spread(h, v):
        for t in range(2):
            fin[h] = PE(lambda e, t=t: e.matmul(BK[row[h]][:, t * P:t * P + P],
                                                rt[:, 2 * h + t:2 * h + t + 1].broadcast_to([P, P]), ident[:, :],
                                                start=True, stop=True), v, *bfree[row[h]], sig=(t == 1))

    def store(h, i):
        tc = slice(256 * h, 256 * h + 256)
        r = BK[row[h]][:, 0:256].unsqueeze(1).broadcast_to([P, 2, 256])
        v = V(lambda e: e.tensor_tensor(X[:, i:i + 2, tc], X[:, i:i + 2, tc], r, ALU.mult), fin[h], last_p[h],
              *x_tok[0:n])
        return DMA("S", "do", out[i:i + 2, :, tc].rearrange("n p t -> p n t"), X[:, i:i + 2, tc], v)

    for k in range(8):
        products(0, k)
    close(0)
    for k in range(8):
        products(1, k)
        if k == 1:
            half_sums(0, 0, SS, ss_tok[0])
        if k == 5:
            half_sums(1, 0, SS, ss_tok[0])
        if k == 2:
            p0 = half_sums(0, 2, q7.ap, last_q[0])
    v = factor(0, p0)
    close(1)
    spread(0, v)
    p = half_sums(1, 2, q7.ap, last_q[1])
    store(0, 0)
    spread(1, factor(1, p, [2]))
    for h, i in ((0, 4), (0, 6), (1, 0), (1, 2), (1, 4), (1, 6)):
        o = store(h, i)
    pr.put("S", None, [o])
    assert cur[0] == NU, (cur[0], NU)

    with ExitStack() as ctx:
        sems = {s: ctx.enter_context(nc.semaphore(f"s_{s}")) for s in pr.n}
        block = ctx.enter_context(nc.Block())

        @block.sync
        def _(e):
            pr.run("S", e, sems)

        @block.scalar
        def _(e):
            pr.run("A", e, sems)

        @block.vector
        def _(e):
            pr.run("V", e, sems)

        @block.gpsimd
        def _(e):
            pr.run("G", e, sems)

        @block.tensor
        def _(e):
            pr.run("P", e, sems)


def _tiles(w):
    k, n = w.shape
    return np.ascontiguousarray(w.reshape(k // P, P, n // P, P).transpose(2, 1, 0, 3))


def _wide(w):
    k, n = w.shape
    return np.ascontiguousarray(w.reshape(k // P, P, n // 512, 512).transpose(2, 1, 0, 3))


def _col(v):
    return v.reshape(-1, P).T


def _layout(a):
    f = np.float32
    m = {}
    m["xt"] = np.ascontiguousarray(a["x"][0].T).reshape(KT, P, T)
    m["w_gu1"] = _tiles(a["ffn1_w_gu"][0])
    m["w_d1"] = _tiles(a["ffn1_w_down"][0])
    m["w_gu2"] = _tiles(a["ffn2_w_gu"][0])
    m["w_d2"] = _tiles(a["ffn2_w_down"][0])
    w = a["w_in"][0]
    sizes = [("cb", D), ("cc", D), ("cu", D), ("q", 512), ("k", 512), ("v", D), ("glr", 16), ("r", D), ("ga", D),
             ("gb", D)]
    o = 0
    for name, n in sizes:
        part = w[:, o:o + n]
        o += n
        if name == "glr":
            part = np.concatenate([part, np.zeros((D, P - n), f)], axis=1)
        m["w_" + name] = _wide(part) if name == "v" else _tiles(part)
    m["w_oc"] = _tiles(a["w_out_conv"][0])
    m["w_og"] = _tiles(a["w_out_gla"][0])
    m["w_o"] = _tiles(a["w_o"][0])
    w = a["w_in_2"][0]
    o = 0
    for name, n in [("nq", 512), ("nk", 512), ("nv", 512), ("rq", 256), ("rk", 256), ("rv", 512), ("rg", 512)]:
        part = w[:, o:o + n]
        o += n
        m["w_" + name] = _wide(part) if name in ("nv", "rv") else _tiles(part)
    m["w_out2"] = _tiles(a["w_out_2"][0])
    m["w_up"] = _tiles(a["w_up_2"][0])
    m["w_dn"] = _tiles(a["w_down_2"][0])
    m["gup"] = np.ascontiguousarray(a["gate_w_up"][0])
    fwd, bwd = a["ret_decay_fwd_2"][0], a["ret_decay_bwd_2"][0]
    dec = np.concatenate([np.broadcast_to(np.concatenate([fwd, bwd]), (P, 8)),
                          np.repeat(fwd.reshape(2, 2).T, 64, axis=0), np.repeat(bwd.reshape(2, 2).T, 64, axis=0)],
                         axis=1)
    parts = dict(g1=_col(a["norm_ffn1_g"][0]), gm=_col(a["norm_mix_g"][0]), g2=_col(a["norm_ffn2_g"][0]),
                 gf=_col(a["final_norm_g"]), gm2=_col(a["norm_mix_2"][0]), gl2=_col(a["norm_mlp_2"][0]),
                 gf2=_col(a["norm_final_2"]), gla=_col(a["gla_norm_g"][0]), gb=_col(a["gate_b"][0]),
                 cw0=_col(a["conv_w"][0, 0]), cw1=_col(a["conv_w"][0, 1]), cw2=_col(a["conv_w"][0, 2]),
                 rg=_col(a["ret_norm_gain_2"][0]), dec=dec)
    m["vec"] = np.ascontiguousarray(np.concatenate([parts[n] for n in VEC], axis=1))
    rpb = a["na_rpb_2"][0]
    flat = np.concatenate([np.zeros((8, 32), f), np.concatenate([rpb, np.zeros((8, 15, 1), f)], axis=2).reshape(8, 480),
                           np.zeros((8, 32), f)], axis=1)
    r, q, n = np.meshgrid(np.arange(8), np.arange(16), np.arange(BW), indexing="ij")
    at = 32 + (7 - r) * 32 + 15 - q - 16 + n
    m["rpb"] = np.ascontiguousarray(flat[:, at.reshape(P, BW)])
    return m


def _constants():
    f = np.float32
    m = {}
    m["ident"] = np.eye(P, dtype=f)
    t = np.arange(T)
    m["scm"] = np.ascontiguousarray(np.broadcast_to((t % 64 != 0).astype(f), (P, T)))
    j, i = np.arange(P)[:, None], (t % P)[None, :]
    m["cau"] = (i >= j).astype(f)
    qj, kj = np.arange(16)[:, None], np.arange(32)[None, :]
    nam = np.zeros((3, 16, 32), f)
    for p, cb in enumerate((0, 1, 3)):
        col = 16 * cb + qj
        key = [0, 8, 24, 32][cb] + kj
        lo = np.clip(col - 8, 0, 48)
        nam[p] = np.where((key >= lo) & (key < lo + 16), 0.0, -1e30)
    m["nam"] = np.ascontiguousarray(np.tile(nam.transpose(1, 0, 2), (8, 1, 1)))
    inv = (f(1.0) / (f(10000.0) ** (np.arange(0, 64, 2, dtype=f) / f(64)))).astype(f)
    ang = (t.astype(f)[None, :] * inv[:, None]).astype(f).astype(np.float64)
    cos, sin = np.cos(ang).astype(f), np.sin(ang).astype(f)
    m["rope"] = np.ascontiguousarray(np.stack([np.concatenate([cos, cos, cos, cos]),
                                               np.concatenate([-sin, sin, -sin, sin])], axis=1))
    i = np.arange(P)
    m["gd"] = np.concatenate([i[None, :] - i[:, None], np.broadcast_to(i + 1, (P, P)), np.broadcast_to(P - i, (P, P))],
                             axis=1).astype(f)
    return m


def kernel(**inputs):
    import concourse.bacc as _bacc
    from concourse.bass_utils import run_bass_kernel_spmd as _run

    arrays = {**_layout({k: np.asarray(v) for k, v in inputs.items()}), **_constants()}
    nc = _bacc.Bacc("TRN2", target_bir_lowering=False, num_devices=1)
    dr = {n: nc.dram_tensor(f"in_{n}", v.shape, F32, kind="ExternalInput").ap() for n, v in arrays.items()}
    out = nc.dram_tensor("out_0", (KT, P, T), F32, kind="ExternalOutput").ap()
    build(nc, dr, out)
    r = _run(nc, [{f"in_{n}": v for n, v in arrays.items()}], core_ids=[0])
    got = r.results[0]["out_0"]
    return np.ascontiguousarray(got.reshape(D, T).T).reshape(1, T, D)
```
